# Optimizing a Trainium2 kernel written in Bass

```python
import math
import jax
import jax.numpy as jnp
from jax import lax
import numpy as np

D_MODEL = 1024
BATCH = 1
SEQ = 128
DEPTH = 2
DEC_BATCH = 1
DEC_SEQ = 256
PAST_LEN = 128

GRID_W = 64
N_EVEN = (DEPTH + 1) // 2
N_ODD = DEPTH // 2
ROPE_THETA = 10000.0
Q_BLOCK = 128
EPS = 1e-6
DN_ALPHA = (2 * DEPTH) ** 0.25
DN_BETA = (8 * DEPTH) ** -0.25

H_A = 4
D_A = 64
H_B = 8
B_NOPE = 64
B_ROPE = 32
B_V = 64
B_QRANK = 256
B_KVRANK = 128
H_C = 8
G_C = 2
D_C = 64
H_D = 8
D_D = 64
NA_ROWS = 8
NA_COLS = 16
PEER_HEADS = 8
PEER_KEYS = 128
PEER_EXPERTS = PEER_KEYS * PEER_KEYS
PEER_DKEY = 256
PEER_TOPK = 16
PEER_CHUNK = 128

EVEN_SIZES = (H_A * 2 * D_A, H_A * 2 * D_A, H_A * 2 * D_A, B_QRANK, B_KVRANK, B_ROPE)
ODD_SIZES = (H_C * D_C, G_C * D_C, G_C * D_C, H_D * D_D, H_D * D_D, H_D * D_D)
EVEN_IN = 3 * H_A * 2 * D_A + B_QRANK + B_KVRANK + B_ROPE
ODD_IN = H_C * D_C + 2 * G_C * D_C + 3 * H_D * D_D
EVEN_MIX = H_A * 2 * D_A + H_B * B_V
ODD_MIX = H_C * D_C + H_D * D_D

kernel_name = 'hybrid_diffusion_prefix_step'

def split_points(sizes):
    pts, acc = [], 0
    for sz in sizes[:-1]:
        acc += sz
        pts.append(acc)
    return pts

def layer_norm(x, g, b):
    xf = x.astype(jnp.float32)
    mu = jnp.mean(xf, axis=-1, keepdims=True)
    var = jnp.mean(jnp.square(xf - mu), axis=-1, keepdims=True)
    return ((xf - mu) * lax.rsqrt(var + EPS) * g.astype(jnp.float32) + b.astype(jnp.float32)).astype(x.dtype)

def rms_norm(x, g):
    xf = x.astype(jnp.float32)
    return (xf * lax.rsqrt(jnp.mean(xf * xf, axis=-1, keepdims=True) + EPS) * g.astype(jnp.float32)).astype(x.dtype)

def softmax_f32(s):
    return jax.nn.softmax(s.astype(jnp.float32), axis=-1)

def grid_angles(n_tok, rot_dim):
    t = jnp.arange(n_tok)
    row = (t // GRID_W).astype(jnp.float32)
    col = (t % GRID_W).astype(jnp.float32)
    n_freq = rot_dim // 4
    inv = ROPE_THETA ** (-jnp.arange(n_freq, dtype=jnp.float32) / n_freq)
    return jnp.concatenate([row[:, None] * inv, col[:, None] * inv], axis=-1)

def apply_rope(x, ang):
    half = x.shape[-1] // 2
    shp = (1, x.shape[1]) + (1,) * (x.ndim - 3) + (half,)
    cos = jnp.cos(ang).reshape(shp).astype(x.dtype)
    sin = jnp.sin(ang).reshape(shp).astype(x.dtype)
    x1, x2 = x[..., :half], x[..., half:]
    return jnp.concatenate([x1 * cos - x2 * sin, x1 * sin + x2 * cos], axis=-1)

def sweep_query_blocks(fn, *qs):
    b, s = qs[0].shape[:2]
    nb = s // Q_BLOCK

    def split(a):
        return jnp.moveaxis(a.reshape((b, nb, Q_BLOCK) + a.shape[2:]), 1, 0)

    out = lax.map(lambda blk: fn(*blk), tuple(split(q) for q in qs))
    return jnp.moveaxis(out, 0, 1).reshape((b, s) + out.shape[3:])

def modulation(cvec, w_mod, b_mod):
    m = jax.nn.silu(cvec) @ w_mod + b_mod
    return jnp.split(m[:, None, :], 6, axis=-1)

def diff_attention(q, k, v, lam):
    s = jnp.einsum('bqhmd,bkhmd->bhmqk', q, k) * (D_A ** -0.5)
    p = softmax_f32(s)
    p = p[:, :, 0] - lam * p[:, :, 1]
    return jnp.einsum('bhqk,bkhe->bqhe', p.astype(v.dtype), v)

def latent_attention(q_nope, q_rope, k_nope, k_rope, v):
    s = jnp.einsum('bqhd,bkhd->bhqk', q_nope, k_nope) + jnp.einsum('bqhd,bkd->bhqk', q_rope, k_rope)
    p = softmax_f32(s * ((B_NOPE + B_ROPE) ** -0.5)).astype(v.dtype)
    return jnp.einsum('bhqk,bkhd->bqhd', p, v)

def gqa_attention(q, k, v):
    b, nq = q.shape[:2]
    qg = q.reshape(b, nq, G_C, H_C // G_C, D_C)
    s = jnp.einsum('bqgrd,bkgd->bgrqk', qg, k) * (D_C ** -0.5)
    p = softmax_f32(s).astype(v.dtype)
    return jnp.einsum('bgrqk,bkgd->bqgrd', p, v).reshape(b, nq, H_C, D_C)

def mha_attention(q, k, v, scale):
    s = jnp.einsum('bqhd,bkhd->bhqk', q, k) * scale
    p = softmax_f32(s).astype(v.dtype)
    return jnp.einsum('bhqk,bkhd->bqhd', p, v)

def neighbourhood_attention(q, k, v, ck, cv, rpb):
    b, s, h, d = q.shape
    rows = s // GRID_W
    wr = min(NA_ROWS, rows)
    wc = min(NA_COLS, GRID_W)
    r = jnp.arange(rows)
    col = jnp.arange(GRID_W)
    r0 = jnp.clip(r - wr // 2, 0, rows - wr)
    c0 = jnp.clip(col - wc // 2, 0, GRID_W - wc)
    key_rows = r0[:, None] + jnp.arange(wr)
    qg = q.reshape(b, rows, GRID_W, h, d)
    kg = k.reshape(b, rows, GRID_W, h, d)[:, key_rows]
    vg = v.reshape(b, rows, GRID_W, h, d)[:, key_rows]
    scale = d ** -0.5
    s_loc = jnp.einsum('brqhd,brjkhd->brhqjk', qg, kg).astype(jnp.float32) * scale
    dr = key_rows - r[:, None]
    dc = jnp.clip(col[None, :] - col[:, None], -(NA_COLS - 1), NA_COLS - 1)
    bias = rpb[:, dr[:, None, :, None] + (NA_ROWS - 1), dc[None, :, None, :] + (NA_COLS - 1)]
    s_loc = s_loc + jnp.moveaxis(bias, 0, 1).astype(jnp.float32)[None]
    col_ok = (col[None, :] >= c0[:, None]) & (col[None, :] < c0[:, None] + wc)
    s_loc = jnp.where(col_ok[None, None, None, :, None, :], s_loc, -jnp.inf)
    s_ctx = jnp.einsum('brqhd,blhd->brhql', qg, ck).astype(jnp.float32) * scale
    n_loc = wr * GRID_W
    p = softmax_f32(jnp.concatenate([s_loc.reshape(b, rows, h, GRID_W, n_loc), s_ctx], axis=-1))
    p = p.astype(v.dtype)
    p_loc = p[..., :n_loc].reshape(b, rows, h, GRID_W, wr, GRID_W)
    out = (jnp.einsum('brhqjk,brjkhd->brqhd', p_loc, vg)
           + jnp.einsum('brhql,blhd->brqhd', p[..., n_loc:], cv))
    return out.reshape(b, s, h, d)

def even_mixer(h, mix, lam_init, cache):
    b, s, _ = h.shape
    a_q, a_k, a_v, b_cq, b_ckv, b_kr = jnp.split(h @ mix['w_in'], split_points(EVEN_SIZES), axis=-1)
    a_q = a_q.reshape(b, s, H_A, 2, D_A)
    a_k = a_k.reshape(b, s, H_A, 2, D_A)
    a_v = a_v.reshape(b, s, H_A, 2 * D_A)
    bq = (rms_norm(b_cq, mix['g_cq']) @ mix['w_uq']).reshape(b, s, H_B, B_NOPE + B_ROPE)
    bq_nope, bq_rope = bq[..., :B_NOPE], bq[..., B_NOPE:]
    ckv = rms_norm(b_ckv, mix['g_ckv'])
    if cache is None:
        new_state = (a_k, a_v, ckv, b_kr)
        k_a, v_a, ckv_all, kr_all = a_k, a_v, ckv, b_kr
    else:
        ang_a = grid_angles(s, D_A)
        ang_b = grid_angles(s, B_ROPE)
        a_q = apply_rope(a_q, ang_a)
        bq_rope = apply_rope(bq_rope, ang_b)
        ck_a, cv_a, c_ckv, c_kr = cache
        k_a = jnp.concatenate([apply_rope(a_k, ang_a), ck_a], axis=1)
        v_a = jnp.concatenate([a_v, cv_a], axis=1)
        ckv_all = jnp.concatenate([ckv, c_ckv], axis=1)
        kr_all = jnp.concatenate([apply_rope(b_kr, ang_b), c_kr], axis=1)
        new_state = None
    n_k = ckv_all.shape[1]
    kv = (ckv_all @ mix['w_ukv']).reshape(b, n_k, H_B, B_NOPE + B_V)
    k_nope, v_b = kv[..., :B_NOPE], kv[..., B_NOPE:]
    f32 = jnp.float32
    lam = (jnp.exp(jnp.sum(mix['lam_q1'].astype(f32) * mix['lam_k1'].astype(f32)))
           - jnp.exp(jnp.sum(mix['lam_q2'].astype(f32) * mix['lam_k2'].astype(f32))) + lam_init)
    o_a = sweep_query_blocks(lambda q: diff_attention(q, k_a, v_a, lam), a_q)
    o_a = rms_norm(o_a, mix['g_sub']) * (1.0 - lam_init)
    o_b = sweep_query_blocks(lambda qn, qr: latent_attention(qn, qr, k_nope, kr_all, v_b), bq_nope, bq_rope)
    o = jnp.concatenate([o_a.reshape(b, s, -1), o_b.reshape(b, s, -1)], axis=-1)
    return o @ mix['w_out'], new_state

def odd_mixer(h, mix, cache):
    b, s, _ = h.shape
    c_q, c_k, c_v, d_q, d_k, d_v = jnp.split(h @ mix['w_in'], split_points(ODD_SIZES), axis=-1)
    c_q = rms_norm(c_q.reshape(b, s, H_C, D_C), mix['g_qn'])
    c_k = rms_norm(c_k.reshape(b, s, G_C, D_C), mix['g_kn'])
    c_v = c_v.reshape(b, s, G_C, D_C)
    d_q = d_q.reshape(b, s, H_D, D_D)
    d_k = d_k.reshape(b, s, H_D, D_D)
    d_v = d_v.reshape(b, s, H_D, D_D)
    if cache is None:
        new_state = (c_k, c_v, d_k, d_v)
        o_c = sweep_query_blocks(lambda q: gqa_attention(q, c_k, c_v), c_q)
        o_d = sweep_query_blocks(lambda q: mha_attention(q, d_k, d_v, D_D ** -0.5), d_q)
    else:
        ck_c, cv_c, ck_d, cv_d = cache
        ang = grid_angles(s, D_C)
        k_c = jnp.concatenate([apply_rope(c_k, ang), ck_c], axis=1)
        v_c = jnp.concatenate([c_v, cv_c], axis=1)
        o_c = sweep_query_blocks(lambda q: gqa_attention(q, k_c, v_c), apply_rope(c_q, ang))
        o_d = neighbourhood_attention(d_q, d_k, d_v, ck_d, cv_d, mix['rpb'])
        new_state = None
    o = jnp.concatenate([o_c.reshape(b, s, -1), o_d.reshape(b, s, -1)], axis=-1)
    return o @ mix['w_out'], new_state

def peer_ffn(h, w_q, sub_k1, sub_k2, u_tab, v_tab):
    b, s, dm = h.shape
    n_tok = b * s
    xt = h.reshape(n_tok, dm)
    q = (xt @ w_q).reshape(n_tok, PEER_HEADS, PEER_DKEY)
    half = PEER_DKEY // 2
    s1 = jnp.einsum('thd,nd->thn', q[..., :half], sub_k1).astype(jnp.float32)
    s2 = jnp.einsum('thd,nd->thn', q[..., half:], sub_k2).astype(jnp.float32)
    v1, i1 = lax.top_k(s1, PEER_TOPK)
    v2, i2 = lax.top_k(s2, PEER_TOPK)
    cand_s = (v1[..., :, None] + v2[..., None, :]).reshape(n_tok, PEER_HEADS, PEER_TOPK * PEER_TOPK)
    cand_i = (i1[..., :, None] * PEER_KEYS + i2[..., None, :]).reshape(n_tok, PEER_HEADS, PEER_TOPK * PEER_TOPK)
    top_s, pos = lax.top_k(cand_s, PEER_TOPK)
    idx = jnp.take_along_axis(cand_i, pos, axis=-1)
    g = jax.nn.softmax(top_s, axis=-1).astype(h.dtype)

    def chunk(args):
        xc, ic, gc = args
        u = jnp.take(u_tab, ic, axis=0)
        act = jax.nn.gelu(jnp.einsum('chkd,cd->chk', u, xc), approximate=False)
        return jnp.einsum('chk,chkd->cd', gc * act, jnp.take(v_tab, ic, axis=0))

    nch = n_tok // PEER_CHUNK
    out = lax.map(chunk, (xt.reshape(nch, PEER_CHUNK, dm),
                          idx.reshape(nch, PEER_CHUNK, PEER_HEADS, PEER_TOPK),
                          g.reshape(nch, PEER_CHUNK, PEER_HEADS, PEER_TOPK)))
    return out.reshape(b, s, dm)

def trunk_layer(x, cvec, l, mix, norm, peer, cache):
    w_m, b_m, g1, b1, g2, b2 = norm
    sh1, sc1, gt1, sh2, sc2, gt2 = modulation(cvec, w_m, b_m)
    h = x * (1.0 + sc1) + sh1
    if l % 2 == 0:
        y, new_state = even_mixer(h, mix, 0.8 - 0.6 * math.exp(-0.3 * l), cache)
    else:
        y, new_state = odd_mixer(h, mix, cache)
    x = layer_norm(DN_ALPHA * x + gt1 * y, g1, b1)
    h = x * (1.0 + sc2) + sh2
    x = layer_norm(DN_ALPHA * x + gt2 * peer_ffn(h, *peer), g2, b2)
    return x, new_state

def setup_inputs(seed: int = 0) -> dict:
    key = jax.random.key(seed)
    ks = iter(jax.random.split(key, 48))
    d = D_MODEL

    def nrm(shape, scale):
        return jax.random.normal(next(ks), shape, jnp.float32) * scale

    def gain(shape):
        return 1.0 + nrm(shape, 0.02)

    return {
        'x_prompt': nrm((BATCH, SEQ, d), 1.0),
        'x_sample': nrm((DEC_BATCH, DEC_SEQ, d), 1.0),
        'cache_a_k': nrm((DEC_BATCH, N_EVEN, PAST_LEN, H_A, 2, D_A), 1.0),
        'cache_a_v': nrm((DEC_BATCH, N_EVEN, PAST_LEN, H_A, 2 * D_A), 1.0),
        'cache_b_ckv': nrm((DEC_BATCH, N_EVEN, PAST_LEN, B_KVRANK), 1.0),
        'cache_b_kr': nrm((DEC_BATCH, N_EVEN, PAST_LEN, B_ROPE), 1.0),
        'cache_c_k': nrm((DEC_BATCH, N_ODD, PAST_LEN, G_C, D_C), 1.0),
        'cache_c_v': nrm((DEC_BATCH, N_ODD, PAST_LEN, G_C, D_C), 1.0),
        'cache_d_k': nrm((DEC_BATCH, N_ODD, PAST_LEN, H_D, D_D), 1.0),
        'cache_d_v': nrm((DEC_BATCH, N_ODD, PAST_LEN, H_D, D_D), 1.0),
        'c': nrm((DEC_BATCH, d), 1.0),
        'c_ctx': nrm((d,), 1.0),
        'w_mod': nrm((DEPTH, d, 6 * d), 0.5 * d ** -0.5),
        'b_mod': nrm((DEPTH, 6 * d), 0.02),
        'ln1_g': gain((DEPTH, d)),
        'ln1_b': nrm((DEPTH, d), 0.02),
        'ln2_g': gain((DEPTH, d)),
        'ln2_b': nrm((DEPTH, d), 0.02),
        'ev_w_in': nrm((N_EVEN, d, EVEN_IN), d ** -0.5),
        'ev_lam_q1': nrm((N_EVEN, D_A), 0.1),
        'ev_lam_k1': nrm((N_EVEN, D_A), 0.1),
        'ev_lam_q2': nrm((N_EVEN, D_A), 0.1),
        'ev_lam_k2': nrm((N_EVEN, D_A), 0.1),
        'ev_g_sub': gain((N_EVEN, 2 * D_A)),
        'ev_g_cq': gain((N_EVEN, B_QRANK)),
        'ev_w_uq': nrm((N_EVEN, B_QRANK, H_B * (B_NOPE + B_ROPE)), B_QRANK ** -0.5),
        'ev_g_ckv': gain((N_EVEN, B_KVRANK)),
        'ev_w_ukv': nrm((N_EVEN, B_KVRANK, H_B * (B_NOPE + B_V)), B_KVRANK ** -0.5),
        'ev_w_out': nrm((N_EVEN, EVEN_MIX, d), DN_BETA * EVEN_MIX ** -0.5),
        'od_w_in': nrm((N_ODD, d, ODD_IN), d ** -0.5),
        'od_g_qn': gain((N_ODD, D_C)),
        'od_g_kn': gain((N_ODD, D_C)),
        'od_rpb': nrm((N_ODD, H_D, 2 * NA_ROWS - 1, 2 * NA_COLS - 1), 0.1),
        'od_w_out': nrm((N_ODD, ODD_MIX, d), DN_BETA * ODD_MIX ** -0.5),
        'pk_w_q': nrm((DEPTH, d, PEER_HEADS * PEER_DKEY), d ** -0.5),
        'pk_k1': nrm((DEPTH, PEER_KEYS, PEER_DKEY // 2), (PEER_DKEY // 2) ** -0.5),
        'pk_k2': nrm((DEPTH, PEER_KEYS, PEER_DKEY // 2), (PEER_DKEY // 2) ** -0.5),
        'pk_u': nrm((DEPTH, PEER_EXPERTS, d), d ** -0.5),
        'pk_v': nrm((DEPTH, PEER_EXPERTS, d), DN_BETA),
    }

def reference(x_prompt, x_sample, cache_a_k, cache_a_v, cache_b_ckv, cache_b_kr,
              cache_c_k, cache_c_v, cache_d_k, cache_d_v, c, c_ctx,
              w_mod, b_mod, ln1_g, ln1_b, ln2_g, ln2_b,
              ev_w_in, ev_lam_q1, ev_lam_k1, ev_lam_q2, ev_lam_k2, ev_g_sub,
              ev_g_cq, ev_w_uq, ev_g_ckv, ev_w_ukv, ev_w_out,
              od_w_in, od_g_qn, od_g_kn, od_rpb, od_w_out,
              pk_w_q, pk_k1, pk_k2, pk_u, pk_v):
    def params_for(l):
        j = l // 2
        if l % 2 == 0:
            mix = {'w_in': ev_w_in[j], 'lam_q1': ev_lam_q1[j], 'lam_k1': ev_lam_k1[j],
                   'lam_q2': ev_lam_q2[j], 'lam_k2': ev_lam_k2[j], 'g_sub': ev_g_sub[j],
                   'g_cq': ev_g_cq[j], 'w_uq': ev_w_uq[j], 'g_ckv': ev_g_ckv[j],
                   'w_ukv': ev_w_ukv[j], 'w_out': ev_w_out[j]}
        else:
            mix = {'w_in': od_w_in[j], 'g_qn': od_g_qn[j], 'g_kn': od_g_kn[j],
                   'rpb': od_rpb[j], 'w_out': od_w_out[j]}
        norm = (w_mod[l], b_mod[l], ln1_g[l], ln1_b[l], ln2_g[l], ln2_b[l])
        peer = (pk_w_q[l], pk_k1[l], pk_k2[l], pk_u[l], pk_v[l])
        return mix, norm, peer

    y = x_prompt
    even_states, odd_states = [], []
    for l in range(DEPTH):
        mix, norm, peer = params_for(l)
        y, st = trunk_layer(y, c_ctx[None, :], l, mix, norm, peer, None)
        (even_states if l % 2 == 0 else odd_states).append(st)

    z = x_sample
    for l in range(DEPTH):
        j = l // 2
        if l % 2 == 0:
            cache = (cache_a_k[:, j], cache_a_v[:, j], cache_b_ckv[:, j], cache_b_kr[:, j])
        else:
            cache = (cache_c_k[:, j], cache_c_v[:, j], cache_d_k[:, j], cache_d_v[:, j])
        mix, norm, peer = params_for(l)
        z, _ = trunk_layer(z, c, l, mix, norm, peer, cache)

    state_a_k = jnp.stack([st[0] for st in even_states], axis=1)
    state_a_v = jnp.stack([st[1] for st in even_states], axis=1)
    state_b_ckv = jnp.stack([st[2] for st in even_states], axis=1)
    state_b_kr = jnp.stack([st[3] for st in even_states], axis=1)
    state_c_k = jnp.stack([st[0] for st in odd_states], axis=1)
    state_c_v = jnp.stack([st[1] for st in odd_states], axis=1)
    state_d_k = jnp.stack([st[2] for st in odd_states], axis=1)
    state_d_v = jnp.stack([st[3] for st in odd_states], axis=1)
    return (y, z, state_a_k, state_a_v, state_b_ckv, state_b_kr, state_c_k, state_c_v, state_d_k, state_d_v)


_drawn_inputs = setup_inputs


def setup_inputs(seed=0):
    import zlib

    import numpy as np

    out = dict(_drawn_inputs(seed))
    spreads = {}
    factors = {'cache_a_k': 3.121,
     'cache_a_v': 2.797,
     'cache_b_ckv': 7.923,
     'cache_b_kr': 8.0,
     'cache_c_k': 8.0,
     'cache_c_v': 8.0,
     'cache_d_k': 7.108,
     'cache_d_v': 6.008,
     'ev_lam_q1': 8.0,
     'ev_lam_k1': 8.0,
     'ev_lam_q2': 8.0,
     'ev_lam_k2': 8.0,
     'ev_g_sub': 8.0,
     'ev_g_cq': 8.0,
     'ev_w_uq': 4.443,
     'ev_g_ckv': 3.148,
     'od_g_qn': 8.0,
     'od_g_kn': 3.619,
     'od_rpb': 8.0}
    for name, (base, spread) in spreads.items():
        noise = np.random.default_rng([zlib.crc32(name.encode()), seed]).standard_normal(out[name].shape)
        drawn = base * np.exp(spread * noise) if base else spread * noise
        out[name] = jnp.asarray(drawn.astype(out[name].dtype))
    for name, factor in factors.items():
        out[name] = (out[name] * factor).astype(out[name].dtype)
    return out
```

```python
from contextlib import ExitStack

import concourse.bass as bass
from concourse import mybir

F32 = mybir.dt.float32
U32 = mybir.dt.uint32
ALU = mybir.AluOpType
ACT = mybir.ActivationFunctionType
AX = mybir.AxisListType

P = 128
D = 1024
KC = D // P
NT = 3
TOK = NT * P
LAYERS = 2
EPS = 1e-6
ALPHA = (2 * LAYERS) ** 0.25
LAM_INIT = 0.2
NEG = -3.0e38
RING = 8
HEADS = 8
TOPK = 16
KEYS = 128
HALF = 64
CORE = HALF * TOK
IN_W = (1952, 2304)
MODS = LAYERS * 6 * KC

C_ID, C_IOTA, C_ONES = 0, 128, 256
C_COSA, C_SINA = 384, 512
C_COSB, C_SINB = 640, 704
C_MASK = 768
C_N = 832
R_LAM, R_SUB, R_CQ, R_CKV, R_QN, R_KN, R_N = 0, 256, 384, 640, 768, 832, 896

A_PR = 0
A_QR = A_PR + 3 * 2304
A_KR = A_QR + 3 * 768
A_VR = A_KR + 4 * 768
A_CA = A_VR + 4 * 512
A_CB = A_CA + 2 * 512
A_QT = A_CB + 256
A_KT = A_QT + 8 * TOK
A_P = A_KT + 8 * 512
A_PT = A_P + 2 * TOK
A_O = A_PT + 2 * TOK
A_TMP = A_O + 3 * D
A_N = A_TMP + 2048
A_BIAS, A_SC = A_QR, A_QR + 4096
Q_S = 0
Q_V = Q_S + NT * 16 * 128
Q_I = Q_V + NT * 16 * 16
Q_IF = Q_I + NT * 16 * 16
Q_TV = Q_IF + NT * 16 * 16
Q_TP = Q_TV + NT * 128
Q_AB = Q_TP + NT * 128
Q_ABF = Q_AB + 2 * NT * 128
Q_EQ = Q_ABF + 2 * NT * 128
Q_ID = Q_EQ + 2048
Q_QS = Q_ID + 3 * NT * 128
assert Q_QS + 2 * TOK <= CORE
Q_W = CORE
Q_OA = Q_W + 4 * TOK
Q_OB = Q_OA + 2048
Q_IT = Q_OB + 1024
ARENA = max(A_N, Q_IT + 3 * TOK)

SIGNALS = {
    **dict.fromkeys(("h_turned",),
                    [6, 6, 6, 6]),
    **dict.fromkeys(("diag",),
                    [2, 2, 2, 2]),
    **dict.fromkeys(("gt_ps", "gt_evicted"),
                    [4, 4, 4, 4]),
    **dict.fromkeys(("hT_dve", "hT_act"),
                    [12, 12, 12, 12]),
    **dict.fromkeys(("var", "std"),
                    [3, 3, 3, 3]),
    **dict.fromkeys(("qk_ps",),
                    [16, 16, 10, 16]),
    **dict.fromkeys(("qkT_dve", "qkT_act"),
                    [8, 8, 5, 8]),
    **dict.fromkeys(("sc_ps", "p_ready", "pT_ready", "pT_ps", "o_ps", "o_ready", "mx"),
                    [24, 24, 24, 24]),
    **dict.fromkeys(("g_ps", "g_ready", "oh_ready"),
                    [48, 48, 48, 48]),
    **dict.fromkeys(("gelu", "w_ready"),
                    [64, 64, 64, 64]),
    **dict.fromkeys(("s_ps", "qs_ready"),
                    [16, 16]),
    **dict.fromkeys(("s_ready",),
                    [12, 12]),
    **dict.fromkeys(("pr_evicted",),
                    [12, 15]),
    **dict.fromkeys(("o_turned", "oT_ready"),
                    [6, 6]),
    **dict.fromkeys(("it_ready", "pick_ps"),
                    [3, 3]),
    **dict.fromkeys(("mixed", "picked", "tv_ready", "tv_exp"),
                    [1, 1]),
}


def since(name, n):
    return sum(SIGNALS[name][:n])


def build(nc, a):
    ctx = ExitStack()
    with ctx:
        sems = {}

        def sem(name):
            if name not in sems:
                sems[name] = ctx.enter_context(nc.semaphore(name))
            return sems[name]

        def sb(name, n):
            return ctx.enter_context(nc.sbuf_tensor(name, [P, n], F32))

        ring = sb("ring", RING * 1024)
        arena = sb("arena", ARENA)
        X = sb("x", 3 * D)
        hT = sb("hT", KC * TOK)
        const = sb("const", C_N)
        rows = sb("rows", R_N)
        mod = sb("mod", MODS * 2)
        bmod = sb("bmod", MODS)
        cT = sb("cT", 16)
        cs = sb("cs", 16)
        gtb = sb("gtb", 2 * D)
        lnr = sb("lnr", 2 * D)
        tmpx = sb("tmpx", D)
        ktab = sb("ktab", 2 * KEYS)
        zero = sb("zero", 512)
        stat = sb("stat", 3 * 12)
        mv = sb("mv", 6)
        rstd = sb("rstd", 3)
        nm = sb("nm", 24)
        nms = sb("nms", 24)
        rs = sb("rs", 24)
        rr = sb("rr", 24)
        lam = sb("lam", 6)
        ss = sb("ss", 32)
        ss2 = sb("ss2", 32)
        ps = ctx.enter_context(nc.psum_tensor("ps", [P, 8, 512], F32))

        def ar(off, n):
            return arena[:, off:off + n]

        uq_w, ukv_w, ckvT = ar(A_O, 1536), ar(A_O + 1536, 1024), ar(A_O + 2560, 512)
        cqT = ar(A_P, 2 * TOK)
        ident = const[:, C_ID:C_ID + 128]
        iota = const[:, C_IOTA:C_IOTA + 128]
        ones = const[:, C_ONES:C_ONES + 128]
        Xv = X[:, :].rearrange("p (t d) -> p t d", t=NT)
        hTv = hT[:, :].rearrange("p (k t) -> p k t", k=KC)
        modv = mod[:, :].rearrange("p (l j k c) -> p l j k c", l=LAYERS, j=6, k=KC)
        gtv = gtb[:, :].rearrange("p (c d) -> p c d", c=2)
        lnv = lnr[:, :].rearrange("p (j d) -> p j d", j=2)
        slot = [ring[:, n * 1024:(n + 1) * 1024] for n in range(RING)]
        PR = ar(A_PR, 3 * 2304).rearrange("p (t n) -> p t n", t=NT)
        QR = ar(A_QR, 3 * 768).rearrange("p (t n) -> p t n", t=NT)
        KR = ar(A_KR, 4 * 768).rearrange("p (b h n) -> p b h n", b=4, h=8)
        VR = ar(A_VR, 4 * 512).rearrange("p (b n) -> p b n", b=4)
        CA = ar(A_CA, 1024).rearrange("p (j n) -> p j n", j=2)
        CB = ar(A_CB, 256)
        QT = ar(A_QT, 8 * TOK).rearrange("p (j t) -> p j t", j=8)
        KT = ar(A_KT, 8 * 512).rearrange("p (j t) -> p j t", j=8)
        PB = ar(A_P, 2 * TOK).rearrange("p (j t) -> p j t", j=2)
        PT = ar(A_PT, 2 * TOK).rearrange("p (j t) -> p j t", j=2)
        O = ar(A_O, 3 * D).rearrange("p (t n) -> p t n", t=NT)
        BIAS = ar(A_BIAS, 4096).rearrange("p (t h n) -> p t h n", t=2, h=8)
        SC = ar(A_SC, 2 * TOK).rearrange("p (j t) -> p j t", j=2)
        lq = lambda j: rows[:, R_LAM + 64 * j:R_LAM + 64 * j + 64]

        plan, uses = {}, [0] * RING

        def staged(stage, chunks):
            plan[stage] = list(uses)
            for c in range(chunks):
                uses[c % RING] += 1

        staged("mod", MODS)
        for l in range(LAYERS):
            staged(("in", l), 4 * -(-IN_W[l] // 512))
            staged(("out", l), 8)
            staged(("q", l), 16)
            for hf in range(2):
                staged(("uv", l, hf), 2 * HALF)

        def nth(stage, c):
            return c % RING, plan[stage][c % RING] + c // RING

        def loaded(pos):
            return sem(f"slot_loaded{pos}")

        def used(pos):
            return sem(f"slot_used{pos}")

        COND = (0, 1, 1)

        def q_rows(l, g, t, j):
            if l == 0:
                return PR[:, t, 64 * j:64 * j + 64] if g == 0 else QR[:, t, 96 * j:96 * j + 96]
            return PR[:, t, 64 * j:64 * j + 64] if g == 0 else PR[:, t, 768 + 64 * j:832 + 64 * j]

        def k_rows(l, g, b, j):
            if l == 0:
                if g == 1:
                    return KR[:, b, j, :]
                return PR[:, b, 512 + 64 * j:576 + 64 * j] if b < 3 else CA[:, 0, 64 * j:64 * j + 64]
            if g == 0:
                return PR[:, b, 512 + 64 * j:576 + 64 * j] if b < 3 else CB[:, 64 * j:64 * j + 64]
            return PR[:, b, 1280 + 64 * j:1344 + 64 * j] if b < 3 else CA[:, 0, 64 * j:64 * j + 64]

        def v_rows(l, g, b, j):
            if l == 0:
                if g == 1:
                    return VR[:, b, 64 * j:64 * j + 64]
                h = j // 2
                return PR[:, b, 1024 + 128 * h:1152 + 128 * h] if b < 3 else CA[:, 1, 128 * h:128 * h + 128]
            if g == 0:
                h = j // 4
                return PR[:, b, 640 + 64 * h:704 + 64 * h] if b < 3 else CB[:, 128 + 64 * h:192 + 64 * h]
            return PR[:, b, 1792 + 64 * j:1856 + 64 * j] if b < 3 else CA[:, 1, 64 * j:64 * j + 64]

        def group(l, g):
            if l == 0 and g == 1:
                return 96, 8, (lambda j: j), 96 ** -0.5
            if l == 1 and g == 0:
                return 64, 2, (lambda j: j // 4), 64 ** -0.5
            return 64, 8, (lambda j: j), 64 ** -0.5

        JOBS = [(j, t) for j in range(8) for t in range(NT)]

        def blocks(t):
            return [0] if t == 0 else [1, 2, 3]

        def out_cols(l, g, j):
            if l == 0 and g == 0:
                return 128 * (j // 2), 128
            return 512 * g + 64 * j, 64

        skew = nc.dram_tensor("skewed_bias", (120, 64, 127), F32, kind="Internal").ap()

        block = ctx.enter_context(nc.Block())

        @block.sync
        def _(sp):
            def load(pos, src, wait):
                if wait is not None:
                    sp.wait_ge(used(pos), wait)
                sp.dma_start(slot[pos], src).then_inc(loaded(pos), 16)

            def stream(stage, src):
                for c in range(src.shape[0]):
                    pos, before = nth(stage, c)
                    load(pos, src[c], before)

            for s in range(RING):
                load(s, a["w_mod"][s], None)
            with sp.Fori(1, MODS // RING) as i:
                for s in range(RING):
                    load(s, a["w_mod"][i * RING + s], i)
            for l in range(LAYERS):
                stream(("in", l), a[f"w_in{l}"])
                stream(("out", l), a[f"w_out{l}"])
                stream(("q", l), a["w_q"][l])
                for hf in range(2):
                    base = plan["uv", l, hf]
                    with sp.Fori(0, HALF // 4) as i:
                        for s in range(4):
                            load(s, a["u"][l][i * 4 + (HALF * hf + s)], i + base[s])
                            load(4 + s, a["v"][l][i * 4 + (HALF * hf + s)], i + base[4 + s])

        @block.gpsimd
        def _(pool):
            pool.dma_start(const[:, :], a["const"]).then_inc(sem("const_in"), 16)
            pool.dma_start(cT[:, :], a["cT"]).then_inc(sem("small_in"), 16)
            pool.dma_start(bmod[:, :], a["b_mod"]).then_inc(sem("small_in"), 16)
            pool.dma_start(rows[:, :], a["rows"].partition_broadcast(P)).then_inc(sem("small_in"), 16)
            pool.dma_start(Xv, a["x"].rearrange("(t p) d -> p t d", p=P)).then_inc(sem("x_in"), 16)
            pool.dma_start(uq_w[:, :].rearrange("p (k n) -> p k n", k=2),
                           a["w_uq"].rearrange("(k p) n -> p k n", p=P)).then_inc(sem("uw_in"), 16)
            pool.dma_start(ukv_w[:, :], a["w_ukv"]).then_inc(sem("uw_in"), 16)
            pool.dma_start(skew,
                           a["rpb"].unsqueeze(1).to_broadcast([120, 64, 127])).then_inc(sem("skew"), 16)
            pool.memset(zero[:, :], 0.0).then_inc(sem("zero_set"), 1)

            def store(dst, src, name):
                pool.dma_start(dst, src).then_inc(sem(name), 16)

            for l in range(LAYERS):
                for w in range(2):
                    n = 2 * l + w
                    if n:
                        pool.wait_ge(sem(f"x_ready{n}"), NT)
                    if w == 0:
                        if l == 0:
                            pool.dma_start(CA[:, 0, :], a["cache_a_k"]).then_inc(sem("cache0"), 16)
                            pool.dma_start(CA[:, 1, :], a["cache_a_v"]).then_inc(sem("cache0"), 16)
                            pool.dma_start(CB[:, 0:128], a["cache_b_ckv"]).then_inc(sem("cache0"), 16)
                            pool.dma_start(CB[:, 128:160], a["cache_b_kr"]).then_inc(sem("cache0"), 16)
                        else:
                            pool.dma_start(CB[:, 0:128], a["cache_c_k"]).then_inc(sem("cache1"), 16)
                            pool.dma_start(CB[:, 128:256], a["cache_c_v"]).then_inc(sem("cache1"), 16)
                            pool.dma_start(CA[:, 0, :], a["cache_d_k"]).then_inc(sem("cache1"), 16)
                            pool.dma_start(CA[:, 1, :], a["cache_d_v"]).then_inc(sem("cache1"), 16)
                            pool.wait_ge(sem("skew"), 16)
                            for r in range(4):
                                for h in range(8):
                                    src = bass.AP(skew.tensor, (h * 15 + 7 - r) * 64 * 127 + 63,
                                                  [[126, 64], [64 * 127, 4], [1, 64]])
                                    p0 = 64 * (r % 2)
                                    dst = BIAS[p0:p0 + 64, r // 2, h, :].rearrange("p (a c) -> p a c", a=4)
                                    pool.dma_start(dst, src).then_inc(sem("bias_in"), 16)
                    pool.dma_start(lnr[:, :], a["ln"][n:n + 1, :].rearrange("a n -> (a n)").partition_broadcast(P)
                                   ).then_inc(sem("ln_in"), 16)
                    if w == 0:
                        pool.wait_ge(sem("pr_evicted"), since("pr_evicted", l) + NT * (4 + l))
                        if l == 0:
                            store(a["state_a_k"], PR[:, 0, 512:1024], "state0")
                            store(a["state_a_v"], PR[:, 0, 1024:1536], "state0")
                            store(a["state_b_kr"], PR[:, 0, 1920:1952], "state0")
                            pool.wait_ge(sem("ckv_ready"), 1)
                            store(a["state_b_ckv"], PR[:, 0, 1792:1920], "state0")
                        else:
                            store(a["state_c_v"], PR[:, 0, 640:768], "state1")
                            store(a["state_d_k"], PR[:, 0, 1280:1792], "state1")
                            store(a["state_d_v"], PR[:, 0, 1792:2304], "state1")
                            pool.wait_ge(sem("prep1"), 1)
                            store(a["state_c_k"], PR[:, 0, 512:640], "state1")
                        pool.dma_start(ktab[:, :].rearrange("p (j n) -> p j n", j=2),
                                       a["keys"][l]).then_inc(sem("keys_in"), 16)
                        pool.wait_ge(sem(f"state{l}"), 64)
            pool.wait_ge(sem("x_ready4"), NT)
            store(a["y"].rearrange("(t p) d -> p t d", p=P), Xv, "y_out")
            pool.wait_ge(sem("y_out"), 16)

        @block.tensor
        def _(pe):
            mm = pe.matmul

            pe.wait_ge(sem("silu_ready"), 1)
            csv = cs[:, :].rearrange("p (k c) -> p k c", k=KC)
            with pe.Fori(0, MODS // RING) as i:
                for s in range(RING):
                    pe.wait_ge(loaded(s), i * 16 + 16)
                    sv = slot[s].rearrange("p (k n) -> p k n", k=KC)
                    for k in range(KC):
                        ins = mm(ps[:, 7, bass.ds(i * (2 * RING) + 2 * s, 2)], sv[:, k, :], csv[:, k, :],
                                 start=(k == 0), stop=(k == KC - 1))
                    ins.then_inc(used(s), 1)

            def turn(name, src, first_wait):
                for t in range(NT):
                    first_wait(t)
                    for q in range(2):
                        for k in range(4):
                            ins = pe.transpose(ps[:, 2 * t + q, 128 * k:128 * k + 128],
                                               src[:, t, 128 * (4 * q + k):128 * (4 * q + k) + 128], ident)
                        ins.then_inc(sem(name), 1)

            def gates(n):
                for c in range(2):
                    pe.wait_ge(sem("diag"), since("diag", n) + c + 1)
                    for q in range(2):
                        if c:
                            pe.wait_ge(sem("gt_evicted"), since("gt_evicted", n) + q + 1)
                        mm(ps[:, 6 + q, :], ones, tmpx[:, 512 * q:512 * q + 512], start=True, stop=True
                           ).then_inc(sem("gt_ps"), 1)

            def project(stage, width):
                for g in range((width + 511) // 512):
                    n = min(512, width - 512 * g)
                    for q in range(4):
                        pos, use = nth(stage, 4 * g + q)
                        pe.wait_ge(loaded(pos), 16 * use + 16)
                        sv = slot[pos].rearrange("p (k n) -> p k n", k=2)
                        for t in range(NT):
                            if g >= 2 and q == 0:
                                pe.wait_ge(sem("pr_evicted"), since("pr_evicted", stage[1]) + NT * (g - 2) + t + 1)
                            for k in range(2):
                                ins = mm(ps[:, t + 3 * (g % 2), 0:n], hTv[:, 2 * q + k, P * t:P * t + P],
                                         sv[:, k, 0:n], start=(q == 0 and k == 0), stop=(q == 3 and k == 1))
                        ins.then_inc(used(pos), 1)

            def wait_h(n):
                pe.wait_ge(sem("hT_dve"), since("hT_dve", n) + 12)
                pe.wait_ge(sem("hT_act"), since("hT_act", n) + 12)

            def attention(l, g):
                d, nk, kmap, _ = group(l, g)
                for n in range(8 + nk):
                    if n >= 2:
                        if n % 2 == 0:
                            pe.wait_ge(sem("qkT_dve"), since("qkT_dve", 2 * l + g) + n // 2)
                        else:
                            pe.wait_ge(sem("qkT_act"), since("qkT_act", 2 * l + g) + n // 2)
                    if n < 8:
                        for t in range(NT):
                            ins = pe.transpose(ps[0:d, 6 + n % 2, P * t:P * t + P], q_rows(l, g, t, n), ident)
                    else:
                        for b in range(4):
                            ins = pe.transpose(ps[0:d, 6 + n % 2, P * b:P * b + P], k_rows(l, g, b, n - 8), ident)
                    ins.then_inc(sem("qk_ps"), 1)
                pe.wait_ge(sem("qkT_dve"), since("qkT_dve", 2 * l + g) + (8 + nk) // 2)
                pe.wait_ge(sem("qkT_act"), since("qkT_act", 2 * l + g) + (8 + nk) // 2)
                N = len(JOBS)
                biased = l == 1 and g == 1
                for i in range(N + 2):
                    if i < N:
                        j, t = JOBS[i]
                        k0, kn = (0, P) if t == 0 else (P, TOK)
                        if i >= 2:
                            pe.wait_ge(sem("p_ready"), since("p_ready", 2 * l + g) + i - 1)
                        mm(ps[:, i % 2, 0:kn], QT[0:d, j, P * t:P * t + P], KT[0:d, kmap(j), k0:k0 + kn],
                           start=True, stop=True).then_inc(sem("sc_ps"), 1)
                    if 1 <= i <= N:
                        m = i - 1
                        j, t = JOBS[m]
                        pe.wait_ge(sem("p_ready"), since("p_ready", 2 * l + g) + m + 1)
                        if m >= 2:
                            pe.wait_ge(sem("pT_ready"), since("pT_ready", 2 * l + g) + m - 1)
                        for b in range(len(blocks(t))):
                            ins = pe.transpose(ps[:, 2 + m % 2, P * b:P * b + P], PB[:, m % 2, P * b:P * b + P], ident)
                        ins.then_inc(sem("pT_ps"), 1)
                    if i >= 2:
                        m = i - 2
                        j, t = JOBS[m]
                        pe.wait_ge(sem("pT_ready"), since("pT_ready", 2 * l + g) + m + 1)
                        if m >= 2:
                            pe.wait_ge(sem("o_ready"), since("o_ready", 2 * l + g) + m - 1)
                        bl = blocks(t)
                        _, dv = out_cols(l, g, j)
                        for x, b in enumerate(bl):
                            ins = mm(ps[:, 4 + m % 2, 0:dv], PT[:, m % 2, P * x:P * x + P], v_rows(l, g, b, j),
                                     start=(x == 0), stop=(x == len(bl) - 1))
                        ins.then_inc(sem("o_ps"), 1)

            def latent():
                pe.wait_ge(sem("cq_ready"), 1)
                pe.wait_ge(sem("ckv_ready"), 1)
                for k in range(2):
                    for t in range(NT):
                        ins = pe.transpose(ps[:, k, P * t:P * t + P], PR[:, t, 1536 + P * k:1664 + P * k], ident)
                    ins.then_inc(sem("c_ps"), 1)
                for b in range(4):
                    src = PR[:, b, 1792:1920] if b < 3 else CB[:, 0:128]
                    ins = pe.transpose(ps[:, 2, P * b:P * b + P], src, ident)
                ins.then_inc(sem("c_ps"), 1)
                pe.wait_ge(sem("cT_ready"), 3)
                pe.wait_ge(sem("uw_in"), 32)
                n = 0
                for t in range(NT):
                    for q in range(2):
                        if n >= 4:
                            pe.wait_ge(sem("up_ready"), n - 3)
                        w = 512 - 256 * q
                        for k in range(2):
                            ins = mm(ps[:, 4 + n % 4, 0:w], cqT[:, TOK * k + P * t:TOK * k + P * t + P],
                                     uq_w[:, 768 * k + 512 * q:768 * k + 512 * q + w], start=(k == 0), stop=(k == 1))
                        ins.then_inc(sem("up_ps"), 1)
                        n += 1
                for b in range(4):
                    for q in range(2):
                        pe.wait_ge(sem("up_ready"), n - 3)
                        mm(ps[:, 4 + n % 4, :], ckvT[:, P * b:P * b + P], ukv_w[:, 512 * q:512 * q + 512],
                           start=True, stop=True).then_inc(sem("up_ps"), 1)
                        n += 1

            def retrieve(l):
                pe.wait_ge(sem("keys_in"), 16 * (l + 1))
                pe.wait_ge(sem("gt_evicted"), since("gt_evicted", 2 * l + 1) + 4)
                for c in range(17):
                    if c < 16:
                        pos, use = nth(("q", l), c)
                        pe.wait_ge(loaded(pos), 16 * use + 16)
                        if c >= 2:
                            pe.wait_ge(sem("qs_ready"), since("qs_ready", l) + c - 1)
                        sv = slot[pos].rearrange("p (k n) -> p k n", k=KC)
                        for k in range(KC):
                            ins = mm(ps[:, 6 + c % 2, 0:TOK], sv[:, k, :], hTv[:, k, :],
                                     start=(k == 0), stop=(k == KC - 1))
                        ins.then_inc(used(pos), 1)
                    if c >= 1:
                        m = c - 1
                        pe.wait_ge(sem("qs_ready"), since("qs_ready", l) + m + 1)
                        if m % 4 == 0 and m >= 8:
                            pe.wait_ge(sem("s_ready"), since("s_ready", l) + NT * (m // 4 - 1))
                        for t in range(NT):
                            ins = mm(ps[:, t + 3 * (m // 4 % 2), P * (m % 4):P * (m % 4) + P],
                                     ar(Q_QS, 2 * TOK)[:, TOK * (m % 2) + P * t:TOK * (m % 2) + P * t + P],
                                     ktab[:, KEYS * (m % 2):KEYS * (m % 2) + KEYS], start=True, stop=True)
                        ins.then_inc(sem("s_ps"), 1)
                pe.wait_ge(sem("picked"), since("picked", l) + 1)
                for q in range(3):
                    for t in range(NT):
                        ins = pe.transpose(ps[:, q, P * t:P * t + P],
                                           ar(Q_ID, 9 * 128)[:, 128 * (NT * q + t):128 * (NT * q + t) + 128], ident)
                    ins.then_inc(sem("pick_ps"), 1)

            def weights(l, hf):

                def pair(i, first):
                    for p in range(2):
                        pe.wait_ge(sem("oh_ready"), since("oh_ready", 2 * l + hf) + i * 2 + (p + 1))
                        if not first:
                            pe.wait_ge(sem("g_ready"), since("g_ready", 2 * l + hf) + i * 2 + (p - 1))
                        for x in range(8):
                            oa = ar(Q_OA, 2048)[:, 1024 * p + P * x:1024 * p + P * x + P]
                            ob = ar(Q_OB, 1024)[:, 512 * p + HALF * x:512 * p + HALF * x + HALF]
                            ins = mm(ps[:, 6 + p, HALF * x:HALF * x + HALF], oa, ob, start=True, stop=True)
                        ins.then_inc(sem("g_ps"), 1)

                pair(0, True)
                with pe.Fori(1, TOK // 16) as i:
                    pair(i, False)

            def experts(l, hf):
                base = plan["uv", l, hf]
                if hf == 0:
                    pe.wait_ge(sem("it_ready"), since("it_ready", l) + 3)
                    pe.wait_ge(sem("zero_set"), 1)
                    for b in range(6):
                        mm(ps[:, b, :], zero[0:1, 0:128], zero[0:1, :], start=True, stop=False,
                           skip_group_check=True)
                wv = ar(Q_W, 4 * TOK).rearrange("p (s t) -> p s t", s=4)

                def hidden(i, s, free):
                    pe.wait_ge(loaded(s), i * 16 + (16 * base[s] + 16))
                    if free:
                        pe.wait_ge(sem("gelu"), since("gelu", 2 * l + hf) + i * 4 + (s - 1))
                    else:
                        pe.wait_ge(sem("g_ready"), since("g_ready", 2 * l + hf) + TOK // 8)
                    sv = slot[s].rearrange("p (k n) -> p k n", k=KC)
                    for k in range(KC):
                        ins = mm(ps[:, 6 + s % 2, 0:TOK], sv[:, k, :], hTv[:, k, :],
                                 start=(k == 0), stop=(k == KC - 1))
                    ins.then_inc(used(s), 1)

                def outer(i, s):
                    pe.wait_ge(loaded(4 + s), i * 16 + (16 * base[4 + s] + 16))
                    pe.wait_ge(sem("w_ready"), since("w_ready", 2 * l + hf) + i * 4 + (s + 1))
                    for t in range(NT):
                        for q in range(2):
                            ins = mm(ps[:, t + 3 * q, :], wv[:, s, P * t:P * t + P],
                                     slot[4 + s][:, 512 * q:512 * q + 512], start=False, stop=False,
                                     skip_group_check=True)
                    ins.then_inc(used(4 + s), 1)

                last = HALF // 4 - 1
                hidden(0, 0, False)
                for s in range(4):
                    if s < 3:
                        hidden(0, s + 1, s >= 1)
                    else:
                        hidden(1, 0, True)
                    outer(0, s)
                with pe.Fori(1, last) as i:
                    for s in range(4):
                        if s < 3:
                            hidden(i, s + 1, True)
                        else:
                            hidden(i + 1, 0, True)
                        outer(i, s)
                for s in range(4):
                    if s < 3:
                        hidden(last, s + 1, True)
                    outer(last, s)
                if hf == 1:
                    for b in range(6):
                        mm(ps[:, b, :], zero[0:1, 0:128], zero[0:1, :], start=False, stop=True,
                           skip_group_check=True).then_inc(sem(f"y_ps{2 * l + 1}"), 1)

            pe.wait_ge(sem("const_in"), 16)
            for l in range(LAYERS):
                n = 2 * l
                turn("h_turned", Xv, lambda t: pe.wait_ge(sem("x_in"), 16) if l == 0 else
                     pe.wait_ge(sem(f"x_ready{n}"), t + 1))
                gates(n)
                wait_h(n)
                project(("in", l), IN_W[l])
                pe.wait_ge(sem(f"prep{l}"), 1)
                pe.wait_ge(sem(f"cache{l}"), 64)
                if l == 0:
                    latent()
                    pe.wait_ge(sem("up_ready"), 14)
                attention(l, 0)
                if l == 0:
                    pe.wait_ge(sem("q_roped"), 2)
                attention(l, 1)
                pe.wait_ge(sem("o_ready"), since("o_ready", 2 * l + 1) + 24)
                turn("o_turned", O, lambda t: pe.wait_ge(sem("sub_normed"), t + 1) if l == 0 else None)
                pe.wait_ge(sem("oT_ready"), since("oT_ready", l) + 6)
                project(("out", l), D)
                turn("h_turned", Xv, lambda t: pe.wait_ge(sem(f"x_ready{n + 1}"), t + 1))
                gates(n + 1)
                wait_h(n + 1)
                retrieve(l)
                for hf in range(2):
                    weights(l, hf)
                    experts(l, hf)

        @block.scalar
        def _(act):
            fn = act.activation

            act.wait_ge(sem("small_in"), 48)
            fn(cs[:, :], cT[:, :], ACT.Exp, scale=-1.0).then_inc(sem("silu_exp"), 1)
            act.wait_ge(sem("lam_dots"), 1)
            fn(lam[:, 2:4], lam[:, 0:2], ACT.Exp).then_inc(sem("lam_exp"), 1)

            def features(n):
                l, w = n // 2, n % 2
                act.wait_ge(sem("mod_ready"), 1)
                for t in range(NT):
                    for q in (1,):
                        act.wait_ge(sem("h_turned"), since("h_turned", n) + 2 * t + q + 1)
                        for k in range(4):
                            kk = 4 * q + k
                            fn(hTv[:, kk, P * t:P * t + P], ps[:, 2 * t + q, P * k:P * k + P], ACT.Identity,
                               scale=modv[:, l, 3 * w + 1, kk, COND[t]:COND[t] + 1],
                               bias=modv[:, l, 3 * w, kk, COND[t]:COND[t] + 1]).then_inc(sem("hT_act"), 1)

            def gate_rows(n):
                for c in range(2):
                    for q in range(2):
                        act.wait_ge(sem("gt_ps"), since("gt_ps", n) + 2 * c + q + 1)
                        fn(gtv[:, c, 512 * q:512 * q + 512], ps[:, 6 + q, :], ACT.Copy
                           ).then_inc(sem("gt_evicted"), 1)

            def attention(l, g):
                d, nk, kmap, scale = group(l, g)
                for n in range(1, 8 + nk, 2):
                    act.wait_ge(sem("qk_ps"), since("qk_ps", 2 * l + g) + n + 1)
                    if n < 8:
                        fn(QT[0:d, n, :], ps[0:d, 6 + n % 2, 0:TOK], ACT.Copy).then_inc(sem("qkT_act"), 1)
                    else:
                        fn(KT[0:d, n - 8, :], ps[0:d, 6 + n % 2, :], ACT.Copy).then_inc(sem("qkT_act"), 1)
                N = len(JOBS)
                biased = l == 1 and g == 1
                for i in range(N + 1):
                    if i < N:
                        j, t = JOBS[i]
                        kn = P if t == 0 else TOK
                        act.wait_ge(sem("mx"), since("mx", 2 * l + g) + i + 1)
                        if i >= 2:
                            act.wait_ge(sem("pT_ps"), since("pT_ps", 2 * l + g) + i - 1)
                        in_sb = biased and t > 0
                        src = SC[:, i % 2, 0:kn] if in_sb else ps[:, i % 2, 0:kn]
                        fn(PB[:, i % 2, 0:kn], src, ACT.Exp, bias=nms[:, i:i + 1], scale=1.0 if in_sb else scale,
                           accum_out=rs[:, i:i + 1]).then_inc(sem("p_ready"), 1)
                    if i >= 1:
                        m = i - 1
                        j, t = JOBS[m]
                        kn = P if t == 0 else TOK
                        act.wait_ge(sem("pT_ps"), since("pT_ps", 2 * l + g) + m + 1)
                        if m >= 2:
                            act.wait_ge(sem("o_ps"), since("o_ps", 2 * l + g) + m - 1)
                        fn(PT[:, m % 2, 0:kn], ps[:, 2 + m % 2, 0:kn], ACT.Copy).then_inc(sem("pT_ready"), 1)

            def root(dst, src, scale, wait, done, pieces=1):
                act.wait_ge(sem(wait), pieces)
                fn(dst, src, ACT.Sqrt, scale=scale, bias=epsc).then_inc(sem(done), 1)

            epsc = lam[:, 5:6]
            for l in range(LAYERS):
                n = 2 * l
                features(n)
                gate_rows(n)
                if l:
                    act.wait_ge(sem("state0"), 64)
                for g in range((IN_W[l] + 511) // 512):
                    w = min(512, IN_W[l] - 512 * g)
                    for t in range(NT):
                        pos, use = nth(("in", l), 4 * g + 3)
                        act.wait_ge(used(pos), use + 1)
                        fn(PR[:, t, 512 * g:512 * g + w], ps[:, t + 3 * (g % 2), 0:w], ACT.Copy
                           ).then_inc(sem("pr_evicted"), 1)
                if l == 0:
                    root(ss2[:, 0:3], ss[:, 0:3], 1 / 256, "cq_ss", "cq_root")
                    root(ss2[:, 3:6], ss[:, 3:6], 1 / 128, "ckv_ss", "ckv_root")
                    for k in range(2):
                        act.wait_ge(sem("c_ps"), k + 1)
                        fn(cqT[:, TOK * k:TOK * k + TOK], ps[:, k, 0:TOK], ACT.Copy).then_inc(sem("cT_ready"), 1)
                    act.wait_ge(sem("c_ps"), 3)
                    fn(ckvT[:, :], ps[:, 2, :], ACT.Copy).then_inc(sem("cT_ready"), 1)
                    m = 0
                    for t in range(NT):
                        for q in range(2):
                            act.wait_ge(sem("up_ps"), m + 1)
                            w = 512 - 256 * q
                            fn(QR[:, t, 512 * q:512 * q + w], ps[:, 4 + m % 4, 0:w], ACT.Copy
                               ).then_inc(sem("up_ready"), 1)
                            m += 1
                    for b in range(4):
                        for q in range(2):
                            act.wait_ge(sem("up_ps"), m + 1)
                            kv = ps[:, 4 + m % 4, :].rearrange("p (h j n) -> p h j n", h=4, j=2)
                            fn(KR[:, b, 4 * q:4 * q + 4, 0:64], kv[:, :, 0, :], ACT.Copy)
                            fn(VR[:, b, 256 * q:256 * q + 256].rearrange("p (h n) -> p h n", h=4), kv[:, :, 1, :],
                               ACT.Copy).then_inc(sem("up_ready"), 1)
                            m += 1
                else:
                    root(ss2[:, 0:30], ss[:, 0:30], 1 / 64, "c_ss", "c_root")
                attention(l, 0)
                attention(l, 1)
                if l == 0:
                    root(ss2[:, 0:12], ss[:, 0:12], 1 / 128, "sub_ss", "sub_root", NT)
                for b in range(6):
                    act.wait_ge(sem("o_turned"), since("o_turned", l) + b + 1)
                    t, q = b // 2, b % 2
                    fn(hTv[:, 4 * q:4 * q + 4, P * t:P * t + P], ps[:, b, :].rearrange("p (k n) -> p k n", k=4),
                       ACT.Copy).then_inc(sem("oT_ready"), 1)
                for w in range(2):
                    m = n + w
                    if w:
                        features(m)
                        gate_rows(m)
                        for c in range(17):
                            if c < 16:
                                pos, use = nth(("q", l), c)
                                act.wait_ge(used(pos), use + 1)
                                if c >= 2:
                                    act.wait_ge(sem("s_ps"), since("s_ps", l) + c - 1)
                                fn(ar(Q_QS, 2 * TOK)[:, TOK * (c % 2):TOK * (c % 2) + TOK], ps[:, 6 + c % 2, 0:TOK],
                                   ACT.Copy).then_inc(sem("qs_ready"), 1)
                            if c >= 1 and c % 4 == 0:
                                cg = c // 4 - 1
                                act.wait_ge(sem("s_ps"), since("s_ps", l) + 4 * cg + 4)
                                for t in range(NT):
                                    o = Q_S + t * 2048 + 512 * cg
                                    fn(ar(o, 512), ps[:, t + 3 * (cg % 2), :], ACT.Copy
                                       ).then_inc(sem("s_ready"), 1)
                        act.wait_ge(sem("tv_ready"), since("tv_ready", l) + 1)
                        fn(ar(Q_TV, 384), ar(Q_TV, 384), ACT.Exp).then_inc(sem("tv_exp"), 1)
                        for q in range(3):
                            act.wait_ge(sem("pick_ps"), since("pick_ps", l) + q + 1)
                            fn(ar(Q_IT + TOK * q, TOK), ps[:, q, 0:TOK], ACT.Copy).then_inc(sem("it_ready"), 1)
                        for hf in range(2):
                            gv = ar(0, CORE).rearrange("p (e t) -> p e t", e=HALF)
                            if hf:
                                act.wait_ge(sem("w_ready"), since("w_ready", 2 * l) + HALF)

                            def evict(i):
                                for p in range(2):
                                    act.wait_ge(sem("g_ps"), since("g_ps", 2 * l + hf) + i * 2 + (p + 1))
                                    fn(gv[:, :, bass.ds(i * 16 + 8 * p, 8)],
                                       ps[:, 6 + p, :].rearrange("p (t e) -> p e t", t=8), ACT.Copy
                                       ).then_inc(sem("g_ready"), 1)

                            with act.Fori(0, TOK // 16) as i:
                                evict(i)
                            wv = ar(Q_W, 4 * TOK).rearrange("p (s t) -> p s t", s=4)

                            base = plan["uv", l, hf]

                            def gelus(i, first):
                                for s in range(4):
                                    act.wait_ge(used(s), i + (base[s] + 1))
                                    if not first:
                                        act.wait_ge(used(4 + s), i + base[4 + s])
                                    fn(wv[:, s, :], ps[:, 6 + s % 2, 0:TOK], ACT.Gelu).then_inc(sem("gelu"), 1)

                            gelus(0, True)
                            with act.Fori(1, HALF // 4) as i:
                                gelus(i, False)
                    for t in range(NT):
                        act.wait_ge(sem("var"), since("var", m) + t + 1)
                        fn(rstd[:, t:t + 1], mv[:, 2 * t + 1:2 * t + 2], ACT.Sqrt, bias=epsc
                           ).then_inc(sem("std"), 1)

        @block.vector
        def _(dve):
            linked = [0]

            def link(ins):
                linked[0] += 1
                ins.then_inc(sem("dve_link"), 1)
                dve.wait_ge(sem("dve_link"), linked[0])

            tt, ts, stt = dve.tensor_tensor, dve.tensor_scalar, dve.scalar_tensor_tensor

            dve.memset(lam[:, 5:6], EPS).then_inc(sem("eps_set"), 1)
            dve.wait_ge(sem("silu_exp"), 1)
            link(ts(cs[:, :], cs[:, :], 1.0, None, ALU.add))
            link(dve.reciprocal(cs[:, :], cs[:, :]))
            tt(cs[:, :], cs[:, :], cT[:, :], ALU.mult).then_inc(sem("silu_ready"), 1)
            for j in range(2):
                link(tt(tmpx[:, 64 * j:64 * j + 64], lq(2 * j), lq(2 * j + 1), ALU.mult))
            dve.tensor_reduce(lam[:, 0:2], tmpx[:, 0:128].rearrange("p (j n) -> p j n", j=2), AX.X, ALU.add
                              ).then_inc(sem("lam_dots"), 1)
            dve.wait_ge(sem("lam_exp"), 1)
            link(tt(lam[:, 4:5], lam[:, 3:4], lam[:, 2:3], ALU.subtract))
            link(ts(lam[:, 4:5], lam[:, 4:5], -LAM_INIT, None, ALU.add))
            link(ts(rows[:, R_SUB:R_SUB + 128], rows[:, R_SUB:R_SUB + 128], 1.0 - LAM_INIT, None, ALU.mult))
            dve.wait_ge(used(RING - 1), MODS // RING)
            link(tt(mod[:, :].rearrange("p (m c) -> p m c", c=2),
                    ps[:, 7, 0:2 * MODS].rearrange("p (m c) -> p m c", c=2),
                    bmod[:, :].unsqueeze(2).to_broadcast([P, MODS, 2]), ALU.add))
            mf = mod[:, :].rearrange("p (l j n) -> p l j n", l=LAYERS, j=6)
            ts(mf[:, :, 1:5:3, :], mf[:, :, 1:5:3, :], 1.0, None, ALU.add).then_inc(sem("mod_ready"), 1)
            dve.wait_ge(sem("mod_ready"), 1)
            dve.wait_ge(sem("const_in"), 16)

            def features(n):
                l, w = n // 2, n % 2
                for t in range(NT):
                    for q in (0,):
                        dve.wait_ge(sem("h_turned"), since("h_turned", n) + 2 * t + q + 1)
                        for k in range(4):
                            kk = 4 * q + k
                            ts(hTv[:, kk, P * t:P * t + P], ps[:, 2 * t + q, P * k:P * k + P],
                               modv[:, l, 3 * w + 1, kk, COND[t]:COND[t] + 1],
                               modv[:, l, 3 * w, kk, COND[t]:COND[t] + 1],
                               ALU.mult, ALU.add).then_inc(sem("hT_dve"), 1)

            def diagonals(n):
                l, w = n // 2, n % 2
                for c in range(2):
                    if c:
                        dve.wait_ge(sem("gt_ps"), since("gt_ps", n) + 2)
                    tt(tmpx[:, :].rearrange("p (k n) -> p k n", k=KC),
                       ident.unsqueeze(1).to_broadcast([P, KC, P]),
                       modv[:, l, 3 * w + 2, :, c:c + 1].to_broadcast([P, KC, P]), ALU.mult
                       ).then_inc(sem("diag"), 1)

            def norm(n):
                dve.wait_ge(sem("gt_evicted"), since("gt_evicted", n) + 4)
                dve.wait_ge(sem("ln_in"), 16 * (n + 1))
                for t in range(NT):
                    for q in range(2):
                        if n % 2 == 0:
                            pos, use = nth(("out", n // 2), 4 * q + 3)
                            dve.wait_ge(used(pos), use + 1)
                        else:
                            dve.wait_ge(sem(f"y_ps{n}"), 6)
                        ins = tt(tmpx[:, 512 * q:512 * q + 512], ps[:, t + 3 * q, :],
                                 gtv[:, COND[t], 512 * q:512 * q + 512], ALU.mult)
                    link(ins)
                    link(stt(Xv[:, t, :], Xv[:, t, :], ALPHA, tmpx[:, :], ALU.mult, ALU.add))
                    for q in range(2):
                        ins = dve.bn_stats(stat[:, 12 * t + 6 * q:12 * t + 6 * q + 6], Xv[:, t, 512 * q:512 * q + 512])
                    link(ins)
                    dve.bn_aggr(mv[:, 2 * t:2 * t + 2], stat[:, 12 * t:12 * t + 12]).then_inc(sem("var"), 1)
                for t in range(NT):
                    dve.wait_ge(sem("std"), since("std", n) + t + 1)
                    link(dve.reciprocal(rstd[:, t:t + 1], rstd[:, t:t + 1]))
                    link(ts(Xv[:, t, :], Xv[:, t, :], mv[:, 2 * t:2 * t + 1], rstd[:, t:t + 1],
                            ALU.subtract, ALU.mult))
                    link(tt(Xv[:, t, :], Xv[:, t, :], lnv[:, 0, :], ALU.mult))
                    tt(Xv[:, t, :], Xv[:, t, :], lnv[:, 1, :], ALU.add).then_inc(sem(f"x_ready{n + 1}"), 1)

            TMP = ar(A_TMP, 2048)

            def rope(x, heads, half, cosv, sinv, done=None):
                tmp = TMP[:, 0:heads * 2 * half].rearrange("p (h n) -> p h n", h=heads)

                def over(v):
                    return v.unsqueeze(1).to_broadcast([P, heads, v.shape[-1]])
                tt(tmp[:, :, 0:half], x[:, :, half:2 * half], over(sinv[:, 0:half]), ALU.mult)
                link(tt(tmp[:, :, half:2 * half], x[:, :, 0:half], over(sinv[:, half:2 * half]), ALU.mult))
                link(tt(x, x, over(cosv), ALU.mult))
                ins = tt(x, x, tmp, ALU.add)
                if done:
                    ins.then_inc(sem(done), 1)
                else:
                    link(ins)

            def table(c, t, w):
                return const[:, c + w * (t - 1):c + w * t]

            def prep0():
                dve.wait_ge(sem("pr_evicted"), since("pr_evicted", 0) + 12)
                for at, w, off, r, name in ((1536, 256, 0, R_CQ, "cq"), (1792, 128, 3, R_CKV, "ckv")):
                    x = PR[:, :, at:at + w]
                    tmp = TMP[:, 0:3 * w].rearrange("p (t n) -> p t n", t=NT)
                    link(tt(tmp, x, x, ALU.mult))
                    dve.tensor_reduce(ss[:, off:off + 3], tmp, AX.X, ALU.add).then_inc(sem(f"{name}_ss"), 1)
                    dve.wait_ge(sem(f"{name}_ss"), 1)
                for at, w, off, r, name in ((1536, 256, 0, R_CQ, "cq"), (1792, 128, 3, R_CKV, "ckv")):
                    x = PR[:, :, at:at + w]
                    dve.wait_ge(sem(f"{name}_root"), 1)
                    link(dve.reciprocal(ss2[:, off:off + 3], ss2[:, off:off + 3]))
                    link(tt(x, x, ss2[:, off:off + 3].unsqueeze(2).to_broadcast([P, NT, w]), ALU.mult))
                    tt(x, x, rows[:, r:r + w].unsqueeze(1).to_broadcast([P, NT, w]), ALU.mult
                       ).then_inc(sem("ckv_ready" if name == "ckv" else "cq_ready"), 1)
                for t in (1, 2):
                    rope(PR[:, t, 0:1024].rearrange("p (h n) -> p h n", h=16), 16, 32,
                         table(C_COSA, t, 64), table(C_SINA, t, 64))
                    rope(PR[:, t, 1920:1952].rearrange("p (h n) -> p h n", h=1), 1, 16,
                         table(C_COSB, t, 32), table(C_SINB, t, 32))
                dve.wait_ge(sem("cache0"), 64)
                for b in range(4):
                    src = PR[:, b, 1920:1952] if b < 3 else CB[:, 128:160]
                    ins = dve.tensor_copy(KR[:, b, :, 64:96], src.unsqueeze(1).to_broadcast([P, 8, 32]))
                ins.then_inc(sem("prep0"), 1)

            def prep1():
                dve.wait_ge(sem("pr_evicted"), since("pr_evicted", 1) + 15)
                x = PR[:, :, 0:640].rearrange("p t (h n) -> p t h n", h=10)
                tmp = TMP[:, 0:1920].rearrange("p (t h n) -> p t h n", t=NT, h=10)
                sv = ss[:, 0:30].rearrange("p (t h) -> p t h", t=NT)
                link(tt(tmp, x, x, ALU.mult))
                dve.tensor_reduce(sv, tmp, AX.X, ALU.add).then_inc(sem("c_ss"), 1)
                dve.wait_ge(sem("c_root"), 1)
                link(dve.reciprocal(ss2[:, 0:30], ss2[:, 0:30]))
                s2 = ss2[:, 0:30].rearrange("p (t h) -> p t h", t=NT)
                link(tt(x, x, s2.unsqueeze(3).to_broadcast([P, NT, 10, 64]), ALU.mult))
                for t in range(NT):
                    tt(x[:, t, 0:8, :], x[:, t, 0:8, :],
                       rows[:, R_QN:R_QN + 64].unsqueeze(1).to_broadcast([P, 8, 64]), ALU.mult)
                    link(tt(x[:, t, 8:10, :], x[:, t, 8:10, :],
                            rows[:, R_KN:R_KN + 64].unsqueeze(1).to_broadcast([P, 2, 64]), ALU.mult))
                for t in (1, 2):
                    rope(PR[:, t, 0:640].rearrange("p (h n) -> p h n", h=10), 10, 32,
                         table(C_COSA, t, 64), table(C_SINA, t, 64))
                dve.wait_ge(sem("bias_in"), 16 * 32)
                bv = ar(A_BIAS, 4096).rearrange("p (n c) -> p n c", c=64)
                tt(bv, bv, const[:, C_MASK:C_MASK + 64].unsqueeze(1).to_broadcast([P, 64, 64]), ALU.add
                   ).then_inc(sem("prep1"), 1)

            def attention(l, g):
                d, nk, kmap, scale = group(l, g)
                if l == 0 and g == 1:
                    dve.wait_ge(sem("up_ready"), 6)
                    for t in (1, 2):
                        if t == 2:
                            dve.wait_ge(sem("q_roped"), 1)
                        rope(QR[:, t, :].rearrange("p (h n) -> p h n", h=8)[:, :, 64:96], 8, 16,
                             table(C_COSB, t, 32), table(C_SINB, t, 32), "q_roped")
                for n in range(0, 8 + nk, 2):
                    dve.wait_ge(sem("qk_ps"), since("qk_ps", 2 * l + g) + n + 1)
                    if n < 8:
                        dve.tensor_copy(QT[0:d, n, :], ps[0:d, 6, 0:TOK]).then_inc(sem("qkT_dve"), 1)
                    else:
                        dve.tensor_copy(KT[0:d, n - 8, :], ps[0:d, 6, :]).then_inc(sem("qkT_dve"), 1)
                N = len(JOBS)
                biased = l == 1 and g == 1
                for i in range(N + 2):
                    if i < N:
                        j, t = JOBS[i]
                        kn = P if t == 0 else TOK
                        dve.wait_ge(sem("sc_ps"), since("sc_ps", 2 * l + g) + i + 1)
                        if biased and t > 0:
                            if i >= 2:
                                dve.wait_ge(sem("p_ready"), since("p_ready", 2 * l + g) + i - 1)
                            stt(SC[:, i % 2, 0:256], ps[:, i % 2, 0:256], scale, BIAS[:, t - 1, j, :],
                                ALU.mult, ALU.add)
                            link(ts(SC[:, i % 2, 256:384], ps[:, i % 2, 256:384], scale, None, ALU.mult))
                            link(dve.tensor_reduce(nm[:, i:i + 1], SC[:, i % 2, :], AX.X, ALU.max))
                            ts(nms[:, i:i + 1], nm[:, i:i + 1], -1.0, None, ALU.mult).then_inc(sem("mx"), 1)
                        else:
                            link(dve.tensor_reduce(nm[:, i:i + 1], ps[:, i % 2, 0:kn], AX.X, ALU.max))
                            ts(nms[:, i:i + 1], nm[:, i:i + 1], -scale, None, ALU.mult).then_inc(sem("mx"), 1)
                    if i >= 2:
                        m = i - 2
                        j, t = JOBS[m]
                        c0, dv = out_cols(l, g, j)
                        dve.wait_ge(sem("o_ps"), since("o_ps", 2 * l + g) + m + 1)
                        link(dve.reciprocal(rr[:, m:m + 1], rs[:, m:m + 1]))
                        dst, src = O[:, t, c0:c0 + dv], ps[:, 4 + m % 2, 0:dv]
                        if l == 0 and g == 0 and j % 2:
                            link(tt(rr[:, m:m + 1], rr[:, m:m + 1], lam[:, 4:5], ALU.mult))
                            stt(dst, src, rr[:, m:m + 1], dst, ALU.mult, ALU.add).then_inc(sem("o_ready"), 1)
                        else:
                            ts(dst, src, rr[:, m:m + 1], None, ALU.mult).then_inc(sem("o_ready"), 1)

            def sub_norm():
                dve.wait_ge(sem("o_ready"), since("o_ready", 0) + 24)
                for t in range(NT):
                    tmp = TMP[:, 0:512].rearrange("p (h n) -> p h n", h=4)
                    x = O[:, t, 0:512].rearrange("p (h n) -> p h n", h=4)
                    link(tt(tmp, x, x, ALU.mult))
                    dve.tensor_reduce(ss[:, 4 * t:4 * t + 4], tmp, AX.X, ALU.add).then_inc(sem("sub_ss"), 1)
                    dve.wait_ge(sem("sub_ss"), t + 1)
                dve.wait_ge(sem("sub_root"), 1)
                link(dve.reciprocal(ss2[:, 0:12], ss2[:, 0:12]))
                for t in range(NT):
                    x = O[:, t, 0:512].rearrange("p (h n) -> p h n", h=4)
                    link(tt(x, x, ss2[:, 4 * t:4 * t + 4].unsqueeze(2).to_broadcast([P, 4, 128]), ALU.mult))
                    tt(x, x, rows[:, R_SUB:R_SUB + 128].unsqueeze(1).to_broadcast([P, 4, 128]), ALU.mult
                       ).then_inc(sem("sub_normed"), 1)

            def retrieve(l):
                S = ar(Q_S, NT * 2048).rearrange("p (t c n) -> p t c n", t=NT, c=16)
                V = ar(Q_V, NT * 256).rearrange("p (t c n) -> p t c n", t=NT, c=16)
                Iu = ar(Q_I, NT * 256).bitcast(U32).rearrange("p (t c n) -> p t c n", t=NT, c=16)
                IF = ar(Q_IF, NT * 256).rearrange("p (t c n) -> p t c n", t=NT, c=16)

                def top16(pieces):
                    for s, v, x in pieces:
                        ins = dve.max(v[:, 0:8], s)
                    link(ins)
                    for s, v, x in pieces:
                        ins = dve.max_index(x[:, 0:8], v[:, 0:8], s)
                    link(ins)
                    for s, v, x in pieces:
                        ins = dve.match_replace(s, v[:, 0:8], s, NEG)
                    link(ins)
                    for s, v, x in pieces:
                        ins = dve.max(v[:, 8:16], s)
                    link(ins)
                    for s, v, x in pieces:
                        ins = dve.max_index(x[:, 8:16], v[:, 8:16], s)
                    link(ins)

                for cg in range(4):
                    dve.wait_ge(sem("s_ready"), since("s_ready", l) + NT * (cg + 1))
                    top16([(S[:, t, c, :], V[:, t, c, :], Iu[:, t, c, :]) for t in range(NT)
                           for c in range(4 * cg, 4 * cg + 4)])
                dve.tensor_copy(ar(Q_IF, NT * 256), ar(Q_I, NT * 256).bitcast(U32))
                Vh = ar(Q_V, NT * 256).rearrange("p (t h j n) -> p t h j n", t=NT, h=HEADS, j=2)
                for t in range(NT):
                    ins = tt(ar(Q_S + 2048 * t, 2048).rearrange("p (h a b) -> p h a b", h=HEADS, a=TOPK),
                             Vh[:, t, :, 0, :].unsqueeze(3).to_broadcast([P, HEADS, TOPK, TOPK]),
                             Vh[:, t, :, 1, :].unsqueeze(2).to_broadcast([P, HEADS, TOPK, TOPK]), ALU.add)
                link(ins)
                C = ar(Q_S, NT * 2048).rearrange("p (t h n) -> p t h n", t=NT, h=HEADS)
                TV = ar(Q_TV, NT * 128).rearrange("p (t h n) -> p t h n", t=NT, h=HEADS)
                TP = ar(Q_TP, NT * 128).bitcast(U32).rearrange("p (t h n) -> p t h n", t=NT, h=HEADS)
                top16([(C[:, t, h, :], TV[:, t, h, :], TP[:, t, h, :]) for t in range(NT) for h in range(HEADS)])
                Tf = ar(Q_TV, NT * 128).rearrange("p (m n) -> p m n", n=TOPK)
                dve.tensor_copy(ss[:, 0:24], Tf[:, :, 0]).then_inc(sem("dve_link"), 1)
                linked[0] += 1
                dve.wait_ge(sem("dve_link"), linked[0])
                tt(Tf, Tf, ss[:, 0:24].unsqueeze(2).to_broadcast([P, 24, TOPK]), ALU.subtract
                   ).then_inc(sem("tv_ready"), 1)
                pos = ar(Q_TP, 384).bitcast(U32)
                ts(ar(Q_AB, 384).bitcast(U32), pos, 4, None, ALU.logical_shift_right)
                link(ts(ar(Q_AB + 384, 384).bitcast(U32), pos, 15, None, ALU.bitwise_and))
                link(dve.tensor_copy(ar(Q_ABF, 768), ar(Q_AB, 768).bitcast(U32)))
                IFh = ar(Q_IF, NT * 256).rearrange("p (t h j n) -> p t h j n", t=NT, h=HEADS, j=2)
                eq = ar(Q_EQ, 2048)
                for j in range(2):
                    for t in range(NT):
                        link(tt(eq.rearrange("p (m n) -> p m n", n=TOPK),
                                ar(Q_ABF + 384 * j + 128 * t, 128).unsqueeze(2).to_broadcast([P, 128, TOPK]),
                                iota[:, 0:TOPK].unsqueeze(1).to_broadcast([P, 128, TOPK]), ALU.is_equal))
                        e4 = eq.rearrange("p (h k n) -> p h k n", h=HEADS, k=TOPK)
                        link(tt(e4, e4, IFh[:, t, :, j, :].unsqueeze(2).to_broadcast([P, HEADS, TOPK, TOPK]), ALU.mult))
                        link(dve.tensor_reduce(ar(Q_ID + 128 * (NT * j + t), 128),
                                               eq.rearrange("p (m n) -> p m n", n=TOPK), AX.X, ALU.add))
                dve.wait_ge(sem("tv_exp"), since("tv_exp", l) + 1)
                link(dve.tensor_reduce(ss[:, 0:24], Tf, AX.X, ALU.add))
                link(dve.reciprocal(ss2[:, 0:24], ss[:, 0:24]))
                tt(ar(Q_ID + 768, 384).rearrange("p (m n) -> p m n", n=TOPK), Tf,
                   ss2[:, 0:24].unsqueeze(2).to_broadcast([P, 24, TOPK]), ALU.mult).then_inc(sem("picked"), 1)

            def experts(l, hf):
                if hf == 0:
                    dve.wait_ge(sem("it_ready"), since("it_ready", l) + 3)

                def pair(i, first):
                    for p in range(2):
                        if not first:
                            dve.wait_ge(sem("g_ps"), since("g_ps", 2 * l + hf) + i * 2 + (p - 1))
                        for x in range(8):
                            col = i * 16 + (8 * p + x)
                            it = [ar(Q_IT, 3 * TOK)[:, bass.ds(col + TOK * q, 1)] for q in range(3)]
                            ts(ar(Q_OA + 1024 * p + P * x, P), iota, it[0], it[2], ALU.is_equal, ALU.mult)
                            ins = ts(ar(Q_OB + 512 * p + HALF * x, HALF), iota[:, HALF * hf:HALF * hf + HALF],
                                     it[1], None, ALU.is_equal)
                        ins.then_inc(sem("oh_ready"), 1)

                pair(0, True)
                with dve.Fori(1, TOK // 16) as i:
                    pair(i, False)
                with dve.Fori(0, HALF // 4) as i:
                    for s in range(4):
                        dve.wait_ge(sem("gelu"), since("gelu", 2 * l + hf) + i * 4 + (s + 1))
                        w = ar(Q_W + TOK * s, TOK)
                        tt(w, w, ar(0, CORE)[:, bass.ds(i * (4 * TOK) + TOK * s, TOK)], ALU.mult
                           ).then_inc(sem("w_ready"), 1)

            for l in range(LAYERS):
                n = 2 * l
                features(n)
                diagonals(n)
                (prep0 if l == 0 else prep1)()
                attention(l, 0)
                attention(l, 1)
                if l == 0:
                    sub_norm()
                norm(n)
                features(n + 1)
                diagonals(n + 1)
                retrieve(l)
                for hf in range(2):
                    experts(l, hf)
                norm(n + 1)


def kernel(**inputs):
    import numpy as np
    import concourse.bacc as _bacc
    from concourse import mybir as _mybir
    from concourse.bass_utils import run_bass_kernel_spmd as _run

    g = {k: np.asarray(v) for k, v in inputs.items()}
    f = np.float32

    def columns(w, n):
        w = w.reshape(8, 128, n // 128, 128)
        return np.ascontiguousarray(w.transpose(2, 1, 0, 3)).reshape(n // 128, 128, 1024)

    def wide(w):
        n = -(-w.shape[1] // 512) * 512
        w = np.pad(w, ((0, 0), (0, n - w.shape[1])))
        w = w.reshape(4, 2, 128, n // 512, 512)
        return np.ascontiguousarray(w.transpose(3, 0, 2, 1, 4)).reshape(n // 128, 128, 1024)

    const = np.zeros((128, C_N), f)
    const[:, C_ID:C_ID + 128] = np.eye(128)
    const[:, C_IOTA:C_IOTA + 128] = np.arange(128)
    const[:, C_ONES:C_ONES + 128] = 1
    tok = np.arange(256)
    for rot, c_cos, c_sin in ((64, C_COSA, C_SINA), (32, C_COSB, C_SINB)):
        nf = rot // 4
        inv = (f(10000.0) ** (-np.arange(nf, dtype=f) / f(nf))).astype(f)
        ang = np.concatenate([(tok // 64).astype(f)[:, None] * inv, (tok % 64).astype(f)[:, None] * inv], 1)
        cos, sin = np.cos(ang).astype(f), np.sin(ang).astype(f)
        for t in range(2):
            r = slice(128 * t, 128 * t + 128)
            const[:, c_cos + rot * t:c_cos + rot * t + rot] = np.concatenate([cos[r], cos[r]], 1)
            const[:, c_sin + rot * t:c_sin + rot * t + rot] = np.concatenate([-sin[r], sin[r]], 1)
    qc = np.arange(128) % 64
    c0 = np.clip(qc - 8, 0, 48)
    kc = np.arange(64)
    ok = (kc[None] >= c0[:, None]) & (kc[None] < c0[:, None] + 16)
    const[:, C_MASK:C_MASK + 64] = np.where(ok, 0, -1e30)

    arrays = {
        "x": np.concatenate([g["x_prompt"][0], g["x_sample"][0]]),
        "const": const,
        "cT": np.stack([g["c_ctx"], g["c"][0]]).reshape(2, 8, 128).transpose(2, 1, 0).reshape(128, 16),
        "b_mod": g["b_mod"].reshape(96, 128).T,
        "rows": np.concatenate([g["ev_lam_q1"][0], g["ev_lam_k1"][0], g["ev_lam_q2"][0], g["ev_lam_k2"][0],
                                g["ev_g_sub"][0], g["ev_g_cq"][0], g["ev_g_ckv"][0], g["od_g_qn"][0],
                                g["od_g_kn"][0]]),
        "ln": np.stack([np.concatenate([g[f"ln{w}_g"][l], g[f"ln{w}_b"][l]]) for l in range(2) for w in (1, 2)]),
        "w_mod": np.concatenate([columns(g["w_mod"][l], 6144) for l in range(2)]),
        "w_in0": wide(g["ev_w_in"][0]), "w_in1": wide(g["od_w_in"][0]),
        "w_out0": wide(g["ev_w_out"][0]), "w_out1": wide(g["od_w_out"][0]),
        "w_q": np.stack([columns(g["pk_w_q"][l], 2048) for l in range(2)]),
        "u": g["pk_u"].reshape(2, 128, 128, 8, 128).transpose(0, 2, 4, 3, 1).reshape(2, 128, 128, 1024),
        "v": g["pk_v"].reshape(2, 128, 128, 1024).transpose(0, 2, 1, 3),
        "keys": np.stack([g["pk_k1"].transpose(0, 2, 1), g["pk_k2"].transpose(0, 2, 1)], 2),
        "w_uq": g["ev_w_uq"][0], "w_ukv": g["ev_w_ukv"][0],
        "rpb": np.pad(g["od_rpb"][0], ((0, 0), (0, 0), (48, 48))).reshape(120, 127),
        "cache_a_k": g["cache_a_k"].reshape(128, 512), "cache_a_v": g["cache_a_v"].reshape(128, 512),
        "cache_b_ckv": g["cache_b_ckv"].reshape(128, 128), "cache_b_kr": g["cache_b_kr"].reshape(128, 32),
        "cache_c_k": g["cache_c_k"].reshape(128, 128), "cache_c_v": g["cache_c_v"].reshape(128, 128),
        "cache_d_k": g["cache_d_k"].reshape(128, 512), "cache_d_v": g["cache_d_v"].reshape(128, 512),
    }
    outs = {"y": (384, 1024), "state_a_k": (128, 512), "state_a_v": (128, 512), "state_b_ckv": (128, 128),
            "state_b_kr": (128, 32), "state_c_k": (128, 128), "state_c_v": (128, 128), "state_d_k": (128, 512),
            "state_d_v": (128, 512)}
    nc = _bacc.Bacc("TRN2", target_bir_lowering=False, num_devices=1)
    sent, args = {}, {}
    for k, v in arrays.items():
        v = np.ascontiguousarray(v)
        assert v.dtype == np.float32, k
        sent[f"in_{k}"] = v
        args[k] = nc.dram_tensor(f"in_{k}", v.shape, _mybir.dt.float32, kind="ExternalInput").ap()
    for k, shape in outs.items():
        args[k] = nc.dram_tensor(f"out_{k}", shape, _mybir.dt.float32, kind="ExternalOutput").ap()
    build(nc, args)
    r = _run(nc, [sent], core_ids=[0]).results[0]
    o = {k: r[f"out_{k}"] for k in outs}
    return (o["y"][:128].reshape(1, 128, 1024), o["y"][128:].reshape(1, 256, 1024),
            o["state_a_k"].reshape(1, 1, 128, 4, 2, 64), o["state_a_v"].reshape(1, 1, 128, 4, 128),
            o["state_b_ckv"].reshape(1, 1, 128, 128), o["state_b_kr"].reshape(1, 1, 128, 32),
            o["state_c_k"].reshape(1, 1, 128, 2, 64), o["state_c_v"].reshape(1, 1, 128, 2, 64),
            o["state_d_k"].reshape(1, 1, 128, 8, 64), o["state_d_v"].reshape(1, 1, 128, 8, 64))
```

```python
from contextlib import ExitStack

import concourse.bass as bass
from concourse import mybir

F32 = mybir.dt.float32
U32 = mybir.dt.uint32
F32R = mybir.dt.float32r
F16 = mybir.dt.float16
ALU = mybir.AluOpType
ACT = mybir.ActivationFunctionType
AX = mybir.AxisListType

P = 128
D = 1024
KC = D // P
NT = 3
TOK = NT * P
LAYERS = 2
EPS = 1e-6
ALPHA = (2 * LAYERS) ** 0.25
LAM_INIT = 0.2
NEG = -3.0e38
RING = 4
HEADS = 8
TOPK = 16
KEYS = 128
QUARTER = 32
PIECE = TOK // QUARTER
G_N = QUARTER * TOK
SPILL = 64
G_SCALE = 16384.0
IN_W = (1952, 2304)
MODS = LAYERS * 6 * KC
MOD_N = MODS * P
MOD_USES = MODS // RING

C_ID, C_IOTA, C_ONES, C_N = 0, 128, 256, 384
T_COSA, T_SINA = 0, 128
T_COSB, T_SINB = 256, 320
T_MASK, T_N = 384, 448
R_SUB, R_CQ, R_CKV, R_QN, R_KN, R_N = 0, 128, 384, 512, 576, 640

A_PR = 0
A_QR = A_PR + 3 * 2304
A_KR = A_QR + 3 * 768
A_VR = A_KR + 4 * 768
A_CA = A_VR + 4 * 512
A_CB = A_CA + 2 * 512
A_QT = A_CB + 256
A_KT = A_QT + 8 * TOK
A_P = A_KT + 8 * 512
A_PT = A_P + 2 * TOK
A_TMP = A_PT + 2 * TOK
A_TAB = A_TMP + 2048
A_N = A_TAB + T_N
A_BIAS, A_SC = A_QR, A_QR + 4096
Q_S = 0
Q_V = Q_S + NT * 16 * 128
Q_I = Q_V + NT * 16 * 16
Q_IF = Q_I + NT * 16 * 16
Q_TV = Q_IF + NT * 16 * 16
Q_TP = Q_TV + NT * 128
Q_AB = Q_TP + NT * 128
Q_ABF = Q_AB + 2 * NT * 128
Q_EQ = Q_ABF + 2 * NT * 128
Q_ID = Q_EQ + 2048
Q_QS = Q_ID + 3 * NT * 128
Q_W32 = Q_QS
assert Q_QS + 2 * TOK <= 2 * G_N
Q_GL = 2 * G_N
Q_OA = Q_GL + 2 * TOK
OA_N = KEYS * PIECE // 2
OB_N = QUARTER * PIECE // 2
Q_OB = Q_OA + OA_N
Q_E2 = Q_OB + 2 * OB_N
Q_IOT = Q_E2 + OB_N
Q_IT = Q_IOT + OA_N
ARENA = max(A_N, Q_IT + 2 * TOK)
A_GT, A_LN, A_DIAG, A_WORK = A_QT, A_KT, A_P, A_QT + 2 * D
Q_GT, Q_LN, Q_DIAG, Q_WORK = 3 * D, 5 * D, 7 * D, 8 * D

SIGNALS = {
    **dict.fromkeys(("h_turned",), [6, 6, 6, 6]),
    **dict.fromkeys(("diag",), [2, 2, 2, 2]),
    **dict.fromkeys(("gt_ps", "gt_evicted"), [4, 4, 4, 4]),
    **dict.fromkeys(("h_act", "xhi_act", "xlo_dve", "xlo_pool"), [3, 3, 3, 3]),
    **dict.fromkeys(("var", "std"), [3, 3, 3, 3]),
    **dict.fromkeys(("qk_ps",), [16, 16, 10, 16]),
    **dict.fromkeys(("qkT_dve", "qkT_act"), [8, 8, 5, 8]),
    **dict.fromkeys(("sc_ps", "p_ready", "pT_ready", "pT_ps", "o_ps", "o_ready", "mx"), [24, 24, 24, 24]),
    **dict.fromkeys(("g_ps", "g_ready", "oh_ready", "e2_ready", "gelu", "w_full", "w_hi", "w_ready"), [128, 128]),
    **dict.fromkeys(("s_ps", "qs_ready"), [16, 16]),
    **dict.fromkeys(("s_ready",), [12, 12]),
    **dict.fromkeys(("pr_evicted",), [12, 15]),
    **dict.fromkeys(("o_turned", "oT_hi", "oT_ready"), [6, 6]),
    **dict.fromkeys(("it_ready", "pick_ps"), [3, 3]),
    **dict.fromkeys(("picked", "tv_ready", "tv_exp"), [1, 1]),
}


def since(name, n):
    return sum(SIGNALS[name][:n])


def build(nc, a):
    ctx = ExitStack()
    with ctx:
        sems = {}

        def sem(name):
            if name not in sems:
                sems[name] = ctx.enter_context(nc.semaphore(name))
            return sems[name]

        def sb(name, n):
            return ctx.enter_context(nc.sbuf_tensor(name, [P, n], F32))

        ring = sb("ring", RING * 1024)
        arena = sb("arena", ARENA)
        X = sb("x", 3 * D)

        def sbr(name, n):
            return ctx.enter_context(nc.sbuf_tensor(name, [P, n], F32R))

        ring_hi, ring_lo = sbr("ring_hi", RING * 1024), sbr("ring_lo", RING * 1024)
        x_hi, x_lo = sbr("x_hi", KC * TOK), sbr("x_lo", KC * TOK)
        w_hi, w_lo = sbr("w_hi", 2 * TOK), sbr("w_lo", 2 * TOK)
        const = sb("const", C_N)
        rows = sb("rows", R_N)
        mod = sb("mod", MODS * 2)
        bmod = sb("bmod", MODS)
        cT = sb("cT", 16)
        cs = sb("cs", 16)
        ktab = sb("ktab", 2 * KEYS)
        stat = sb("stat", 3 * 12)
        mv = sb("mv", 6)
        rstd = sb("rstd", 3)
        nm = sb("nm", 24)
        nms = sb("nms", 24)
        rs = sb("rs", 24)
        rr = sb("rr", 24)
        lam = sb("lam", 6)
        ss = sb("ss", 32)
        ss2 = sb("ss2", 32)
        ps = ctx.enter_context(nc.psum_tensor("ps", [P, 8, 512], F32))

        def ar(off, n):
            return arena[:, off:off + n]

        uq_w, ukv_w, ckvT = ar(A_KT, 1536), ar(A_KT + 1536, 1024), ar(A_KT + 2560, 512)
        cqT = ar(A_P, 2 * TOK)
        ident = const[:, C_ID:C_ID + 128]
        iota = const[:, C_IOTA:C_IOTA + 128]
        ones = const[:, C_ONES:C_ONES + 128]
        Xv = X[:, :].rearrange("p (t d) -> p t d", t=NT)
        HF = ar(0, KC * TOK).rearrange("p (k t) -> p k t", k=KC)
        xh = x_hi[:, :].rearrange("p (k t) -> p k t", k=KC)
        xl = x_lo[:, :].rearrange("p (k t) -> p k t", k=KC)
        modv = mod[:, :].rearrange("p (c l j k) -> p l j k c", c=2, l=LAYERS, j=6)

        def gate_room(n):
            return ar(Q_GT if n % 2 else A_GT, 2 * D).rearrange("p (c d) -> p c d", c=2)

        def norm_room(n):
            return ar(Q_LN if n % 2 else A_LN, 2 * D)

        def diag_room(n, c):
            return work_room(n) if c == 0 else ar(Q_DIAG if n % 2 else A_DIAG, D)

        def work_room(n):
            return ar(Q_WORK if n % 2 else A_WORK, D)

        def f32(x):
            return x.bitcast(F32)

        slot = [ring[:, n * 1024:(n + 1) * 1024] for n in range(RING)]
        slot_hi = [ring_hi[:, n * 1024:(n + 1) * 1024] for n in range(RING)]
        slot_lo = [ring_lo[:, n * 1024:(n + 1) * 1024] for n in range(RING)]
        GL = ar(Q_GL, 2 * TOK).rearrange("p (s t) -> p s t", s=2)
        PR = ar(A_PR, 3 * 2304).rearrange("p (t n) -> p t n", t=NT)
        QR = ar(A_QR, 3 * 768).rearrange("p (t n) -> p t n", t=NT)
        KR = ar(A_KR, 4 * 768).rearrange("p (b h n) -> p b h n", b=4, h=8)
        VR = ar(A_VR, 4 * 512).rearrange("p (b n) -> p b n", b=4)
        CA = ar(A_CA, 1024).rearrange("p (j n) -> p j n", j=2)
        CB = ar(A_CB, 256)
        QT = ar(A_QT, 8 * TOK).rearrange("p (j t) -> p j t", j=8)
        KT = ar(A_KT, 8 * 512).rearrange("p (j t) -> p j t", j=8)
        PB = ar(A_P, 2 * TOK).rearrange("p (j t) -> p j t", j=2)
        PT = ar(A_PT, 2 * TOK).rearrange("p (j t) -> p j t", j=2)
        TAB = ar(A_TAB, T_N)

        def out_rows(l, t, c, n):
            if c < 512:
                return PR[:, t, c:c + n]
            return QR[:, t, c - 512:c - 512 + n] if l == 0 else PR[:, t, c + 256:c + 256 + n]

        BIAS = ar(A_BIAS, 4096).rearrange("p (t h n) -> p t h n", t=2, h=8)
        SC = ar(A_SC, 2 * TOK).rearrange("p (j t) -> p j t", j=2)
        IOT = ar(Q_IOT, OA_N).bitcast(F16).rearrange("p (e t) -> p e t", e=KEYS)
        IT16 = ar(Q_IT, 2 * TOK).bitcast(F16).rearrange("p (q t) -> p q t", q=4)
        MODC = ar(MOD_N, 2 * P)[0:MODS, :]
        lq = lambda j: ar(A_TMP + 256 + 64 * j, 64)

        start, total = {}, 0
        for l in range(LAYERS):
            for stage, chunks in ((("in", l), 4 * -(-IN_W[l] // 512)), (("out", l), 8), (("q", l), 16),
                                  (("uv", l), 2 * KEYS)):
                start[stage] = total
                total += chunks

        def turn_of(c):
            return c // RING + 1

        def loaded(pos):
            return sem(f"slot_loaded{pos}")

        def mod_used(pos):
            return sem(f"mod_used{pos}")

        def hi_done(pos):
            return sem(f"slot_hi{pos}")

        def lo_done(pos):
            return sem(f"slot_lo{pos}")

        def used(pos):
            return sem(f"slot_used{pos}")

        ROUNDS = SPILL // 2

        COND = (0, 1, 1)

        def q_rows(l, g, t, j):
            if l == 0:
                return PR[:, t, 64 * j:64 * j + 64] if g == 0 else QR[:, t, 96 * j:96 * j + 96]
            return PR[:, t, 64 * j:64 * j + 64] if g == 0 else PR[:, t, 768 + 64 * j:832 + 64 * j]

        def k_rows(l, g, b, j):
            if l == 0:
                if g == 1:
                    return KR[:, b, j, :]
                return PR[:, b, 512 + 64 * j:576 + 64 * j] if b < 3 else CA[:, 0, 64 * j:64 * j + 64]
            if g == 0:
                return PR[:, b, 512 + 64 * j:576 + 64 * j] if b < 3 else CB[:, 64 * j:64 * j + 64]
            return PR[:, b, 1280 + 64 * j:1344 + 64 * j] if b < 3 else CA[:, 0, 64 * j:64 * j + 64]

        def v_rows(l, g, b, j):
            if l == 0:
                h = j // 2
                if g == 1:
                    return VR[:, b, 128 * h:128 * h + 128]
                return PR[:, b, 1024 + 128 * h:1152 + 128 * h] if b < 3 else CA[:, 1, 128 * h:128 * h + 128]
            if g == 0:
                return PR[:, b, 640:768] if b < 3 else CB[:, 128:256]
            h = j // 2
            return PR[:, b, 1792 + 128 * h:1920 + 128 * h] if b < 3 else CA[:, 1, 128 * h:128 * h + 128]

        def v_off(l, g, j):
            if l == 0 and g == 0:
                return 0
            return 64 * (j // 4) if l == 1 and g == 0 else 64 * (j % 2)

        def group(l, g):
            if l == 0 and g == 1:
                return 96, 8, (lambda j: j), 96 ** -0.5
            if l == 1 and g == 0:
                return 64, 2, (lambda j: j // 4), 64 ** -0.5
            return 64, 8, (lambda j: j), 64 ** -0.5

        JOBS = [(j, t) for j in range(8) for t in range(NT)]

        def blocks(t):
            return [0] if t == 0 else [1, 2, 3]

        def out_cols(l, g, j):
            if l == 0 and g == 0:
                return 128 * (j // 2), 128
            return 512 * g + 64 * j, 64

        gl_dram = nc.dram_tensor("gelu_half", (SPILL, P, TOK), F32, kind="Internal").ap()
        mod_dram = nc.dram_tensor("mod_rows", (2, MOD_N), F32, kind="Internal").ap()
        skew = nc.dram_tensor("skewed_bias", (120, 64, 127), F32, kind="Internal").ap()

        block = ctx.enter_context(nc.Block())

        @block.sync
        def _(sp):
            def load(pos, src, turn):
                sp.wait_ge(lo_done(pos), turn)
                sp.dma_start(slot[pos], src).then_inc(loaded(pos), 16)

            def stream(stage, src):
                for c in range(src.shape[0]):
                    g = start[stage] + c
                    if g < RING:
                        sp.wait_ge(mod_used(g), MOD_USES)
                        sp.dma_start(slot[g], src[c]).then_inc(loaded(g), 16)
                    else:
                        load(g % RING, src[c], g // RING)

            for s in range(RING):
                sp.dma_start(slot[s], a["w_mod"][s]).then_inc(loaded(s), 16)
            with sp.Fori(1, MOD_USES) as i:
                for s in range(RING):
                    sp.wait_ge(mod_used(s), i)
                    sp.dma_start(slot[s], a["w_mod"][i * RING + s]).then_inc(loaded(s), 16)
            for l in range(LAYERS):
                stream(("in", l), a[f"w_in{l}"])
                stream(("out", l), a[f"w_out{l}"])
                stream(("q", l), a["w_q"][l])
                u, v = a["u"][l], a["v"][l]
                b0 = start["uv", l] // RING
                groups = SPILL // 4

                def store(i, s):
                    sp.wait_ge(sem("gelu"), i * 4 + (since("gelu", l) + s + 1))
                    sp.dma_start(gl_dram[i * 4 + s], GL[:, s % 2, :]).then_inc(sem(f"gl_stored{s % 2}"), 16)

                def fetch(i, s):
                    sp.wait_ge(sem("w_ready"), i * 4 + (since("w_ready", l) + s + 1))
                    sp.dma_start(GL[:, s % 2, :], gl_dram[i * 4 + (s + 2)]).then_inc(sem(f"gl_loaded{s % 2}"), 16)

                for c in range(8):
                    load(c % 4, u[c], b0 + c // 4)
                with sp.Fori(0, groups - 2) as i:
                    for s in range(4):
                        store(i, s)
                        load(s, u[i * 4 + (8 + s)], i + (b0 + 2))
                with sp.Fori(groups - 2, groups) as i:
                    for s in range(4):
                        store(i, s)
                        load(s, v[i * 4 + (8 + s - SPILL)], i + (b0 + 2))
                for s in range(2):
                    sp.wait_ge(sem(f"gl_stored{s}"), 8 * SPILL * (l + 1))
                    sp.dma_start(GL[:, s, :], gl_dram[s]).then_inc(sem(f"gl_loaded{s}"), 16)
                with sp.Fori(0, groups - 2) as i:
                    for s in range(4):
                        fetch(i, s)
                        load(s, v[i * 4 + (8 + s)], i + (b0 + groups + 2))
                for s, src in enumerate((u[SPILL], u[SPILL + 1], v[SPILL], u[SPILL + 2])):
                    fetch(groups - 2, s)
                    load(s, src, b0 + 2 * groups)
                for s in range(2):
                    fetch(groups - 1, s)
                load(0, v[SPILL + 1], b0 + 2 * groups + 1)
                with sp.Fori(1, ROUNDS - 1) as i:
                    load(1, u[i * 2 + (SPILL + 1)], i + (b0 + 2 * groups))
                    load(2, v[i * 2 + SPILL], i + (b0 + 2 * groups))
                    load(3, u[i * 2 + (SPILL + 2)], i + (b0 + 2 * groups))
                    load(0, v[i * 2 + (SPILL + 1)], i + (b0 + 2 * groups + 1))
                for pos, src in ((1, u[KEYS - 1]), (2, v[KEYS - 2]), (3, v[KEYS - 1])):
                    load(pos, src, b0 + 2 * groups + ROUNDS - 1)

        @block.gpsimd
        def _(pool):
            pool.dma_start(const[:, :], a["const"]).then_inc(sem("const_in"), 16)
            pool.dma_start(cT[:, :], a["cT"]).then_inc(sem("small_in"), 16)
            pool.dma_start(bmod[:, :], a["b_mod"]).then_inc(sem("small_in"), 16)
            pool.dma_start(rows[:, :], a["rows"].partition_broadcast(P)).then_inc(sem("small_in"), 16)
            pool.dma_start(ar(A_TMP + 256, 256), a["lam"].partition_broadcast(P)).then_inc(sem("small_in"), 16)
            pool.dma_start(Xv, a["x"].rearrange("(t p) d -> p t d", p=P)).then_inc(sem("x_in"), 16)
            pool.dma_start(uq_w[:, :].rearrange("p (k n) -> p k n", k=2),
                           a["w_uq"].rearrange("(k p) n -> p k n", p=P)).then_inc(sem("uw_in"), 16)
            pool.dma_start(ukv_w[:, :], a["w_ukv"]).then_inc(sem("uw_in"), 16)
            pool.dma_start(skew,
                           a["rpb"].unsqueeze(1).to_broadcast([120, 64, 127])).then_inc(sem("skew"), 16)

            def store(dst, src, name):
                pool.dma_start(dst, src).then_inc(sem(name), 16)

            def split(first, last):
                def four(t):
                    for s in range(RING):
                        pool.wait_ge(hi_done(s), t + 1)
                        pool.tensor_tensor(slot_lo[s], slot[s], f32(slot_hi[s]), ALU.subtract
                                           ).then_inc(lo_done(s), 1)
                first, last = first // RING, min(last, total) // RING
                if last - first > 4:
                    with pool.Fori(first, last) as t:
                        four(t)
                else:
                    for t in range(first, last):
                        four(t)

            def ahead(stage, first=0, last=None):
                chunks = {"in": 4 * -(-IN_W[stage[1]] // 512), "out": 8, "q": 16, "uv": 2 * KEYS}[stage[0]]
                split(start[stage] + first + RING, start[stage] + (chunks if last is None else last) + RING)

            def features(n):
                for t in range(NT):
                    pool.wait_ge(sem("xhi_act"), since("xhi_act", n) + t + 1)
                    r = slice(P * t, P * t + P)
                    pool.tensor_tensor(xl[:, 4:8, r], HF[:, 4:8, r], f32(xh[:, 4:8, r]), ALU.subtract
                                       ).then_inc(sem("xlo_pool"), 1)

            def norm_rows(n):
                pool.dma_start(norm_room(n), a["ln"][n:n + 1, :].rearrange("a n -> (a n)").partition_broadcast(P)
                               ).then_inc(sem("ln_in"), 16)

            pool.wait_ge(sem("mod_rows"), MODS * P // 512)
            store(mod_dram, ar(0, MOD_N)[0:2, :], "mod_out")
            pool.wait_ge(sem("mod_out"), 16)
            pool.dma_start(MODC.rearrange("m (c n) -> m c n", c=2),
                           mod_dram.rearrange("c (m n) -> m c n", n=P)).then_inc(sem("mod_back"), 16)
            split(0, RING)
            for l in range(LAYERS):
                n = 2 * l
                features(n)
                pool.dma_start(TAB, a["table"]).then_inc(sem("table_in"), 16)
                if l == 0:
                    pool.dma_start(CA[:, 0, :], a["cache_a_k"]).then_inc(sem("cache0"), 16)
                    pool.dma_start(CA[:, 1, :], a["cache_a_v"]).then_inc(sem("cache0"), 16)
                    pool.dma_start(CB[:, 0:128], a["cache_b_ckv"]).then_inc(sem("cache0"), 16)
                    pool.dma_start(CB[:, 128:160], a["cache_b_kr"]).then_inc(sem("cache0"), 16)
                else:
                    pool.dma_start(CB[:, 0:128], a["cache_c_k"]).then_inc(sem("cache1"), 16)
                    pool.dma_start(CB[:, 128:256], a["cache_c_v"]).then_inc(sem("cache1"), 16)
                    pool.dma_start(CA[:, 0, :], a["cache_d_k"]).then_inc(sem("cache1"), 16)
                    pool.dma_start(CA[:, 1, :], a["cache_d_v"]).then_inc(sem("cache1"), 16)
                    pool.wait_ge(sem("skew"), 16)
                    for r in range(4):
                        for h in range(8):
                            src = bass.AP(skew.tensor, (h * 15 + 7 - r) * 64 * 127 + 63,
                                          [[126, 64], [64 * 127, 4], [1, 64]])
                            p0 = 64 * (r % 2)
                            dst = BIAS[p0:p0 + 64, r // 2, h, :].rearrange("p (a c) -> p a c", a=4)
                            pool.dma_start(dst, src).then_inc(sem("bias_in"), 16)
                ahead(("in", l))
                pool.wait_ge(sem("pr_evicted"), since("pr_evicted", l) + NT * (4 + l))
                if l == 0:
                    store(a["state_a_k"], PR[:, 0, 512:1024], "state0")
                    store(a["state_a_v"], PR[:, 0, 1024:1536], "state0")
                    store(a["state_b_kr"], PR[:, 0, 1920:1952], "state0")
                    pool.wait_ge(sem("ckv_ready"), 1)
                    store(a["state_b_ckv"], PR[:, 0, 1792:1920], "state0")
                else:
                    store(a["state_c_v"], PR[:, 0, 640:768], "state1")
                    store(a["state_d_k"], PR[:, 0, 1280:1792], "state1")
                    store(a["state_d_v"], PR[:, 0, 1792:2304], "state1")
                    pool.wait_ge(sem("prep1"), 1)
                    store(a["state_c_k"], PR[:, 0, 512:640], "state1")
                pool.dma_start(ktab[:, :].rearrange("p (j n) -> p j n", j=2),
                               a["keys"][l]).then_inc(sem("keys_in"), 16)
                pool.wait_ge(sem(f"state{l}"), 64)
                pool.wait_ge(sem("o_ready"), since("o_ready", n + 1) + 24)
                norm_rows(n)
                ahead(("out", l))
                features(n + 1)
                ahead(("q", l))
                late = 2 * SPILL + SPILL + 8
                ahead(("uv", l), 0, late)
                pool.wait_ge(sem("w_ready"), since("w_ready", l) + 3 * QUARTER)
                norm_rows(n + 1)
                ahead(("uv", l), late)
            pool.wait_ge(sem("x_ready4"), NT)
            store(a["y"].rearrange("(t p) d -> p t d", p=P), Xv, "y_out")
            pool.wait_ge(sem("y_out"), 16)

        @block.tensor
        def _(pe):
            mm = pe.matmul

            pe.wait_ge(sem("silu_ready"), 1)
            csv = cs[:, :].rearrange("p (k c) -> p k c", k=KC)

            def parts(out, x, y, first, last, check=False):
                mm(out, x[0], y[0], start=first, stop=False, skip_group_check=check)
                mm(out, x[0], y[1], start=False, stop=False, skip_group_check=check)
                return mm(out, x[1], y[0], start=False, stop=last, skip_group_check=check)

            def mod_groups(i, first):
                for g in range(2):
                    for q in range(4):
                        pe.wait_ge(loaded(q), i * 32 + 16 * (g + 1))
                        if q == 0 and not first:
                            pe.wait_ge(sem("mod_rows"), i * 2 + (g - 1))
                        for k in range(2):
                            ins = mm(ps[0:2, g, :], csv[:, 2 * q + k, :], slot[q][:, 512 * k:512 * k + 512],
                                     start=(q == 0 and k == 0), stop=(q == 3 and k == 1))
                        ins.then_inc(mod_used(q), 1)

            mod_groups(0, True)
            with pe.Fori(1, MOD_USES // 2) as i:
                mod_groups(i, False)

            def turn(name, src, first_wait):
                for t in range(NT):
                    first_wait(t)
                    for q in range(2):
                        for k in range(4):
                            ins = pe.transpose(ps[:, 2 * t + q, P * k:P * k + P], src(t, P * (4 * q + k)), ident)
                        ins.then_inc(sem(name), 1)

            def gate(n, c, q, bank):
                pe.wait_ge(sem("diag"), since("diag", n) + c + 1)
                mm(ps[:, bank, :], ones, diag_room(n, c)[:, 512 * q:512 * q + 512], start=True, stop=True
                   ).then_inc(sem("gt_ps"), 1)

            def project(stage, width, between=None):
                for g in range((width + 511) // 512):
                    n = min(512, width - 512 * g)
                    for q in range(4):
                        c = start[stage] + 4 * g + q
                        pos = c % RING
                        pe.wait_ge(lo_done(pos), turn_of(c))
                        for t in range(NT):
                            if g >= 2 and q == 0:
                                pe.wait_ge(sem("pr_evicted"), since("pr_evicted", stage[1]) + NT * (g - 2) + t + 1)
                            for k in range(2):
                                r = slice(P * t, P * t + P)
                                w = slice(512 * k, 512 * k + n)
                                ins = parts(ps[:, t + 3 * (g % 2), 0:n], (xh[:, 2 * q + k, r], xl[:, 2 * q + k, r]),
                                            (slot_hi[pos][:, w], slot_lo[pos][:, w]),
                                            q == 0 and k == 0, q == 3 and k == 1)
                        ins.then_inc(used(pos), 1)
                    if between and g == 0:
                        between()

            def wait_h(n):
                pe.wait_ge(sem("xlo_dve"), since("xlo_dve", n) + NT)
                pe.wait_ge(sem("xlo_pool"), since("xlo_pool", n) + NT)

            def columns_of(pos, out):
                for k in range(KC):
                    r = slice(P * k, P * k + P)
                    ins = parts(out, (slot_hi[pos][:, r], slot_lo[pos][:, r]), (xh[:, k, :], xl[:, k, :]),
                                k == 0, k == KC - 1)
                ins.then_inc(used(pos), 1)

            def attention(l, g):
                d, nk, kmap, _ = group(l, g)
                for n in range(8 + nk):
                    if n >= 2:
                        if n % 2 == 0:
                            pe.wait_ge(sem("qkT_dve"), since("qkT_dve", 2 * l + g) + n // 2)
                        else:
                            pe.wait_ge(sem("qkT_act"), since("qkT_act", 2 * l + g) + n // 2)
                    if n < 8:
                        for t in range(NT):
                            ins = pe.transpose(ps[0:d, 6 + n % 2, P * t:P * t + P], q_rows(l, g, t, n), ident)
                    else:
                        for b in range(4):
                            ins = pe.transpose(ps[0:d, 6 + n % 2, P * b:P * b + P], k_rows(l, g, b, n - 8), ident)
                    ins.then_inc(sem("qk_ps"), 1)
                pe.wait_ge(sem("qkT_dve"), since("qkT_dve", 2 * l + g) + (8 + nk) // 2)
                pe.wait_ge(sem("qkT_act"), since("qkT_act", 2 * l + g) + (8 + nk) // 2)
                N = len(JOBS)
                biased = l == 1 and g == 1
                for i in range(N + 2):
                    if i < N:
                        j, t = JOBS[i]
                        k0, kn = (0, P) if t == 0 else (P, TOK)
                        if i >= 2:
                            pe.wait_ge(sem("p_ready"), since("p_ready", 2 * l + g) + i - 1)
                        mm(ps[:, i % 2, 0:kn], QT[0:d, j, P * t:P * t + P], KT[0:d, kmap(j), k0:k0 + kn],
                           start=True, stop=True).then_inc(sem("sc_ps"), 1)
                    if 1 <= i <= N:
                        m = i - 1
                        j, t = JOBS[m]
                        pe.wait_ge(sem("p_ready"), since("p_ready", 2 * l + g) + m + 1)
                        if m >= 2:
                            pe.wait_ge(sem("pT_ready"), since("pT_ready", 2 * l + g) + m - 1)
                        for b in range(len(blocks(t))):
                            ins = pe.transpose(ps[:, 2 + m % 2, P * b:P * b + P], PB[:, m % 2, P * b:P * b + P], ident)
                        ins.then_inc(sem("pT_ps"), 1)
                    if i >= 2:
                        m = i - 2
                        j, t = JOBS[m]
                        pe.wait_ge(sem("pT_ready"), since("pT_ready", 2 * l + g) + m + 1)
                        if m >= 2:
                            pe.wait_ge(sem("o_ready"), since("o_ready", 2 * l + g) + m - 1)
                        bl = blocks(t)
                        for x, b in enumerate(bl):
                            ins = mm(ps[:, 4 + m % 2, 0:P], PT[:, m % 2, P * x:P * x + P], v_rows(l, g, b, j),
                                     start=(x == 0), stop=(x == len(bl) - 1))
                        ins.then_inc(sem("o_ps"), 1)

            def latent():
                pe.wait_ge(sem("cq_ready"), 1)
                pe.wait_ge(sem("ckv_ready"), 1)
                for k in range(2):
                    for t in range(NT):
                        ins = pe.transpose(ps[:, k, P * t:P * t + P], PR[:, t, 1536 + P * k:1664 + P * k], ident)
                    ins.then_inc(sem("c_ps"), 1)
                for b in range(4):
                    src = PR[:, b, 1792:1920] if b < 3 else CB[:, 0:128]
                    ins = pe.transpose(ps[:, 2, P * b:P * b + P], src, ident)
                ins.then_inc(sem("c_ps"), 1)
                pe.wait_ge(sem("cT_ready"), 3)
                pe.wait_ge(sem("uw_in"), 32)
                n = 0
                for t in range(NT):
                    for q in range(2):
                        if n >= 4:
                            pe.wait_ge(sem("up_ready"), n - 3)
                        w = 512 - 256 * q
                        for k in range(2):
                            ins = mm(ps[:, 4 + n % 4, 0:w], cqT[:, TOK * k + P * t:TOK * k + P * t + P],
                                     uq_w[:, 768 * k + 512 * q:768 * k + 512 * q + w], start=(k == 0), stop=(k == 1))
                        ins.then_inc(sem("up_ps"), 1)
                        n += 1
                for b in range(4):
                    for q in range(2):
                        pe.wait_ge(sem("up_ready"), n - 3)
                        mm(ps[:, 4 + n % 4, :], ckvT[:, P * b:P * b + P], ukv_w[:, 512 * q:512 * q + 512],
                           start=True, stop=True).then_inc(sem("up_ps"), 1)
                        n += 1

            def retrieve(l):
                pe.wait_ge(sem("keys_in"), 16 * (l + 1))
                for c in range(17):
                    if c < 16:
                        g = start["q", l] + c
                        pe.wait_ge(lo_done(g % RING), turn_of(g))
                        if c >= 2:
                            pe.wait_ge(sem("qs_ready"), since("qs_ready", l) + c - 1)
                        columns_of(g % RING, ps[:, 6 + c % 2, 0:TOK])
                    if c >= 1:
                        m = c - 1
                        pe.wait_ge(sem("qs_ready"), since("qs_ready", l) + m + 1)
                        if m % 4 == 0 and m >= 8:
                            pe.wait_ge(sem("s_ready"), since("s_ready", l) + NT * (m // 4 - 1))
                        for t in range(NT):
                            ins = mm(ps[:, t + 3 * (m // 4 % 2), P * (m % 4):P * (m % 4) + P],
                                     ar(Q_QS, 2 * TOK)[:, TOK * (m % 2) + P * t:TOK * (m % 2) + P * t + P],
                                     ktab[:, KEYS * (m % 2):KEYS * (m % 2) + KEYS], start=True, stop=True)
                        ins.then_inc(sem("s_ps"), 1)

            def picks(l):
                pe.wait_ge(sem("s_ready"), since("s_ready", l) + 12)
                pe.wait_ge(sem("picked"), since("picked", l) + 1)
                for q in range(3):
                    for t in range(NT):
                        ins = pe.transpose(ps[:, 2 + q, P * t:P * t + P],
                                           ar(Q_ID, 9 * 128)[:, 128 * (NT * q + t):128 * (NT * q + t) + 128], ident)
                    ins.then_inc(sem("pick_ps"), 1)

            def experts(l):
                b0 = start["uv", l] // RING
                groups = SPILL // 4
                at = {name: since(name, l) for name in ("gelu", "w_ready", "g_ps", "g_ready", "oh_ready")}

                def build(p, bank, free):
                    pe.wait_ge(sem("oh_ready"), p + (at["oh_ready"] + 1))
                    if free is not None:
                        pe.wait_ge(sem("g_ready"), p + (at["g_ready"] + free))
                    oa = ar(Q_OA, OA_N).bitcast(F16).rearrange("p (e t) -> p e t", e=KEYS)
                    ob = ar(Q_OB, 2 * OB_N).bitcast(F16).rearrange("p (j e t) -> p j e t", j=2,
                                                                                      e=QUARTER)
                    for t in range(PIECE):
                        for j in range(2):
                            ins = mm(ps[:, bank, QUARTER * t:QUARTER * t + QUARTER], oa[:, :, t], ob[:, j, :, t],
                                     start=(j == 0), stop=(j == 1))
                    ins.then_inc(sem("g_ps"), 1)

                def hidden(pos, turn, bank, gelus):
                    pe.wait_ge(lo_done(pos), turn)
                    if gelus is not None:
                        pe.wait_ge(sem("gelu"), gelus)
                    columns_of(pos, ps[:, bank, 0:TOK])

                def outer(pos, turn, odd, ready, first=False, last=False):
                    pe.wait_ge(lo_done(pos), turn)
                    pe.wait_ge(sem("w_ready"), ready)
                    for t in range(NT):
                        r = slice(TOK * odd + P * t, TOK * odd + P * t + P)
                        for q in range(2):
                            c = slice(512 * q, 512 * q + 512)
                            ins = parts(ps[:, t + 3 * q, :], (w_hi[:, r], w_lo[:, r]),
                                        (slot_hi[pos][:, c], slot_lo[pos][:, c]), first, last, True)
                    ins.then_inc(used(pos), 1)

                for s in range(4):
                    hidden(s, b0 + 1, 6 + s % 2, at["gelu"] + s - 1 if s >= 2 else None)
                with pe.Fori(1, groups // 2) as i:
                    for s in range(4):
                        hidden(s, i + (b0 + 1), 6 + s % 2, i * 4 + (at["gelu"] + s - 1))
                picks(l)

                def both(i, first):
                    for s in range(4):
                        hidden(s, i + (b0 + 1), 6 + s % 2, i * 4 + (at["gelu"] + s - 1))
                        build(i * 4 + (s - QUARTER), s % 2, None if first and s < 2 else -1)

                both(groups // 2, True)
                with pe.Fori(groups // 2 + 1, groups) as i:
                    both(i, False)
                pe.wait_ge(sem("it_ready"), since("it_ready", l) + 3)
                pe.wait_ge(sem("g_ready"), at["g_ready"] + QUARTER)
                pe.wait_ge(sem("gelu"), at["gelu"] + SPILL)

                def four(i, first):
                    for s in range(4):
                        build(i * 4 + (QUARTER + s), 7, 0)
                        outer(s, i + (b0 + groups + 1), s % 2, i * 4 + (at["w_ready"] + s + 1), first and s == 0)

                four(0, True)
                with pe.Fori(1, groups) as i:
                    four(i, False)
                b1 = b0 + 2 * groups
                hidden(0, b1 + 1, 6, None)

                def step(i, s, piece, last=False, gates=None):
                    j = i * 2 + s
                    if not last:
                        hidden(1 + 2 * s, i + (b1 + 1), 6, j + (at["gelu"] + SPILL + 1))
                    if piece:
                        build(j + 3 * QUARTER, 7, 0)
                    if gates is not None:
                        if gates == 0:
                            pe.wait_ge(sem("g_ready"), at["g_ready"] + 4 * QUARTER)
                        else:
                            pe.wait_ge(sem("gt_evicted"), since("gt_evicted", 2 * l + 1) + gates)
                        gate(2 * l + 1, gates // 2, gates % 2, 7)
                    if last:
                        outer(3, i + (b1 + 1), s, j + (at["w_ready"] + SPILL + 1), last=True)
                    else:
                        outer((2 + 2 * s) % 4, i + (b1 + 1 + s), s, j + (at["w_ready"] + SPILL + 1))

                with pe.Fori(0, ROUNDS // 2) as i:
                    for s in range(2):
                        step(i, s, True)
                with pe.Fori(ROUNDS // 2, ROUNDS - 2) as i:
                    for s in range(2):
                        step(i, s, False)
                for i in (ROUNDS - 2, ROUNDS - 1):
                    for s in range(2):
                        step(i, s, False, i == ROUNDS - 1 and s == 1, 2 * (i - ROUNDS + 2) + s)

            pe.wait_ge(sem("const_in"), 16)
            pe.wait_ge(sem("mod_rows"), MODS * P // 512)
            for l in range(LAYERS):
                n = 2 * l
                turn("h_turned", lambda t, c: Xv[:, t, c:c + P], lambda t: pe.wait_ge(sem("x_in"), 16) if l == 0 else
                     pe.wait_ge(sem(f"x_ready{n}"), t + 1))
                if l == 0:
                    pe.wait_ge(sem("mod_back"), 16)
                    for c in range(2):
                        ins = pe.transpose(ps[:, 7, MODS * c:MODS * c + MODS], MODC[:, P * c:P * c + P],
                                           ident[0:MODS, 0:MODS])
                    ins.then_inc(sem("mod_turned"), 1)
                wait_h(n)
                project(("in", l), IN_W[l])
                pe.wait_ge(sem(f"prep{l}"), 1)
                pe.wait_ge(sem(f"cache{l}"), 64)
                if l == 0:
                    latent()
                    pe.wait_ge(sem("up_ready"), 14)
                attention(l, 0)
                if l == 0:
                    pe.wait_ge(sem("q_roped"), 2)
                attention(l, 1)
                pe.wait_ge(sem("o_ready"), since("o_ready", 2 * l + 1) + 24)
                turn("o_turned", lambda t, c: out_rows(l, t, c, P), lambda t: pe.wait_ge(sem("sub_normed"), t + 1) if l == 0 else None)
                for q in range(2):
                    gate(n, 0, q, 6 + q)

                def second_gate():
                    for q in range(2):
                        pe.wait_ge(sem("gt_evicted"), since("gt_evicted", n) + q + 1)
                        gate(n, 1, q, 6 + q)

                pe.wait_ge(sem("oT_ready"), since("oT_ready", l) + 6)
                project(("out", l), D, second_gate)
                turn("h_turned", lambda t, c: Xv[:, t, c:c + P], lambda t: pe.wait_ge(sem(f"x_ready{n + 1}"), t + 1))
                wait_h(n + 1)
                retrieve(l)
                experts(l)

        @block.scalar
        def _(act):
            fn = act.activation

            act.wait_ge(sem("small_in"), 64)
            fn(cs[:, :], cT[:, :], ACT.Exp, scale=-1.0).then_inc(sem("silu_exp"), 1)
            act.wait_ge(sem("lam_dots"), 1)
            fn(lam[:, 2:4], lam[:, 0:2], ACT.Exp).then_inc(sem("lam_exp"), 1)
            with act.Fori(0, MOD_USES // 2) as i:
                for g in range(2):
                    act.wait_ge(mod_used(3), i * 2 + (g + 1))
                    fn(ar(0, MOD_N)[0:2, bass.ds(i * 1024 + 512 * g, 512)], ps[0:2, g, :], ACT.Copy
                       ).then_inc(sem("mod_rows"), 1)

            def high(pos, turn):
                act.wait_ge(loaded(pos), turn * 16 + 16 * MOD_USES)
                fn(slot_hi[pos], slot[pos], ACT.Copy).then_inc(hi_done(pos), 1)

            def done(c):
                act.wait_ge(used(c % RING), turn_of(c))
                if c + RING < total:
                    high(c % RING, turn_of(c + RING))

            for s in range(RING):
                high(s, 1)

            def features(n):
                l, w = n // 2, n % 2
                act.wait_ge(sem("mod_ready"), 1)
                if n:
                    act.wait_ge(sem(f"state{(n - 1) // 2}"), 64)
                for t in range(NT):
                    r = slice(P * t, P * t + P)
                    act.wait_ge(sem("h_turned"), since("h_turned", n) + 2 * t + 2)
                    for k in range(4):
                        ins = fn(HF[:, 4 + k, r], ps[:, 2 * t + 1, P * k:P * k + P], ACT.Identity,
                                 scale=modv[:, l, 3 * w + 1, 4 + k, COND[t]:COND[t] + 1],
                                 bias=modv[:, l, 3 * w, 4 + k, COND[t]:COND[t] + 1])
                    ins.then_inc(sem("h_act"), 1)
                    act.wait_ge(sem("h_act"), since("h_act", n) + t + 1)
                    fn(xh[:, 4:8, r], HF[:, 4:8, r], ACT.Copy).then_inc(sem("xhi_act"), 1)

            def gate_row(n, m, bank):
                act.wait_ge(sem("gt_ps"), since("gt_ps", n) + m + 1)
                fn(gate_room(n)[:, m // 2, 512 * (m % 2):512 * (m % 2) + 512], ps[:, bank, :], ACT.Copy
                   ).then_inc(sem("gt_evicted"), 1)

            def attention(l, g):
                d, nk, kmap, scale = group(l, g)
                for n in range(1, 8 + nk, 2):
                    act.wait_ge(sem("qk_ps"), since("qk_ps", 2 * l + g) + n + 1)
                    if n < 8:
                        fn(QT[0:d, n, :], ps[0:d, 6 + n % 2, 0:TOK], ACT.Copy).then_inc(sem("qkT_act"), 1)
                    else:
                        fn(KT[0:d, n - 8, :], ps[0:d, 6 + n % 2, :], ACT.Copy).then_inc(sem("qkT_act"), 1)
                N = len(JOBS)
                biased = l == 1 and g == 1
                for i in range(N + 1):
                    if i < N:
                        j, t = JOBS[i]
                        kn = P if t == 0 else TOK
                        act.wait_ge(sem("mx"), since("mx", 2 * l + g) + i + 1)
                        if i >= 2:
                            act.wait_ge(sem("pT_ps"), since("pT_ps", 2 * l + g) + i - 1)
                        in_sb = biased and t > 0
                        src = SC[:, i % 2, 0:kn] if in_sb else ps[:, i % 2, 0:kn]
                        fn(PB[:, i % 2, 0:kn], src, ACT.Exp, bias=nms[:, i:i + 1], scale=1.0 if in_sb else scale,
                           accum_out=rs[:, i:i + 1]).then_inc(sem("p_ready"), 1)
                    if i >= 1:
                        m = i - 1
                        j, t = JOBS[m]
                        kn = P if t == 0 else TOK
                        act.wait_ge(sem("pT_ps"), since("pT_ps", 2 * l + g) + m + 1)
                        if m >= 2:
                            act.wait_ge(sem("o_ps"), since("o_ps", 2 * l + g) + m - 1)
                        fn(PT[:, m % 2, 0:kn], ps[:, 2 + m % 2, 0:kn], ACT.Copy).then_inc(sem("pT_ready"), 1)

            def root(dst, src, scale, wait, done, pieces=1):
                act.wait_ge(sem(wait), pieces)
                fn(dst, src, ACT.Sqrt, scale=scale, bias=epsc).then_inc(sem(done), 1)

            def queries(l):
                for c in range(17):
                    if c < 16:
                        g = start["q", l] + c
                        act.wait_ge(used(g % RING), turn_of(g))
                        if c >= 2:
                            act.wait_ge(sem("s_ps"), since("s_ps", l) + c - 1)
                        fn(ar(Q_QS, 2 * TOK)[:, TOK * (c % 2):TOK * (c % 2) + TOK], ps[:, 6 + c % 2, 0:TOK],
                           ACT.Copy).then_inc(sem("qs_ready"), 1)
                        done(g)
                    if c >= 1 and c % 4 == 0:
                        cg = c // 4 - 1
                        act.wait_ge(sem("s_ps"), since("s_ps", l) + 4 * cg + 4)
                        for t in range(NT):
                            o = Q_S + t * 2048 + 512 * cg
                            fn(ar(o, 512), ps[:, t + 3 * (cg % 2), :], ACT.Copy
                               ).then_inc(sem("s_ready"), 1)

            def experts(l):
                b0 = start["uv", l] // RING
                groups = SPILL // 4
                b1 = b0 + 2 * groups
                at = {name: since(name, l) for name in ("gelu", "w_ready", "g_ps", "g_ready")}

                def gelu(pos, turn, bank, s):
                    act.wait_ge(used(pos), turn)
                    fn(GL[:, s, :], ps[:, bank, 0:TOK], ACT.Gelu).then_inc(sem("gelu"), 1)

                def part(p, bank, half, col):
                    act.wait_ge(sem("g_ps"), p + (at["g_ps"] + 1))
                    gv = ar(G_N * half, G_N).rearrange("p (e t) -> p e t", e=QUARTER)
                    fn(gv[:, :, bass.ds(col, PIECE)],
                       ps[:, bank, 0:PIECE * QUARTER].rearrange("p (t e) -> p e t", t=PIECE), ACT.Copy
                       ).then_inc(sem("g_ready"), 1)

                def early(i, s, piece=False, first=False):
                    if not first:
                        act.wait_ge(sem(f"gl_stored{s % 2}"), i * 32 + (16 * (s // 2) + 8 * SPILL * l))
                    gelu(s, i + (b0 + 1), 6 + s % 2, s % 2)
                    high(s, i + (b0 + 2))
                    if piece:
                        part(i * 4 + (s - QUARTER), s % 2, 0, i * (4 * PIECE) + PIECE * (s - QUARTER))

                for s in range(4):
                    early(0, s, first=s < 2)
                with act.Fori(1, groups // 2 - 1) as i:
                    for s in range(4):
                        early(i, s)
                act.wait_ge(sem("tv_ready"), since("tv_ready", l) + 1)
                fn(ar(Q_TV, 384), ar(Q_TV, 384), ACT.Exp).then_inc(sem("tv_exp"), 1)
                for s in range(4):
                    early(groups // 2 - 1, s)
                for q in range(3):
                    act.wait_ge(sem("pick_ps"), since("pick_ps", l) + q + 1)
                    dst = IT16[:, q, :] if q < 2 else ar(Q_W32, TOK)
                    fn(dst, ps[:, 2 + q, 0:TOK], ACT.Copy, scale=1.0 if q < 2 else G_SCALE
                       ).then_inc(sem("it_ready"), 1)
                act.wait_ge(sem("weights_split"), l + 1)
                with act.Fori(groups // 2, groups) as i:
                    for s in range(4):
                        early(i, s, True)
                for quarter in range(2):
                    if quarter:
                        act.wait_ge(sem("w_ready"), at["w_ready"] + QUARTER)
                    with act.Fori(quarter * groups // 2, (quarter + 1) * groups // 2) as i:
                        for s in range(4):
                            part(i * 4 + (QUARTER + s), 7, 1 - quarter,
                                 i * (4 * PIECE) + PIECE * (s - QUARTER * quarter))
                            act.wait_ge(used(s), i + (b0 + groups + 1))
                            high(s, i + (b0 + groups + 2))
                act.wait_ge(sem("w_ready"), at["w_ready"] + SPILL - 1)
                gelu(0, b1 + 1, 6, 0)
                high(0, b1 + 2)

                def step(i, s, piece, last=False, gates=None):
                    j = i * 2 + s
                    more = not (l == LAYERS - 1 and gates is not None)
                    if not last:
                        act.wait_ge(sem("w_ready"), j + (at["w_ready"] + SPILL))
                        gelu(1 + 2 * s, i + (b1 + 1), 6, (s + 1) % 2)
                        if more or gates < 2:
                            high(1 + 2 * s, i + (b1 + 2))
                    if piece:
                        part(j + 3 * QUARTER, 7, 1, i * (2 * PIECE) + PIECE * s)
                    if gates is not None:
                        gate_row(2 * l + 1, gates, 7)
                    pos = 3 if last else (2 + 2 * s) % 4
                    act.wait_ge(used(pos), i + (b1 + 1 + (0 if last else s)))
                    if more or gates < 1:
                        high(pos, i + (b1 + 2 + (0 if last else s)))

                act.wait_ge(sem("w_ready"), at["w_ready"] + 2 * QUARTER)
                with act.Fori(0, ROUNDS // 2) as i:
                    for s in range(2):
                        step(i, s, True)
                with act.Fori(ROUNDS // 2, ROUNDS - 2) as i:
                    for s in range(2):
                        step(i, s, False)
                for i in (ROUNDS - 2, ROUNDS - 1):
                    for s in range(2):
                        step(i, s, False, i == ROUNDS - 1 and s == 1, 2 * (i - ROUNDS + 2) + s)

            epsc = lam[:, 5:6]
            for l in range(LAYERS):
                n = 2 * l
                features(n)
                for g in range((IN_W[l] + 511) // 512):
                    w = min(512, IN_W[l] - 512 * g)
                    for q in range(4):
                        done(start["in", l] + 4 * g + q)
                    for t in range(NT):
                        fn(PR[:, t, 512 * g:512 * g + w], ps[:, t + 3 * (g % 2), 0:w], ACT.Copy
                           ).then_inc(sem("pr_evicted"), 1)
                if l == 0:
                    root(ss2[:, 0:3], ss[:, 0:3], 1 / 256, "cq_ss", "cq_root")
                    root(ss2[:, 3:6], ss[:, 3:6], 1 / 128, "ckv_ss", "ckv_root")
                    for k in range(2):
                        act.wait_ge(sem("c_ps"), k + 1)
                        fn(cqT[:, TOK * k:TOK * k + TOK], ps[:, k, 0:TOK], ACT.Copy).then_inc(sem("cT_ready"), 1)
                    act.wait_ge(sem("c_ps"), 3)
                    fn(ckvT[:, :], ps[:, 2, :], ACT.Copy).then_inc(sem("cT_ready"), 1)
                    m = 0
                    for t in range(NT):
                        for q in range(2):
                            act.wait_ge(sem("up_ps"), m + 1)
                            w = 512 - 256 * q
                            fn(QR[:, t, 512 * q:512 * q + w], ps[:, 4 + m % 4, 0:w], ACT.Copy
                               ).then_inc(sem("up_ready"), 1)
                            m += 1
                    for b in range(4):
                        for q in range(2):
                            act.wait_ge(sem("up_ps"), m + 1)
                            kv = ps[:, 4 + m % 4, :].rearrange("p (h j n) -> p h j n", h=4, j=2)
                            fn(KR[:, b, 4 * q:4 * q + 4, 0:64], kv[:, :, 0, :], ACT.Copy)
                            fn(VR[:, b, 256 * q:256 * q + 256].rearrange("p (h n) -> p h n", h=4), kv[:, :, 1, :],
                               ACT.Copy).then_inc(sem("up_ready"), 1)
                            m += 1
                else:
                    root(ss2[:, 0:30], ss[:, 0:30], 1 / 64, "c_ss", "c_root")
                attention(l, 0)
                attention(l, 1)
                if l == 0:
                    root(ss2[:, 0:12], ss[:, 0:12], 1 / 128, "sub_ss", "sub_root", NT)
                for b in range(6):
                    act.wait_ge(sem("o_turned"), since("o_turned", l) + b + 1)
                    t, q = b // 2, b % 2
                    fn(xh[:, 4 * q:4 * q + 4, P * t:P * t + P], ps[:, b, :].rearrange("p (k n) -> p k n", k=4),
                       ACT.Copy).then_inc(sem("oT_hi"), 1)
                for m in range(2):
                    gate_row(n, m, 6 + m)
                for c in range(8):
                    done(start["out", l] + c)
                    if c == 3:
                        for m in range(2):
                            gate_row(n, 2 + m, 6 + m)
                for w in range(2):
                    m = n + w
                    if w:
                        features(m)
                        queries(l)
                        experts(l)
                    for t in range(NT):
                        act.wait_ge(sem("var"), since("var", m) + t + 1)
                        fn(rstd[:, t:t + 1], mv[:, 2 * t + 1:2 * t + 2], ACT.Sqrt, bias=epsc
                           ).then_inc(sem("std"), 1)

        @block.vector
        def _(dve):
            linked = [0]

            def link(ins):
                linked[0] += 1
                ins.then_inc(sem("dve_link"), 1)
                dve.wait_ge(sem("dve_link"), linked[0])

            tt, ts, stt = dve.tensor_tensor, dve.tensor_scalar, dve.scalar_tensor_tensor

            dve.memset(lam[:, 5:6], EPS).then_inc(sem("eps_set"), 1)
            dve.wait_ge(sem("silu_exp"), 1)
            link(ts(cs[:, :], cs[:, :], 1.0, None, ALU.add))
            link(dve.reciprocal(cs[:, :], cs[:, :]))
            tt(cs[:, :], cs[:, :], cT[:, :], ALU.mult).then_inc(sem("silu_ready"), 1)
            for j in range(2):
                link(tt(ar(A_TMP + 64 * j, 64), lq(2 * j), lq(2 * j + 1), ALU.mult))
            dve.tensor_reduce(lam[:, 0:2], ar(A_TMP, 128).rearrange("p (j n) -> p j n", j=2), AX.X, ALU.add
                              ).then_inc(sem("lam_dots"), 1)
            dve.wait_ge(sem("lam_exp"), 1)
            link(tt(lam[:, 4:5], lam[:, 3:4], lam[:, 2:3], ALU.subtract))
            link(ts(lam[:, 4:5], lam[:, 4:5], -LAM_INIT, None, ALU.add))
            link(ts(rows[:, R_SUB:R_SUB + 128], rows[:, R_SUB:R_SUB + 128], 1.0 - LAM_INIT, None, ALU.mult))
            dve.wait_ge(sem("mod_turned"), 1)
            link(tt(mod[:, :].rearrange("p (c m) -> p c m", c=2),
                    ps[:, 7, 0:2 * MODS].rearrange("p (c m) -> p c m", c=2),
                    bmod[:, :].unsqueeze(1).to_broadcast([P, 2, MODS]), ALU.add))
            mf = mod[:, :].rearrange("p (a j k) -> p a j k", a=2 * LAYERS, j=6)
            ts(mf[:, :, 1:5:3, :], mf[:, :, 1:5:3, :], 1.0, None, ALU.add).then_inc(sem("mod_ready"), 1)
            dve.wait_ge(sem("mod_ready"), 1)
            dve.wait_ge(sem("const_in"), 16)

            def features(n):
                l, w = n // 2, n % 2
                if n:
                    dve.wait_ge(sem(f"state{(n - 1) // 2}"), 64)
                for t in range(NT):
                    r = slice(P * t, P * t + P)
                    dve.wait_ge(sem("h_turned"), since("h_turned", n) + 2 * t + 1)
                    for k in range(4):
                        ins = ts(HF[:, k, r], ps[:, 2 * t, P * k:P * k + P],
                                 modv[:, l, 3 * w + 1, k, COND[t]:COND[t] + 1],
                                 modv[:, l, 3 * w, k, COND[t]:COND[t] + 1], ALU.mult, ALU.add)
                    link(ins)
                    link(dve.tensor_copy(xh[:, 0:4, r], HF[:, 0:4, r]))
                    tt(xl[:, 0:4, r], HF[:, 0:4, r], f32(xh[:, 0:4, r]), ALU.subtract).then_inc(sem("xlo_dve"), 1)

            def diagonals(n):
                l, w = n // 2, n % 2
                for c in range(2):
                    tt(diag_room(n, c).rearrange("p (k n) -> p k n", k=KC),
                       ident.unsqueeze(1).to_broadcast([P, KC, P]),
                       modv[:, l, 3 * w + 2, :, c:c + 1].to_broadcast([P, KC, P]), ALU.mult
                       ).then_inc(sem("diag"), 1)

            def out_columns(l):
                for b in range(6):
                    dve.wait_ge(sem("oT_hi"), since("oT_hi", l) + b + 1)
                    t, q = b // 2, b % 2
                    r = slice(P * t, P * t + P)
                    tt(xl[:, 4 * q:4 * q + 4, r], ps[:, b, :].rearrange("p (k n) -> p k n", k=4),
                       f32(xh[:, 4 * q:4 * q + 4, r]), ALU.subtract).then_inc(sem("oT_ready"), 1)

            def norm(n):
                dve.wait_ge(sem("gt_evicted"), since("gt_evicted", n) + 4)
                dve.wait_ge(sem("ln_in"), 16 * (n + 1))
                gtv = gate_room(n)
                tmp = work_room(n)
                lnv = norm_room(n).rearrange("p (j d) -> p j d", j=2)
                for t in range(NT):
                    for q in range(2):
                        if n % 2 == 0:
                            c = start["out", n // 2] + 4 * q + 3
                            dve.wait_ge(used(c % RING), turn_of(c))
                        else:
                            dve.wait_ge(used(3), turn_of(start["uv", n // 2] + 2 * KEYS - 1))
                        ins = tt(tmp[:, 512 * q:512 * q + 512], ps[:, t + 3 * q, :],
                                 gtv[:, COND[t], 512 * q:512 * q + 512], ALU.mult)
                    link(ins)
                    link(stt(Xv[:, t, :], Xv[:, t, :], ALPHA, tmp, ALU.mult, ALU.add))
                    for q in range(2):
                        ins = dve.bn_stats(stat[:, 12 * t + 6 * q:12 * t + 6 * q + 6], Xv[:, t, 512 * q:512 * q + 512])
                    link(ins)
                    dve.bn_aggr(mv[:, 2 * t:2 * t + 2], stat[:, 12 * t:12 * t + 12]).then_inc(sem("var"), 1)
                for t in range(NT):
                    dve.wait_ge(sem("std"), since("std", n) + t + 1)
                    link(dve.reciprocal(rstd[:, t:t + 1], rstd[:, t:t + 1]))
                    link(ts(Xv[:, t, :], Xv[:, t, :], mv[:, 2 * t:2 * t + 1], rstd[:, t:t + 1],
                            ALU.subtract, ALU.mult))
                    link(tt(Xv[:, t, :], Xv[:, t, :], lnv[:, 0, :], ALU.mult))
                    tt(Xv[:, t, :], Xv[:, t, :], lnv[:, 1, :], ALU.add).then_inc(sem(f"x_ready{n + 1}"), 1)

            TMP = ar(A_TMP, 2048)

            def rope(x, heads, half, cosv, sinv, done=None):
                tmp = TMP[:, 0:heads * 2 * half].rearrange("p (h n) -> p h n", h=heads)

                def over(v):
                    return v.unsqueeze(1).to_broadcast([P, heads, v.shape[-1]])
                tt(tmp[:, :, 0:half], x[:, :, half:2 * half], over(sinv[:, 0:half]), ALU.mult)
                link(tt(tmp[:, :, half:2 * half], x[:, :, 0:half], over(sinv[:, half:2 * half]), ALU.mult))
                link(tt(x, x, over(cosv), ALU.mult))
                ins = tt(x, x, tmp, ALU.add)
                if done:
                    ins.then_inc(sem(done), 1)
                else:
                    link(ins)

            def table(c, t, w):
                return TAB[:, c + w * (t - 1):c + w * t]

            def prep0():
                dve.wait_ge(sem("pr_evicted"), since("pr_evicted", 0) + 12)
                dve.wait_ge(sem("table_in"), 16)
                for at, w, off, r, name in ((1536, 256, 0, R_CQ, "cq"), (1792, 128, 3, R_CKV, "ckv")):
                    x = PR[:, :, at:at + w]
                    tmp = TMP[:, 0:3 * w].rearrange("p (t n) -> p t n", t=NT)
                    link(tt(tmp, x, x, ALU.mult))
                    dve.tensor_reduce(ss[:, off:off + 3], tmp, AX.X, ALU.add).then_inc(sem(f"{name}_ss"), 1)
                    dve.wait_ge(sem(f"{name}_ss"), 1)
                for at, w, off, r, name in ((1536, 256, 0, R_CQ, "cq"), (1792, 128, 3, R_CKV, "ckv")):
                    x = PR[:, :, at:at + w]
                    dve.wait_ge(sem(f"{name}_root"), 1)
                    link(dve.reciprocal(ss2[:, off:off + 3], ss2[:, off:off + 3]))
                    link(tt(x, x, ss2[:, off:off + 3].unsqueeze(2).to_broadcast([P, NT, w]), ALU.mult))
                    tt(x, x, rows[:, r:r + w].unsqueeze(1).to_broadcast([P, NT, w]), ALU.mult
                       ).then_inc(sem("ckv_ready" if name == "ckv" else "cq_ready"), 1)
                for t in (1, 2):
                    rope(PR[:, t, 0:1024].rearrange("p (h n) -> p h n", h=16), 16, 32,
                         table(T_COSA, t, 64), table(T_SINA, t, 64))
                    rope(PR[:, t, 1920:1952].rearrange("p (h n) -> p h n", h=1), 1, 16,
                         table(T_COSB, t, 32), table(T_SINB, t, 32))
                dve.wait_ge(sem("cache0"), 64)
                for b in range(4):
                    src = PR[:, b, 1920:1952] if b < 3 else CB[:, 128:160]
                    ins = dve.tensor_copy(KR[:, b, :, 64:96], src.unsqueeze(1).to_broadcast([P, 8, 32]))
                ins.then_inc(sem("prep0"), 1)

            def prep1():
                dve.wait_ge(sem("pr_evicted"), since("pr_evicted", 1) + 15)
                dve.wait_ge(sem("table_in"), 32)
                x = PR[:, :, 0:640].rearrange("p t (h n) -> p t h n", h=10)
                tmp = TMP[:, 0:1920].rearrange("p (t h n) -> p t h n", t=NT, h=10)
                sv = ss[:, 0:30].rearrange("p (t h) -> p t h", t=NT)
                link(tt(tmp, x, x, ALU.mult))
                dve.tensor_reduce(sv, tmp, AX.X, ALU.add).then_inc(sem("c_ss"), 1)
                dve.wait_ge(sem("c_root"), 1)
                link(dve.reciprocal(ss2[:, 0:30], ss2[:, 0:30]))
                s2 = ss2[:, 0:30].rearrange("p (t h) -> p t h", t=NT)
                link(tt(x, x, s2.unsqueeze(3).to_broadcast([P, NT, 10, 64]), ALU.mult))
                for t in range(NT):
                    tt(x[:, t, 0:8, :], x[:, t, 0:8, :],
                       rows[:, R_QN:R_QN + 64].unsqueeze(1).to_broadcast([P, 8, 64]), ALU.mult)
                    link(tt(x[:, t, 8:10, :], x[:, t, 8:10, :],
                            rows[:, R_KN:R_KN + 64].unsqueeze(1).to_broadcast([P, 2, 64]), ALU.mult))
                for t in (1, 2):
                    rope(PR[:, t, 0:640].rearrange("p (h n) -> p h n", h=10), 10, 32,
                         table(T_COSA, t, 64), table(T_SINA, t, 64))
                dve.wait_ge(sem("bias_in"), 16 * 32)
                bv = ar(A_BIAS, 4096).rearrange("p (n c) -> p n c", c=64)
                tt(bv, bv, TAB[:, T_MASK:T_MASK + 64].unsqueeze(1).to_broadcast([P, 64, 64]), ALU.add
                   ).then_inc(sem("prep1"), 1)

            def attention(l, g):
                d, nk, kmap, scale = group(l, g)
                if l == 0 and g == 1:
                    dve.wait_ge(sem("up_ready"), 6)
                    for t in (1, 2):
                        if t == 2:
                            dve.wait_ge(sem("q_roped"), 1)
                        rope(QR[:, t, :].rearrange("p (h n) -> p h n", h=8)[:, :, 64:96], 8, 16,
                             table(T_COSB, t, 32), table(T_SINB, t, 32), "q_roped")
                for n in range(0, 8 + nk, 2):
                    dve.wait_ge(sem("qk_ps"), since("qk_ps", 2 * l + g) + n + 1)
                    if n < 8:
                        dve.tensor_copy(QT[0:d, n, :], ps[0:d, 6, 0:TOK]).then_inc(sem("qkT_dve"), 1)
                    else:
                        dve.tensor_copy(KT[0:d, n - 8, :], ps[0:d, 6, :]).then_inc(sem("qkT_dve"), 1)
                N = len(JOBS)
                biased = l == 1 and g == 1
                for i in range(N + 2):
                    if i < N:
                        j, t = JOBS[i]
                        kn = P if t == 0 else TOK
                        dve.wait_ge(sem("sc_ps"), since("sc_ps", 2 * l + g) + i + 1)
                        if biased and t > 0:
                            if i >= 2:
                                dve.wait_ge(sem("p_ready"), since("p_ready", 2 * l + g) + i - 1)
                            stt(SC[:, i % 2, 0:256], ps[:, i % 2, 0:256], scale, BIAS[:, t - 1, j, :],
                                ALU.mult, ALU.add)
                            link(ts(SC[:, i % 2, 256:384], ps[:, i % 2, 256:384], scale, None, ALU.mult))
                            link(dve.tensor_reduce(nm[:, i:i + 1], SC[:, i % 2, :], AX.X, ALU.max))
                            ts(nms[:, i:i + 1], nm[:, i:i + 1], -1.0, None, ALU.mult).then_inc(sem("mx"), 1)
                        else:
                            link(dve.tensor_reduce(nm[:, i:i + 1], ps[:, i % 2, 0:kn], AX.X, ALU.max))
                            ts(nms[:, i:i + 1], nm[:, i:i + 1], -scale, None, ALU.mult).then_inc(sem("mx"), 1)
                    if i >= 2:
                        m = i - 2
                        j, t = JOBS[m]
                        c0, dv = out_cols(l, g, j)
                        dve.wait_ge(sem("o_ps"), since("o_ps", 2 * l + g) + m + 1)
                        link(dve.reciprocal(rr[:, m:m + 1], rs[:, m:m + 1]))
                        off = v_off(l, g, j)
                        dst, src = out_rows(l, t, c0, dv), ps[:, 4 + m % 2, off:off + dv]
                        if l == 0 and g == 0 and j % 2:
                            link(tt(rr[:, m:m + 1], rr[:, m:m + 1], lam[:, 4:5], ALU.mult))
                            stt(dst, src, rr[:, m:m + 1], dst, ALU.mult, ALU.add).then_inc(sem("o_ready"), 1)
                        else:
                            ts(dst, src, rr[:, m:m + 1], None, ALU.mult).then_inc(sem("o_ready"), 1)

            def sub_norm():
                dve.wait_ge(sem("o_ready"), since("o_ready", 0) + 24)
                for t in range(NT):
                    tmp = TMP[:, 0:512].rearrange("p (h n) -> p h n", h=4)
                    x = out_rows(0, t, 0, 512).rearrange("p (h n) -> p h n", h=4)
                    link(tt(tmp, x, x, ALU.mult))
                    dve.tensor_reduce(ss[:, 4 * t:4 * t + 4], tmp, AX.X, ALU.add).then_inc(sem("sub_ss"), 1)
                    dve.wait_ge(sem("sub_ss"), t + 1)
                dve.wait_ge(sem("sub_root"), 1)
                link(dve.reciprocal(ss2[:, 0:12], ss2[:, 0:12]))
                for t in range(NT):
                    x = out_rows(0, t, 0, 512).rearrange("p (h n) -> p h n", h=4)
                    link(tt(x, x, ss2[:, 4 * t:4 * t + 4].unsqueeze(2).to_broadcast([P, 4, 128]), ALU.mult))
                    tt(x, x, rows[:, R_SUB:R_SUB + 128].unsqueeze(1).to_broadcast([P, 4, 128]), ALU.mult
                       ).then_inc(sem("sub_normed"), 1)

            def retrieve(l):
                S = ar(Q_S, NT * 2048).rearrange("p (t c n) -> p t c n", t=NT, c=16)
                V = ar(Q_V, NT * 256).rearrange("p (t c n) -> p t c n", t=NT, c=16)
                Iu = ar(Q_I, NT * 256).bitcast(U32).rearrange("p (t c n) -> p t c n", t=NT, c=16)
                dve.tensor_copy(IOT, iota.unsqueeze(2).to_broadcast([P, KEYS, PIECE]))

                def top16(pieces):
                    for s, v, x in pieces:
                        ins = dve.max(v[:, 0:8], s)
                    link(ins)
                    for s, v, x in pieces:
                        ins = dve.max_index(x[:, 0:8], v[:, 0:8], s)
                    link(ins)
                    for s, v, x in pieces:
                        ins = dve.match_replace(s, v[:, 0:8], s, NEG)
                    link(ins)
                    for s, v, x in pieces:
                        ins = dve.max(v[:, 8:16], s)
                    link(ins)
                    for s, v, x in pieces:
                        ins = dve.max_index(x[:, 8:16], v[:, 8:16], s)
                    link(ins)

                for cg in range(4):
                    dve.wait_ge(sem("s_ready"), since("s_ready", l) + NT * (cg + 1))
                    top16([(S[:, t, c, :], V[:, t, c, :], Iu[:, t, c, :]) for t in range(NT)
                           for c in range(4 * cg, 4 * cg + 4)])
                dve.tensor_copy(ar(Q_IF, NT * 256), ar(Q_I, NT * 256).bitcast(U32))
                Vh = ar(Q_V, NT * 256).rearrange("p (t h j n) -> p t h j n", t=NT, h=HEADS, j=2)
                for t in range(NT):
                    ins = tt(ar(Q_S + 2048 * t, 2048).rearrange("p (h a b) -> p h a b", h=HEADS, a=TOPK),
                             Vh[:, t, :, 0, :].unsqueeze(3).to_broadcast([P, HEADS, TOPK, TOPK]),
                             Vh[:, t, :, 1, :].unsqueeze(2).to_broadcast([P, HEADS, TOPK, TOPK]), ALU.add)
                link(ins)
                C = ar(Q_S, NT * 2048).rearrange("p (t h n) -> p t h n", t=NT, h=HEADS)
                TV = ar(Q_TV, NT * 128).rearrange("p (t h n) -> p t h n", t=NT, h=HEADS)
                TP = ar(Q_TP, NT * 128).bitcast(U32).rearrange("p (t h n) -> p t h n", t=NT, h=HEADS)
                top16([(C[:, t, h, :], TV[:, t, h, :], TP[:, t, h, :]) for t in range(NT) for h in range(HEADS)])
                Tf = ar(Q_TV, NT * 128).rearrange("p (m n) -> p m n", n=TOPK)
                dve.tensor_copy(ss[:, 0:24], Tf[:, :, 0]).then_inc(sem("dve_link"), 1)
                linked[0] += 1
                dve.wait_ge(sem("dve_link"), linked[0])
                tt(Tf, Tf, ss[:, 0:24].unsqueeze(2).to_broadcast([P, 24, TOPK]), ALU.subtract
                   ).then_inc(sem("tv_ready"), 1)
                pos = ar(Q_TP, 384).bitcast(U32)
                ts(ar(Q_AB, 384).bitcast(U32), pos, 4, None, ALU.logical_shift_right)
                link(ts(ar(Q_AB + 384, 384).bitcast(U32), pos, 15, None, ALU.bitwise_and))
                link(dve.tensor_copy(ar(Q_ABF, 768), ar(Q_AB, 768).bitcast(U32)))
                IFh = ar(Q_IF, NT * 256).rearrange("p (t h j n) -> p t h j n", t=NT, h=HEADS, j=2)
                eq = ar(Q_EQ, 2048)
                for j in range(2):
                    for t in range(NT):
                        link(tt(eq.rearrange("p (m n) -> p m n", n=TOPK),
                                ar(Q_ABF + 384 * j + 128 * t, 128).unsqueeze(2).to_broadcast([P, 128, TOPK]),
                                iota[:, 0:TOPK].unsqueeze(1).to_broadcast([P, 128, TOPK]), ALU.is_equal))
                        e4 = eq.rearrange("p (h k n) -> p h k n", h=HEADS, k=TOPK)
                        link(tt(e4, e4, IFh[:, t, :, j, :].unsqueeze(2).to_broadcast([P, HEADS, TOPK, TOPK]), ALU.mult))
                        link(dve.tensor_reduce(ar(Q_ID + 128 * (NT * j + t), 128),
                                               eq.rearrange("p (m n) -> p m n", n=TOPK), AX.X, ALU.add))
                dve.wait_ge(sem("tv_exp"), since("tv_exp", l) + 1)
                link(dve.tensor_reduce(ss[:, 0:24], Tf, AX.X, ALU.add))
                link(dve.reciprocal(ss2[:, 0:24], ss[:, 0:24]))
                tt(ar(Q_ID + 768, 384).rearrange("p (m n) -> p m n", n=TOPK), Tf,
                   ss2[:, 0:24].unsqueeze(2).to_broadcast([P, 24, TOPK]), ALU.mult).then_inc(sem("picked"), 1)

            def experts(l):
                b0 = start["uv", l] // RING
                groups = SPILL // 4
                b1 = b0 + 2 * groups
                at = {name: since(name, l) for name in ("gelu", "w_ready", "g_ps", "oh_ready", "e2_ready", "w_full", "w_hi")}
                dve.wait_ge(sem("it_ready"), since("it_ready", l) + 3)
                link(dve.tensor_copy(IT16[:, 2, :], ar(Q_W32, TOK)))
                tt(IT16[:, 3, :], ar(Q_W32, TOK), IT16[:, 2, :], ALU.subtract).then_inc(sem("weights_split"), 1)
                dve.wait_ge(sem("weights_split"), l + 1)

                def one_hots(p, quarter, col, first=False):
                    def it(q, n):
                        return IT16[:, q, bass.ds(col, PIECE)].unsqueeze(1).to_broadcast([P, n, PIECE])
                    oa = ar(Q_OA, OA_N).bitcast(F16).rearrange("p (e t) -> p e t", e=KEYS)
                    ob = ar(Q_OB, 2 * OB_N).bitcast(F16).rearrange("p (j e t) -> p j e t", j=2,
                                                                                      e=QUARTER)
                    e2 = ar(Q_E2, OB_N).bitcast(F16).rearrange("p (e t) -> p e t", e=QUARTER)
                    if not first:
                        dve.wait_ge(sem("oh_ready"), p + at["oh_ready"])
                    tt(e2, it(1, QUARTER), IOT[:, QUARTER * quarter:QUARTER * quarter + QUARTER, :], ALU.is_equal
                       ).then_inc(sem("e2_ready"), 1)
                    if not first:
                        dve.wait_ge(sem("g_ps"), p + at["g_ps"])
                    tt(oa, it(0, KEYS), IOT[:, :, :], ALU.is_equal)
                    dve.wait_ge(sem("e2_ready"), p + (at["e2_ready"] + 1))
                    tt(ob[:, 0], e2, it(2, QUARTER), ALU.mult)
                    tt(ob[:, 1], e2, it(3, QUARTER), ALU.mult).then_inc(sem("oh_ready"), 1)

                def product(e, s, odd, half, col, pos, turn):
                    w = GL[:, s, :]
                    stt(w, w, 1.0 / G_SCALE, ar(G_N * half, G_N)[:, bass.ds(col, TOK)], ALU.mult, ALU.mult
                        ).then_inc(sem("w_full"), 1)
                    dve.wait_ge(used(pos), turn)
                    dve.wait_ge(sem("w_full"), e + (at["w_full"] + 1))
                    hi, lo = w_hi[:, TOK * odd:TOK * odd + TOK], w_lo[:, TOK * odd:TOK * odd + TOK]
                    dve.tensor_copy(hi, w).then_inc(sem("w_hi"), 1)
                    dve.wait_ge(sem("w_hi"), e + (at["w_hi"] + 1))
                    tt(lo, w, f32(hi), ALU.subtract).then_inc(sem("w_ready"), 1)

                for s in range(4):
                    one_hots(s, 0, PIECE * s, s == 0)
                with dve.Fori(1, groups // 2) as i:
                    for s in range(4):
                        one_hots(i * 4 + s, 0, i * (4 * PIECE) + PIECE * s)
                dve.wait_ge(sem("g_ready"), since("g_ready", l) + QUARTER)
                for quarter in range(2):
                    if quarter:
                        dve.wait_ge(sem("g_ready"), since("g_ready", l) + 2 * QUARTER)
                    with dve.Fori(quarter * groups // 2, (quarter + 1) * groups // 2) as i:
                        for s in range(4):
                            one_hots(i * 4 + (QUARTER + s), quarter + 1,
                                     i * (4 * PIECE) + PIECE * (s - QUARTER * quarter))
                            dve.wait_ge(sem(f"gl_loaded{s % 2}"), i * 32 + (16 * (s // 2 + 1) + 8 * SPILL * l))
                            product(i * 4 + s, s % 2, s % 2, quarter,
                                    i * (4 * TOK) + TOK * (s - QUARTER * quarter),
                                    (s + 2) % 4, i + (b0 + groups + (s >= 2)))

                def step(i, s, quarter, col):
                    j = i * 2 + s
                    if quarter == 2:
                        one_hots(j + 3 * QUARTER, 3, i * (2 * PIECE) + PIECE * s)
                    dve.wait_ge(sem("gelu"), j + (at["gelu"] + SPILL + 1))
                    product(j + SPILL, s, s, quarter % 2, col, 2 - 2 * s, i + (b1 + s))

                for quarter in (2, 3):
                    dve.wait_ge(sem("g_ready"), since("g_ready", l) + (quarter + 1) * QUARTER)
                    if quarter == 3:
                        diagonals(2 * l + 1)
                    with dve.Fori((quarter - 2) * ROUNDS // 2, (quarter - 1) * ROUNDS // 2) as i:
                        for s in range(2):
                            step(i, s, quarter, i * (2 * TOK) + TOK * (s - QUARTER * (quarter - 2)))

            for l in range(LAYERS):
                n = 2 * l
                features(n)
                (prep0 if l == 0 else prep1)()
                attention(l, 0)
                attention(l, 1)
                if l == 0:
                    sub_norm()
                diagonals(n)
                out_columns(l)
                norm(n)
                features(n + 1)
                retrieve(l)
                experts(l)
                norm(n + 1)


def kernel(**inputs):
    import numpy as np
    import concourse.bacc as _bacc
    from concourse import mybir as _mybir
    from concourse.bass_utils import run_bass_kernel_spmd as _run

    g = {k: np.asarray(v) for k, v in inputs.items()}
    f = np.float32

    def columns(w, n):
        w = w.reshape(8, 128, n // 128, 128)
        return np.ascontiguousarray(w.transpose(2, 1, 0, 3)).reshape(n // 128, 128, 1024)

    def wide(w):
        n = -(-w.shape[1] // 512) * 512
        w = np.pad(w, ((0, 0), (0, n - w.shape[1])))
        w = w.reshape(4, 2, 128, n // 512, 512)
        return np.ascontiguousarray(w.transpose(3, 0, 2, 1, 4)).reshape(n // 128, 128, 1024)

    const = np.zeros((128, C_N), f)
    const[:, C_ID:C_ID + 128] = np.eye(128)
    const[:, C_IOTA:C_IOTA + 128] = np.arange(128)
    const[:, C_ONES:C_ONES + 128] = 1
    table = np.zeros((128, T_N), f)
    tok = np.arange(256)
    for rot, c_cos, c_sin in ((64, T_COSA, T_SINA), (32, T_COSB, T_SINB)):
        nf = rot // 4
        inv = (f(10000.0) ** (-np.arange(nf, dtype=f) / f(nf))).astype(f)
        ang = np.concatenate([(tok // 64).astype(f)[:, None] * inv, (tok % 64).astype(f)[:, None] * inv], 1)
        cos, sin = np.cos(ang).astype(f), np.sin(ang).astype(f)
        for t in range(2):
            r = slice(128 * t, 128 * t + 128)
            table[:, c_cos + rot * t:c_cos + rot * t + rot] = np.concatenate([cos[r], cos[r]], 1)
            table[:, c_sin + rot * t:c_sin + rot * t + rot] = np.concatenate([-sin[r], sin[r]], 1)
    qc = np.arange(128) % 64
    c0 = np.clip(qc - 8, 0, 48)
    kc = np.arange(64)
    ok = (kc[None] >= c0[:, None]) & (kc[None] < c0[:, None] + 16)
    table[:, T_MASK:T_MASK + 64] = np.where(ok, 0, -1e30)

    arrays = {
        "x": np.concatenate([g["x_prompt"][0], g["x_sample"][0]]),
        "const": const,
        "cT": np.stack([g["c_ctx"], g["c"][0]]).reshape(2, 8, 128).transpose(2, 1, 0).reshape(128, 16),
        "b_mod": g["b_mod"].reshape(96, 128).T,
        "table": table,
        "lam": np.concatenate([g["ev_lam_q1"][0], g["ev_lam_k1"][0], g["ev_lam_q2"][0], g["ev_lam_k2"][0]]),
        "rows": np.concatenate([g["ev_g_sub"][0], g["ev_g_cq"][0], g["ev_g_ckv"][0], g["od_g_qn"][0],
                                g["od_g_kn"][0]]),
        "ln": np.stack([np.concatenate([g[f"ln{w}_g"][l], g[f"ln{w}_b"][l]]) for l in range(2) for w in (1, 2)]),
        "w_mod": np.concatenate([wide(g["w_mod"][l]) for l in range(2)]),
        "w_in0": wide(g["ev_w_in"][0]), "w_in1": wide(g["od_w_in"][0]),
        "w_out0": wide(g["ev_w_out"][0]), "w_out1": wide(g["od_w_out"][0]),
        "w_q": np.stack([columns(g["pk_w_q"][l], 2048) for l in range(2)]),
        "u": g["pk_u"].reshape(2, 128, 128, 8, 128).transpose(0, 2, 4, 3, 1).reshape(2, 128, 128, 1024),
        "v": g["pk_v"].reshape(2, 128, 128, 1024).transpose(0, 2, 1, 3),
        "keys": np.stack([g["pk_k1"].transpose(0, 2, 1), g["pk_k2"].transpose(0, 2, 1)], 2),
        "w_uq": g["ev_w_uq"][0], "w_ukv": g["ev_w_ukv"][0],
        "rpb": np.pad(g["od_rpb"][0], ((0, 0), (0, 0), (48, 48))).reshape(120, 127),
        "cache_a_k": g["cache_a_k"].reshape(128, 512), "cache_a_v": g["cache_a_v"].reshape(128, 512),
        "cache_b_ckv": g["cache_b_ckv"].reshape(128, 128), "cache_b_kr": g["cache_b_kr"].reshape(128, 32),
        "cache_c_k": g["cache_c_k"].reshape(128, 128), "cache_c_v": g["cache_c_v"].reshape(128, 128),
        "cache_d_k": g["cache_d_k"].reshape(128, 512), "cache_d_v": g["cache_d_v"].reshape(128, 512),
    }
    outs = {"y": (384, 1024), "state_a_k": (128, 512), "state_a_v": (128, 512), "state_b_ckv": (128, 128),
            "state_b_kr": (128, 32), "state_c_k": (128, 128), "state_c_v": (128, 128), "state_d_k": (128, 512),
            "state_d_v": (128, 512)}
    nc = _bacc.Bacc("TRN2", target_bir_lowering=False, num_devices=1)
    sent, args = {}, {}
    for k, v in arrays.items():
        v = np.ascontiguousarray(v)
        assert v.dtype == np.float32, k
        sent[f"in_{k}"] = v
        args[k] = nc.dram_tensor(f"in_{k}", v.shape, _mybir.dt.float32, kind="ExternalInput").ap()
    for k, shape in outs.items():
        args[k] = nc.dram_tensor(f"out_{k}", shape, _mybir.dt.float32, kind="ExternalOutput").ap()
    build(nc, args)
    r = _run(nc, [sent], core_ids=[0]).results[0]
    o = {k: r[f"out_{k}"] for k in outs}
    return (o["y"][:128].reshape(1, 128, 1024), o["y"][128:].reshape(1, 256, 1024),
            o["state_a_k"].reshape(1, 1, 128, 4, 2, 64), o["state_a_v"].reshape(1, 1, 128, 4, 128),
            o["state_b_ckv"].reshape(1, 1, 128, 128), o["state_b_kr"].reshape(1, 1, 128, 32),
            o["state_c_k"].reshape(1, 1, 128, 2, 64), o["state_c_v"].reshape(1, 1, 128, 2, 64),
            o["state_d_k"].reshape(1, 1, 128, 8, 64), o["state_d_v"].reshape(1, 1, 128, 8, 64))
```

```python
from contextlib import ExitStack

import concourse.bass as bass
from concourse import mybir

F32 = mybir.dt.float32
U32 = mybir.dt.uint32
F32R = mybir.dt.float32r
F16 = mybir.dt.float16
ALU = mybir.AluOpType
ACT = mybir.ActivationFunctionType
AX = mybir.AxisListType

P = 128
D = 1024
KC = D // P
NT = 3
TOK = NT * P
LAYERS = 2
EPS = 1e-6
ALPHA = (2 * LAYERS) ** 0.25
LAM_INIT = 0.2
NEG = -3.0e38
RING = 4
HEADS = 8
TOPK = 16
KEYS = 128
QUARTER = 32
PIECE = TOK // QUARTER
G_N = QUARTER * TOK
SPILL = 64
G_SCALE = 16384.0
IN_W = (1952, 2304)
MODS = LAYERS * 6 * KC
MOD_N = MODS * P
MOD_FIRST = 4
MOD_STAGES = {"mod_b": (4, 8), "mod_c": (12, 6), "mod_d": (18, 6)}
MOD_BATCHES = ((0, 16), (16, 56), (72, 24))

C_ID, C_IOTA, C_ONES, C_N = 0, 128, 256, 384
T_COSA, T_SINA = 0, 128
T_COSB, T_SINB = 256, 320
T_MASK, T_N = 384, 448
R_SUB, R_CQ, R_CKV, R_QN, R_KN, R_N = 0, 128, 384, 512, 576, 640

A_PR = 0
A_QR = A_PR + 3 * 2304
A_KR = A_QR + 3 * 768
A_VR = A_KR + 4 * 768
A_CA = A_VR + 4 * 512
A_CB = A_CA + 2 * 512
A_QT = A_CB + 256
A_KT = A_QT + 8 * TOK
A_P = A_KT + 8 * 512
A_PT = A_P + 2 * TOK
A_TMP = A_PT + 2 * TOK
A_TAB = A_TMP + 2048
A_MROW = A_TAB + T_N
A_MCOL = A_MROW + 512
A_N = A_MCOL + 512
A_BIAS, A_SC = A_QR, A_QR + 4096
Q_S = 0
Q_V = Q_S + NT * 16 * 128
Q_I = Q_V + NT * 16 * 16
Q_IF = Q_I + NT * 16 * 16
Q_TV = Q_IF + NT * 16 * 16
Q_TP = Q_TV + NT * 128
Q_AB = Q_TP + NT * 128
Q_ABF = Q_AB + 2 * NT * 128
Q_EQ = Q_ABF + 2 * NT * 128
Q_ID = Q_EQ + 2048
Q_QS = Q_ID + 3 * NT * 128
Q_W32 = Q_QS
Q_KEYS = Q_QS + 2 * TOK
assert A_CA <= Q_KEYS and Q_KEYS + 2 * KEYS <= A_QT
Q_GL = 2 * G_N
Q_OA = Q_GL + 2 * TOK
OA_N = KEYS * PIECE // 2
OB_N = QUARTER * PIECE // 2
Q_OB = Q_OA + OA_N
Q_E2 = Q_OB + 2 * OB_N
Q_IOT = Q_E2 + OB_N
Q_IT = Q_IOT + OA_N
ARENA = max(A_N, Q_IT + 2 * TOK)
A_GT, A_LN, A_DIAG, A_WORK = A_QT, A_KT, A_P, A_QT + 2 * D
Q_GT, Q_LN, Q_DIAG, Q_WORK = 3 * D, 5 * D, 7 * D, 8 * D

SIGNALS = {
    **dict.fromkeys(("h_turned",), [6, 6, 6, 6]),
    **dict.fromkeys(("diag",), [2, 2, 2, 2]),
    **dict.fromkeys(("gt_ps", "gt_evicted"), [4, 4, 4, 4]),
    **dict.fromkeys(("h_act", "xhi_act", "xlo_dve", "xlo_pool"), [3, 3, 3, 3]),
    **dict.fromkeys(("var", "std"), [3, 3, 3, 3]),
    **dict.fromkeys(("qk_ps",), [16, 16, 10, 16]),
    **dict.fromkeys(("qkT_dve", "qkT_act"), [8, 8, 5, 8]),
    **dict.fromkeys(("sc_ps", "p_ready", "pT_ready", "pT_ps", "o_ps", "o_ready", "mx"), [24, 24, 24, 24]),
    **dict.fromkeys(("rows_ps",), [2, 2, 2, 2]),
    **dict.fromkeys(("g_ps", "g_ready", "oh_ready", "e2_ready", "gelu", "w_full", "w_hi", "w_ready"), [128, 128]),
    **dict.fromkeys(("s_ps", "qs_ready"), [16, 16]),
    **dict.fromkeys(("s_ready",), [12, 12]),
    **dict.fromkeys(("pr_evicted",), [12, 15]),
    **dict.fromkeys(("o_turned", "oT_hi", "oT_ready"), [6, 6]),
    **dict.fromkeys(("it_ready", "pick_ps"), [3, 3]),
    **dict.fromkeys(("picked", "tv_ready", "tv_exp"), [1, 1]),
}


def since(name, n):
    return sum(SIGNALS[name][:n])


def build(nc, a):
    ctx = ExitStack()
    with ctx:
        sems = {}

        def sem(name):
            if name not in sems:
                sems[name] = ctx.enter_context(nc.semaphore(name))
            return sems[name]

        def sb(name, n):
            return ctx.enter_context(nc.sbuf_tensor(name, [P, n], F32))

        ring = sb("ring", RING * 1024)
        arena = sb("arena", ARENA)
        X = sb("x", 3 * D)

        def sbr(name, n):
            return ctx.enter_context(nc.sbuf_tensor(name, [P, n], F32R))

        ring_hi, ring_lo = sbr("ring_hi", RING * 1024), sbr("ring_lo", RING * 1024)
        x_hi, x_lo = sbr("x_hi", KC * TOK), sbr("x_lo", KC * TOK)
        cs_parts = sbr("silu_parts", KC * 4 + P)
        w_hi, w_lo = sbr("w_hi", 2 * TOK), sbr("w_lo", 2 * TOK)
        const = sb("const", C_N)
        rows = sb("rows", R_N)
        mod = sb("mod", MODS * 2)
        bmod = sb("bmod", MODS)
        cT = sb("cT", 16)
        cs = sb("cs", 16)
        stat = sb("stat", 3 * 12)
        mv = sb("mv", 6)
        rstd = sb("rstd", 3)
        nm = sb("nm", 24)
        nms = sb("nms", 24)
        rs = sb("rs", 24)
        rr = sb("rr", 24)
        lam = sb("lam", 6)
        ss = sb("ss", 32)
        ss2 = sb("ss2", 32)
        ps = ctx.enter_context(nc.psum_tensor("ps", [P, 8, 512], F32))

        def ar(off, n):
            return arena[:, off:off + n]

        uq_w, ukv_w, ckvT = ar(A_KT, 1536), ar(A_KT + 1536, 1024), ar(A_KT + 2560, 512)
        cqT = ar(A_P, 2 * TOK)
        ident = const[:, C_ID:C_ID + 128]
        iota = const[:, C_IOTA:C_IOTA + 128]
        ones = const[:, C_ONES:C_ONES + 128]
        Xv = X[:, :].rearrange("p (t d) -> p t d", t=NT)
        HF = ar(0, KC * TOK).rearrange("p (k t) -> p k t", k=KC)
        xh = x_hi[:, :].rearrange("p (k t) -> p k t", k=KC)
        xl = x_lo[:, :].rearrange("p (k t) -> p k t", k=KC)
        modv = mod[:, :].rearrange("p (c l j k) -> p l j k c", c=2, l=LAYERS, j=6)

        def gate_room(n):
            return ar(Q_GT if n % 2 else A_GT, 2 * D).rearrange("p (c d) -> p c d", c=2)

        def norm_room(n):
            return ar(Q_LN if n % 2 else A_LN, 2 * D)

        def diag_room(n, c):
            return work_room(n) if c == 0 else ar(Q_DIAG if n % 2 else A_DIAG, D)

        def work_room(n):
            return ar(Q_WORK if n % 2 else A_WORK, D)

        def f32(x):
            return x.bitcast(F32)

        slot = [ring[:, n * 1024:(n + 1) * 1024] for n in range(RING)]
        slot_hi = [ring_hi[:, n * 1024:(n + 1) * 1024] for n in range(RING)]
        slot_lo = [ring_lo[:, n * 1024:(n + 1) * 1024] for n in range(RING)]
        GL = ar(Q_GL, 2 * TOK).rearrange("p (s t) -> p s t", s=2)
        PR = ar(A_PR, 3 * 2304).rearrange("p (t n) -> p t n", t=NT)
        QR = ar(A_QR, 3 * 768).rearrange("p (t n) -> p t n", t=NT)
        KR = ar(A_KR, 4 * 768).rearrange("p (b h n) -> p b h n", b=4, h=8)
        VR = ar(A_VR, 4 * 512).rearrange("p (b n) -> p b n", b=4)
        CA = ar(A_CA, 1024).rearrange("p (j n) -> p j n", j=2)
        CB = ar(A_CB, 256)
        QT = ar(A_QT, 8 * TOK).rearrange("p (j t) -> p j t", j=8)
        KT = ar(A_KT, 8 * 512).rearrange("p (j t) -> p j t", j=8)
        PB = ar(A_P, 2 * TOK).rearrange("p (j t) -> p j t", j=2)
        PT = ar(A_PT, 2 * TOK).rearrange("p (j t) -> p j t", j=2)
        TAB = ar(A_TAB, T_N)

        def out_rows(l, t, c, n):
            if c < 512:
                return PR[:, t, c:c + n]
            return QR[:, t, c - 512:c - 512 + n] if l == 0 else PR[:, t, c + 256:c + 256 + n]

        BIAS = ar(A_BIAS, 4096).rearrange("p (t h n) -> p t h n", t=2, h=8)
        SC = ar(A_SC, 2 * TOK).rearrange("p (j t) -> p j t", j=2)
        IOT = ar(Q_IOT, OA_N).bitcast(F16).rearrange("p (e t) -> p e t", e=KEYS)
        IT16 = ar(Q_IT, 2 * TOK).bitcast(F16).rearrange("p (q t) -> p q t", q=4)
        MROW = ar(A_MROW, 512)
        ktab = ar(Q_KEYS, 2 * KEYS)
        lq = lambda j: ar(A_TMP + 256 + 64 * j, 64)

        start, size, total = {}, {}, 0
        for l in range(LAYERS):
            for stage, chunks in ((("in", l), 4 * -(-IN_W[l] // 512)),
                                  *((m, 4 * MOD_STAGES[m][1]) for m in (("mod_b", "mod_c"), ("mod_d",))[l]),
                                  (("out", l), 8), (("q", l), 16), (("uv", l), 2 * KEYS)):
                start[stage], size[stage] = total, chunks
                total += chunks

        def turn_of(c):
            return c // RING + 1

        def loaded(pos):
            return sem(f"slot_loaded{pos}")

        def mod_used(pos):
            return sem(f"mod_used{pos}")

        def hi_done(pos):
            return sem(f"slot_hi{pos}")

        def lo_done(pos):
            return sem(f"slot_lo{pos}")

        def used(pos):
            return sem(f"slot_used{pos}")

        ROUNDS = SPILL // 2

        COND = (0, 1, 1)

        def q_rows(l, g, t, j):
            if l == 0:
                return PR[:, t, 64 * j:64 * j + 64] if g == 0 else QR[:, t, 96 * j:96 * j + 96]
            return PR[:, t, 64 * j:64 * j + 64] if g == 0 else PR[:, t, 768 + 64 * j:832 + 64 * j]

        def k_rows(l, g, b, j):
            if l == 0:
                if g == 1:
                    return KR[:, b, j, :]
                return PR[:, b, 512 + 64 * j:576 + 64 * j] if b < 3 else CA[:, 0, 64 * j:64 * j + 64]
            if g == 0:
                return PR[:, b, 512 + 64 * j:576 + 64 * j] if b < 3 else CB[:, 64 * j:64 * j + 64]
            return PR[:, b, 1280 + 64 * j:1344 + 64 * j] if b < 3 else CA[:, 0, 64 * j:64 * j + 64]

        def v_rows(l, g, b, j):
            if l == 0:
                h = j // 2
                if g == 1:
                    return VR[:, b, 128 * h:128 * h + 128]
                return PR[:, b, 1024 + 128 * h:1152 + 128 * h] if b < 3 else CA[:, 1, 128 * h:128 * h + 128]
            if g == 0:
                return PR[:, b, 640:768] if b < 3 else CB[:, 128:256]
            h = j // 2
            return PR[:, b, 1792 + 128 * h:1920 + 128 * h] if b < 3 else CA[:, 1, 128 * h:128 * h + 128]

        def v_off(l, g, j):
            if l == 0 and g == 0:
                return 0
            return 64 * (j // 4) if l == 1 and g == 0 else 64 * (j % 2)

        def group(l, g):
            if l == 0 and g == 1:
                return 96, 8, (lambda j: j), 96 ** -0.5
            if l == 1 and g == 0:
                return 64, 2, (lambda j: j // 4), 64 ** -0.5
            return 64, 8, (lambda j: j), 64 ** -0.5

        JOBS = [(j, t) for j in range(8) for t in range(NT)]

        def blocks(t):
            return [0] if t == 0 else [1, 2, 3]

        def out_cols(l, g, j):
            if l == 0 and g == 0:
                return 128 * (j // 2), 128
            return 512 * g + 64 * j, 64

        gl_dram = nc.dram_tensor("gelu_half", (SPILL, P, TOK), F32, kind="Internal").ap()
        mod_dram = nc.dram_tensor("modulation", (4, MOD_N), F32, kind="Internal").ap()
        skew = nc.dram_tensor("skewed_bias", (120, 64, 127), F32, kind="Internal").ap()

        block = ctx.enter_context(nc.Block())

        @block.sync
        def _(sp):
            def load(pos, src, turn):
                sp.wait_ge(lo_done(pos), turn)
                sp.dma_start(slot[pos], src).then_inc(loaded(pos), 16)

            def stream(stage, src):
                for c in range(src.shape[0]):
                    g = start[stage] + c
                    if g < RING:
                        sp.wait_ge(mod_used(g), MOD_FIRST)
                        sp.dma_start(slot[g], src[c]).then_inc(loaded(g), 16)
                    else:
                        load(g % RING, src[c], g // RING)

            for g in range(MOD_FIRST):
                for s in range(RING):
                    if g:
                        sp.wait_ge(mod_used(s), g)
                    sp.dma_start(slot[s], a["w_mod"][g * RING + s]).then_inc(loaded(s), 16)
            for l in range(LAYERS):
                stream(("in", l), a[f"w_in{l}"])
                if l:
                    sp.wait_ge(sem("skew"), 16)
                    for r in range(4):
                        for h in range(8):
                            src = bass.AP(skew.tensor, (h * 15 + 7 - r) * 64 * 127 + 63,
                                          [[126, 64], [64 * 127, 4], [1, 64]])
                            p0 = 64 * (r % 2)
                            dst = BIAS[p0:p0 + 64, r // 2, h, :].rearrange("p (a c) -> p a c", a=4)
                            sp.dma_start(dst, src).then_inc(sem("bias_in"), 16)
                for stage in (("mod_b", "mod_c"), ("mod_d",))[l]:
                    first, groups = MOD_STAGES[stage]
                    stream(stage, a["w_mod"][RING * first:RING * (first + groups)])
                stream(("out", l), a[f"w_out{l}"])
                stream(("q", l), a["w_q"][l])
                u, v = a["u"][l], a["v"][l]
                b0 = start["uv", l] // RING
                groups = SPILL // 4

                def store(i, s):
                    sp.wait_ge(sem("gelu"), i * 4 + (since("gelu", l) + s + 1))
                    sp.dma_start(gl_dram[i * 4 + s], GL[:, s % 2, :]).then_inc(sem(f"gl_stored{s % 2}"), 16)

                def fetch(i, s):
                    sp.wait_ge(sem("w_ready"), i * 4 + (since("w_ready", l) + s + 1))
                    sp.dma_start(GL[:, s % 2, :], gl_dram[i * 4 + (s + 2)]).then_inc(sem(f"gl_loaded{s % 2}"), 16)

                for c in range(8):
                    load(c % 4, u[c], b0 + c // 4)
                with sp.Fori(0, groups - 2) as i:
                    for s in range(4):
                        store(i, s)
                        load(s, u[i * 4 + (8 + s)], i + (b0 + 2))
                with sp.Fori(groups - 2, groups) as i:
                    for s in range(4):
                        store(i, s)
                        load(s, v[i * 4 + (8 + s - SPILL)], i + (b0 + 2))
                for s in range(2):
                    sp.wait_ge(sem(f"gl_stored{s}"), 8 * SPILL * (l + 1))
                    sp.dma_start(GL[:, s, :], gl_dram[s]).then_inc(sem(f"gl_loaded{s}"), 16)
                with sp.Fori(0, groups - 2) as i:
                    for s in range(4):
                        fetch(i, s)
                        load(s, v[i * 4 + (8 + s)], i + (b0 + groups + 2))
                for s, src in enumerate((u[SPILL], u[SPILL + 1], v[SPILL], u[SPILL + 2])):
                    fetch(groups - 2, s)
                    load(s, src, b0 + 2 * groups)
                for s in range(2):
                    fetch(groups - 1, s)
                load(0, v[SPILL + 1], b0 + 2 * groups + 1)
                with sp.Fori(1, ROUNDS - 1) as i:
                    load(1, u[i * 2 + (SPILL + 1)], i + (b0 + 2 * groups))
                    load(2, v[i * 2 + SPILL], i + (b0 + 2 * groups))
                    load(3, u[i * 2 + (SPILL + 2)], i + (b0 + 2 * groups))
                    load(0, v[i * 2 + (SPILL + 1)], i + (b0 + 2 * groups + 1))
                for pos, src in ((1, u[KEYS - 1]), (2, v[KEYS - 2]), (3, v[KEYS - 1])):
                    load(pos, src, b0 + 2 * groups + ROUNDS - 1)

        @block.gpsimd
        def _(pool):
            pool.dma_start(cT[:, :], a["cT"]).then_inc(sem("cT_in"), 16)
            pool.dma_start(const[:, :], a["const"]).then_inc(sem("const_in"), 16)
            pool.dma_start(bmod[:, :], a["b_mod"]).then_inc(sem("small_in"), 16)
            pool.dma_start(rows[:, :], a["rows"].partition_broadcast(P)).then_inc(sem("small_in"), 16)
            pool.dma_start(ar(A_TMP + 256, 256), a["lam"].partition_broadcast(P)).then_inc(sem("small_in"), 16)
            pool.dma_start(Xv, a["x"].rearrange("(t p) d -> p t d", p=P)).then_inc(sem("x_in"), 16)
            pool.dma_start(uq_w[:, :].rearrange("p (k n) -> p k n", k=2),
                           a["w_uq"].rearrange("(k p) n -> p k n", p=P)).then_inc(sem("uw_in"), 16)
            pool.dma_start(ukv_w[:, :], a["w_ukv"]).then_inc(sem("uw_in"), 16)

            def store(dst, src, name):
                pool.dma_start(dst, src).then_inc(sem(name), 16)

            def split(first, last):
                def four(t):
                    for s in range(RING):
                        pool.wait_ge(hi_done(s), t + 1)
                        pool.tensor_tensor(slot_lo[s], slot[s], f32(slot_hi[s]), ALU.subtract
                                           ).then_inc(lo_done(s), 1)
                first, last = first // RING, min(last, total) // RING
                if last - first > 4:
                    with pool.Fori(first, last) as t:
                        four(t)
                else:
                    for t in range(first, last):
                        four(t)

            def ahead(stage, first=0, last=None):
                split(start[stage] + first + RING, start[stage] + (size[stage] if last is None else last) + RING)

            def features(n):
                for t in range(NT):
                    pool.wait_ge(sem("xhi_act"), since("xhi_act", n) + t + 1)
                    r = slice(P * t, P * t + P)
                    pool.tensor_tensor(xl[:, 4:8, r], HF[:, 4:8, r], f32(xh[:, 4:8, r]), ALU.subtract
                                       ).then_inc(sem("xlo_pool"), 1)

            def norm_rows(n):
                pool.dma_start(norm_room(n), a["ln"][n:n + 1, :].rearrange("a n -> (a n)").partition_broadcast(P)
                               ).then_inc(sem("ln_in"), 16)

            split(0, RING)
            for l in range(LAYERS):
                n = 2 * l
                features(n)
                pool.dma_start(TAB, a["table"]).then_inc(sem("table_in"), 16)
                if l == 0:
                    pool.dma_start(CA[:, 0, :], a["cache_a_k"]).then_inc(sem("cache0"), 16)
                    pool.dma_start(CA[:, 1, :], a["cache_a_v"]).then_inc(sem("cache0"), 16)
                    pool.dma_start(CB[:, 0:128], a["cache_b_ckv"]).then_inc(sem("cache0"), 16)
                    pool.dma_start(CB[:, 128:160], a["cache_b_kr"]).then_inc(sem("cache0"), 16)
                else:
                    pool.dma_start(CB[:, 0:128], a["cache_c_k"]).then_inc(sem("cache1"), 16)
                    pool.dma_start(CB[:, 128:256], a["cache_c_v"]).then_inc(sem("cache1"), 16)
                    pool.dma_start(CA[:, 0, :], a["cache_d_k"]).then_inc(sem("cache1"), 16)
                    pool.dma_start(CA[:, 1, :], a["cache_d_v"]).then_inc(sem("cache1"), 16)
                ahead(("in", l))
                pool.wait_ge(sem("pr_evicted"), since("pr_evicted", l) + NT * (4 + l))
                if l == 0:
                    store(a["state_a_k"], PR[:, 0, 512:1024], "state0")
                    store(a["state_a_v"], PR[:, 0, 1024:1536], "state0")
                    store(a["state_b_kr"], PR[:, 0, 1920:1952], "state0")
                    pool.wait_ge(sem("ckv_ready"), 1)
                    store(a["state_b_ckv"], PR[:, 0, 1792:1920], "state0")
                else:
                    store(a["state_c_v"], PR[:, 0, 640:768], "state1")
                    store(a["state_d_k"], PR[:, 0, 1280:1792], "state1")
                    store(a["state_d_v"], PR[:, 0, 1792:2304], "state1")
                    pool.wait_ge(sem("prep1"), 1)
                    store(a["state_c_k"], PR[:, 0, 512:640], "state1")
                if l == 0:
                    pool.dma_start(skew,
                                   a["rpb"].unsqueeze(1).to_broadcast([120, 64, 127])).then_inc(sem("skew"), 16)
                for stage in (("mod_b", "mod_c"), ("mod_d",))[l]:
                    ahead(stage)
                pool.wait_ge(sem(f"state{l}"), 64)
                pool.wait_ge(sem("o_ready"), since("o_ready", n + 1) + 24)
                norm_rows(n)
                pool.dma_start(ktab[:, :].rearrange("p (j n) -> p j n", j=2),
                               a["keys"][l]).then_inc(sem("keys_in"), 16)
                ahead(("out", l))
                features(n + 1)
                ahead(("q", l))
                late = 2 * SPILL + SPILL + 8
                ahead(("uv", l), 0, late)
                pool.wait_ge(sem("w_ready"), since("w_ready", l) + 3 * QUARTER)
                norm_rows(n + 1)
                ahead(("uv", l), late)
            for t in range(NT):
                pool.wait_ge(sem("x_ready4"), t + 1)
                store(a["y"][P * t:P * t + P, :], Xv[:, t, :], "y_out")
            pool.wait_ge(sem("y_out"), 16 * NT)

        @block.tensor
        def _(pe):
            mm = pe.matmul

            pe.wait_ge(sem("silu_ready"), 1)
            csv = cs[:, :].rearrange("p (k c) -> p k c", k=KC)

            def parts(out, x, y, first, last, check=False):
                mm(out, x[0], y[0], start=first, stop=False, skip_group_check=check)
                mm(out, x[0], y[1], start=False, stop=False, skip_group_check=check)
                return mm(out, x[1], y[0], start=False, stop=last, skip_group_check=check)

            for g in range(MOD_FIRST):
                for q in range(4):
                    pe.wait_ge(loaded(q), 16 * (g + 1))
                    if q == 0 and g >= 2:
                        pe.wait_ge(sem("mod_rows"), g - 1)
                    for k in range(2):
                        ins = mm(ps[0:2, 6 + g % 2, :], csv[:, 2 * q + k, :], slot[q][:, 512 * k:512 * k + 512],
                                 start=(q == 0 and k == 0), stop=(q == 3 and k == 1))
                    ins.then_inc(mod_used(q), 1)

            def mod_chunk(stage, n):
                g, q = MOD_STAGES[stage][0] + n // 4, n % 4
                c = start[stage] + n
                pe.wait_ge(lo_done(c % RING), turn_of(c))
                if q == 0:
                    pe.wait_ge(sem("mod_rows"), g - 1)
                for k in range(2):
                    x = cs_parts[:, 4 * (2 * q + k):4 * (2 * q + k) + P]
                    r = slice(512 * k, 512 * k + 512)
                    mm(ps[:, 6 + g % 2, :], x, slot_hi[c % RING][:, r], start=(q == 0 and k == 0), stop=False)
                    ins = mm(ps[:, 6 + g % 2, :], x, slot_lo[c % RING][:, r], start=False, stop=(q == 3 and k == 1))
                ins.then_inc(used(c % RING), 1)

            def mod_columns(b):
                m = MOD_BATCHES[b][1]
                pe.wait_ge(sem("mod_back"), 16 * (b + 1))
                pieces = 2 if b else 1
                for c in range(2):
                    for p in range(pieces):
                        r = P * (2 * p + c)
                        ins = mm(ps[:, 7, m * c:m * c + m], ar(A_MCOL, 512)[0:m, r:r + P], ident[0:m, 0:m],
                                 start=(p == 0), stop=(p == pieces - 1))
                ins.then_inc(sem("mod_turned"), 1)

            def turn(name, src, first_wait):
                for t in range(NT):
                    first_wait(t)
                    for q in range(2):
                        for k in range(4):
                            ins = pe.transpose(ps[:, 2 * t + q, P * k:P * k + P], src(t, P * (4 * q + k)), ident)
                        ins.then_inc(sem(name), 1)

            def gate(n, c, q, bank):
                pe.wait_ge(sem("diag"), since("diag", n) + c + 1)
                mm(ps[:, bank, :], ones, diag_room(n, c)[:, 512 * q:512 * q + 512], start=True, stop=True
                   ).then_inc(sem("gt_ps"), 1)

            def project(stage, width, columns, between=None):
                groups = (width + 511) // 512

                def share(g, q, t):
                    n = min(512, width - 512 * g)
                    pos = (start[stage] + 4 * g + q) % RING
                    r = slice(P * t, P * t + P)
                    for k in range(2):
                        w = slice(512 * k, 512 * k + n)
                        ins = parts(ps[:, t + 3 * (g % 2), 0:n], (xh[:, 2 * q + k, r], xl[:, 2 * q + k, r]),
                                    (slot_hi[pos][:, w], slot_lo[pos][:, w]), q == 0 and k == 0, q == 3 and k == 1)
                    return ins

                for g in range(groups):
                    c = start[stage] + 4 * g

                    def bank_free(t):
                        if g >= 2:
                            pe.wait_ge(sem("pr_evicted"), since("pr_evicted", stage[1]) + NT * (g - 2) + t + 1)

                    if g < groups - 1:
                        for q in range(4):
                            pe.wait_ge(lo_done((c + q) % RING), turn_of(c + q))
                            for t in range(NT):
                                if q == 0:
                                    bank_free(t)
                                if g == 0 and q == 0:
                                    columns(t)
                                ins = share(g, q, t)
                            ins.then_inc(used((c + q) % RING), 1)
                    else:
                        for t in range(NT):
                            bank_free(t)
                            for q in range(4):
                                if t == 0:
                                    pe.wait_ge(lo_done((c + q) % RING), turn_of(c + q))
                                ins = share(g, q, t)
                                if t == NT - 1:
                                    ins.then_inc(used((c + q) % RING), 1)
                            if t < NT - 1:
                                ins.then_inc(sem("rows_ps"), 1)
                    if between and g == 0:
                        between()

            def wait_h(n, t=NT - 1):
                pe.wait_ge(sem("xlo_dve"), since("xlo_dve", n) + t + 1)
                pe.wait_ge(sem("xlo_pool"), since("xlo_pool", n) + t + 1)

            def columns_of(pos, out):
                for k in range(KC):
                    r = slice(P * k, P * k + P)
                    ins = parts(out, (slot_hi[pos][:, r], slot_lo[pos][:, r]), (xh[:, k, :], xl[:, k, :]),
                                k == 0, k == KC - 1)
                ins.then_inc(used(pos), 1)

            def attention(l, g, mods=None):
                d, nk, kmap, _ = group(l, g)
                for n in range(8 + nk):
                    if n >= 2:
                        if n % 2 == 0:
                            pe.wait_ge(sem("qkT_dve"), since("qkT_dve", 2 * l + g) + n // 2)
                        else:
                            pe.wait_ge(sem("qkT_act"), since("qkT_act", 2 * l + g) + n // 2)
                    if n < 8:
                        for t in range(NT):
                            ins = pe.transpose(ps[0:d, 6 + n % 2, P * t:P * t + P], q_rows(l, g, t, n), ident)
                    else:
                        for b in range(4):
                            ins = pe.transpose(ps[0:d, 6 + n % 2, P * b:P * b + P], k_rows(l, g, b, n - 8), ident)
                    ins.then_inc(sem("qk_ps"), 1)
                pe.wait_ge(sem("qkT_dve"), since("qkT_dve", 2 * l + g) + (8 + nk) // 2)
                pe.wait_ge(sem("qkT_act"), since("qkT_act", 2 * l + g) + (8 + nk) // 2)
                N = len(JOBS)
                biased = l == 1 and g == 1
                for i in range(N + 3):
                    if i < N:
                        j, t = JOBS[i]
                        k0, kn = (0, P) if t == 0 else (P, TOK)
                        if i >= 2:
                            pe.wait_ge(sem("p_ready"), since("p_ready", 2 * l + g) + i - 1)
                        mm(ps[:, i % 2, 0:kn], QT[0:d, j, P * t:P * t + P], KT[0:d, kmap(j), k0:k0 + kn],
                           start=True, stop=True).then_inc(sem("sc_ps"), 1)
                    if 2 <= i <= N + 1:
                        m = i - 2
                        j, t = JOBS[m]
                        pe.wait_ge(sem("p_ready"), since("p_ready", 2 * l + g) + m + 1)
                        if m >= 2:
                            pe.wait_ge(sem("pT_ready"), since("pT_ready", 2 * l + g) + m - 1)
                        for b in range(len(blocks(t))):
                            ins = pe.transpose(ps[:, 2 + m % 2, P * b:P * b + P], PB[:, m % 2, P * b:P * b + P], ident)
                        ins.then_inc(sem("pT_ps"), 1)
                    if i >= 3:
                        m = i - 3
                        j, t = JOBS[m]
                        pe.wait_ge(sem("pT_ready"), since("pT_ready", 2 * l + g) + m + 1)
                        if m >= 2:
                            pe.wait_ge(sem("o_ready"), since("o_ready", 2 * l + g) + m - 1)
                        bl = blocks(t)
                        for x, b in enumerate(bl):
                            ins = mm(ps[:, 4 + m % 2, 0:P], PT[:, m % 2, P * x:P * x + P], v_rows(l, g, b, j),
                                     start=(x == 0), stop=(x == len(bl) - 1))
                        ins.then_inc(sem("o_ps"), 1)
                    if mods and i < N:
                        mod_chunk(mods[0], mods[1] + i)

            def latent():
                pe.wait_ge(sem("cq_ready"), 1)
                pe.wait_ge(sem("ckv_ready"), 1)
                for k in range(2):
                    for t in range(NT):
                        ins = pe.transpose(ps[:, k, P * t:P * t + P], PR[:, t, 1536 + P * k:1664 + P * k], ident)
                    ins.then_inc(sem("c_ps"), 1)
                for b in range(4):
                    src = PR[:, b, 1792:1920] if b < 3 else CB[:, 0:128]
                    ins = pe.transpose(ps[:, 2, P * b:P * b + P], src, ident)
                ins.then_inc(sem("c_ps"), 1)
                pe.wait_ge(sem("cT_ready"), 3)
                pe.wait_ge(sem("uw_in"), 32)
                pe.wait_ge(sem("mod_rows"), 5)
                n = 0
                for t in range(NT):
                    for q in range(2):
                        if n >= 4:
                            pe.wait_ge(sem("up_ready"), n - 3)
                        w = 512 - 256 * q
                        for k in range(2):
                            ins = mm(ps[:, 4 + n % 4, 0:w], cqT[:, TOK * k + P * t:TOK * k + P * t + P],
                                     uq_w[:, 768 * k + 512 * q:768 * k + 512 * q + w], start=(k == 0), stop=(k == 1))
                        ins.then_inc(sem("up_ps"), 1)
                        n += 1
                for b in range(4):
                    for q in range(2):
                        pe.wait_ge(sem("up_ready"), n - 3)
                        mm(ps[:, 4 + n % 4, :], ckvT[:, P * b:P * b + P], ukv_w[:, 512 * q:512 * q + 512],
                           start=True, stop=True).then_inc(sem("up_ps"), 1)
                        n += 1

            def retrieve(l):
                pe.wait_ge(sem("keys_in"), 16 * (l + 1))
                for c in range(17):
                    if c < 16:
                        g = start["q", l] + c
                        pe.wait_ge(lo_done(g % RING), turn_of(g))
                        if c >= 2:
                            pe.wait_ge(sem("qs_ready"), since("qs_ready", l) + c - 1)
                        columns_of(g % RING, ps[:, 6 + c % 2, 0:TOK])
                    if c >= 1:
                        m = c - 1
                        pe.wait_ge(sem("qs_ready"), since("qs_ready", l) + m + 1)
                        if m % 4 == 0 and m >= 8:
                            pe.wait_ge(sem("s_ready"), since("s_ready", l) + NT * (m // 4 - 1))
                        for t in range(NT):
                            ins = mm(ps[:, t + 3 * (m // 4 % 2), P * (m % 4):P * (m % 4) + P],
                                     ar(Q_QS, 2 * TOK)[:, TOK * (m % 2) + P * t:TOK * (m % 2) + P * t + P],
                                     ktab[:, KEYS * (m % 2):KEYS * (m % 2) + KEYS], start=True, stop=True)
                        ins.then_inc(sem("s_ps"), 1)

            def picks(l):
                pe.wait_ge(sem("s_ready"), since("s_ready", l) + 12)
                pe.wait_ge(sem("picked"), since("picked", l) + 1)
                for q in range(3):
                    for t in range(NT):
                        ins = pe.transpose(ps[:, 2 + q, P * t:P * t + P],
                                           ar(Q_ID, 9 * 128)[:, 128 * (NT * q + t):128 * (NT * q + t) + 128], ident)
                    ins.then_inc(sem("pick_ps"), 1)

            def experts(l):
                b0 = start["uv", l] // RING
                groups = SPILL // 4
                at = {name: since(name, l) for name in ("gelu", "w_ready", "g_ps", "g_ready", "oh_ready")}

                def build(p, bank, free):
                    pe.wait_ge(sem("oh_ready"), p + (at["oh_ready"] + 1))
                    if free is not None:
                        pe.wait_ge(sem("g_ready"), p + (at["g_ready"] + free))
                    oa = ar(Q_OA, OA_N).bitcast(F16).rearrange("p (e t) -> p e t", e=KEYS)
                    ob = ar(Q_OB, 2 * OB_N).bitcast(F16).rearrange("p (j e t) -> p j e t", j=2,
                                                                                      e=QUARTER)
                    for t in range(PIECE):
                        for j in range(2):
                            ins = mm(ps[:, bank, QUARTER * t:QUARTER * t + QUARTER], oa[:, :, t], ob[:, j, :, t],
                                     start=(j == 0), stop=(j == 1))
                    ins.then_inc(sem("g_ps"), 1)

                def hidden(pos, turn, bank, gelus):
                    pe.wait_ge(lo_done(pos), turn)
                    if gelus is not None:
                        pe.wait_ge(sem("gelu"), gelus)
                    columns_of(pos, ps[:, bank, 0:TOK])

                def outer(pos, turn, odd, ready, first=False, last=False):
                    pe.wait_ge(lo_done(pos), turn)
                    pe.wait_ge(sem("w_ready"), ready)
                    for t in range(NT):
                        r = slice(TOK * odd + P * t, TOK * odd + P * t + P)
                        for q in range(2):
                            c = slice(512 * q, 512 * q + 512)
                            ins = parts(ps[:, t + 3 * q, :], (w_hi[:, r], w_lo[:, r]),
                                        (slot_hi[pos][:, c], slot_lo[pos][:, c]), first, last, True)
                    ins.then_inc(used(pos), 1)

                for s in range(4):
                    hidden(s, b0 + 1, 6 + s % 2, at["gelu"] + s - 1 if s >= 2 else None)
                with pe.Fori(1, groups // 2) as i:
                    for s in range(4):
                        hidden(s, i + (b0 + 1), 6 + s % 2, i * 4 + (at["gelu"] + s - 1))
                picks(l)

                def both(i, first):
                    for s in range(4):
                        hidden(s, i + (b0 + 1), 6 + s % 2, i * 4 + (at["gelu"] + s - 1))
                        build(i * 4 + (s - QUARTER), s % 2, None if first and s < 2 else -1)

                both(groups // 2, True)
                with pe.Fori(groups // 2 + 1, groups) as i:
                    both(i, False)
                pe.wait_ge(sem("it_ready"), since("it_ready", l) + 3)
                pe.wait_ge(sem("g_ready"), at["g_ready"] + QUARTER)
                pe.wait_ge(sem("gelu"), at["gelu"] + SPILL)

                def four(i, first):
                    for s in range(4):
                        build(i * 4 + (QUARTER + s), 7, 0)
                        outer(s, i + (b0 + groups + 1), s % 2, i * 4 + (at["w_ready"] + s + 1), first and s == 0)

                four(0, True)
                with pe.Fori(1, groups) as i:
                    four(i, False)
                b1 = b0 + 2 * groups
                hidden(0, b1 + 1, 6, None)

                def step(i, s, piece, last=False, gates=None):
                    j = i * 2 + s
                    if not last:
                        hidden(1 + 2 * s, i + (b1 + 1), 6, j + (at["gelu"] + SPILL + 1))
                    if piece:
                        build(j + 3 * QUARTER, 7, 0)
                    if gates is not None:
                        if gates == 0:
                            pe.wait_ge(sem("g_ready"), at["g_ready"] + 4 * QUARTER)
                        else:
                            pe.wait_ge(sem("gt_evicted"), since("gt_evicted", 2 * l + 1) + gates)
                        gate(2 * l + 1, gates // 2, gates % 2, 7)
                    if last:
                        outer(3, i + (b1 + 1), s, j + (at["w_ready"] + SPILL + 1), last=True)
                    else:
                        outer((2 + 2 * s) % 4, i + (b1 + 1 + s), s, j + (at["w_ready"] + SPILL + 1))

                with pe.Fori(0, ROUNDS // 2) as i:
                    for s in range(2):
                        step(i, s, True)
                with pe.Fori(ROUNDS // 2, ROUNDS - 2) as i:
                    for s in range(2):
                        step(i, s, False)
                for i in (ROUNDS - 2, ROUNDS - 1):
                    for s in range(2):
                        step(i, s, False, i == ROUNDS - 1 and s == 1, 2 * (i - ROUNDS + 2) + s)

            pe.wait_ge(sem("const_in"), 16)
            for l in range(LAYERS):
                n = 2 * l
                turn("h_turned", lambda t, c: Xv[:, t, c:c + P], lambda t: pe.wait_ge(sem("x_in"), 16) if l == 0 else
                     pe.wait_ge(sem(f"x_ready{n}"), t + 1))
                if l == 0:
                    mod_columns(0)
                project(("in", l), IN_W[l], lambda t: wait_h(n, t))
                if l == 0:
                    for m in range(4):
                        mod_chunk("mod_b", m)
                pe.wait_ge(sem("pr_evicted"), since("pr_evicted", l + 1))
                pe.wait_ge(sem(f"prep{l}"), 1)
                pe.wait_ge(sem(f"cache{l}"), 64)
                if l == 0:
                    latent()
                    pe.wait_ge(sem("up_ready"), 14)
                attention(l, 0, ("mod_b", 4) if l == 0 else ("mod_d", 0))
                if l == 0:
                    for m in range(28, 32):
                        mod_chunk("mod_b", m)
                    pe.wait_ge(sem("q_roped"), 2)
                pe.wait_ge(sem("mod_rows"), 24 if l else 12)
                attention(l, 1, None if l else ("mod_c", 0))
                pe.wait_ge(sem("o_ready"), since("o_ready", 2 * l + 1) + 24)
                turn("o_turned", lambda t, c: out_rows(l, t, c, P), lambda t: pe.wait_ge(sem("sub_normed"), t + 1) if l == 0 else None)
                mod_columns(l + 1)
                for q in range(2):
                    gate(n, 0, q, 6 + q)

                def second_gate():
                    for q in range(2):
                        pe.wait_ge(sem("gt_evicted"), since("gt_evicted", n) + q + 1)
                        gate(n, 1, q, 6 + q)

                project(("out", l), D, lambda t: pe.wait_ge(sem("oT_ready"), since("oT_ready", l) + 2 * t + 2),
                        second_gate)
                turn("h_turned", lambda t, c: Xv[:, t, c:c + P], lambda t: pe.wait_ge(sem(f"x_ready{n + 1}"), t + 1))
                wait_h(n + 1)
                retrieve(l)
                experts(l)

        @block.scalar
        def _(act):
            fn = act.activation

            act.wait_ge(sem("cT_in"), 16)
            fn(cs[:, :], cT[:, :], ACT.Exp, scale=-1.0).then_inc(sem("silu_exp"), 1)

            def mod_rows(g, rows):
                if g:
                    act.wait_ge(sem("mod_out"), 16 * g)
                fn(MROW[0:rows, :], ps[0:rows, 6 + g % 2, :], ACT.Copy).then_inc(sem("mod_rows"), 1)
                act.wait_ge(sem("mod_rows"), g + 1)
                act.dma_start(mod_dram[0:rows, 512 * g:512 * g + 512], MROW[0:rows, :]).then_inc(sem("mod_out"), 16)

            def mod_back(b):
                m0, m = MOD_BATCHES[b]
                rows = 4 if b else 2
                act.wait_ge(sem("mod_out"), 4 * (m0 + m))
                act.dma_start(ar(A_MCOL, P * rows)[0:m, :].rearrange("m (c n) -> m c n", c=rows),
                              mod_dram[0:rows, P * m0:P * (m0 + m)].rearrange("c (m n) -> m c n", n=P)
                              ).then_inc(sem("mod_back"), 16)

            for g in range(MOD_FIRST):
                act.wait_ge(mod_used(3), g + 1)
                mod_rows(g, 2)
            mod_back(0)
            act.wait_ge(sem("lam_dots"), 1)
            fn(lam[:, 2:4], lam[:, 0:2], ACT.Exp).then_inc(sem("lam_exp"), 1)

            def high(pos, turn):
                act.wait_ge(loaded(pos), turn * 16 + 16 * MOD_FIRST)
                fn(slot_hi[pos], slot[pos], ACT.Copy).then_inc(hi_done(pos), 1)

            def done(c):
                act.wait_ge(used(c % RING), turn_of(c))
                if c + RING < total:
                    high(c % RING, turn_of(c + RING))

            def mod_done(stage, n):
                done(start[stage] + n)
                if n % 4 == 3:
                    mod_rows(MOD_STAGES[stage][0] + n // 4, 4)

            for s in range(RING):
                high(s, 1)

            def features(n):
                l, w = n // 2, n % 2
                act.wait_ge(sem("mod_ready"), (1, 2, 2, 3)[n])
                if n:
                    act.wait_ge(sem(f"state{(n - 1) // 2}"), 64)
                for t in range(NT):
                    r = slice(P * t, P * t + P)
                    act.wait_ge(sem("h_turned"), since("h_turned", n) + 2 * t + 2)
                    for k in range(4):
                        ins = fn(HF[:, 4 + k, r], ps[:, 2 * t + 1, P * k:P * k + P], ACT.Identity,
                                 scale=modv[:, l, 3 * w + 1, 4 + k, COND[t]:COND[t] + 1],
                                 bias=modv[:, l, 3 * w, 4 + k, COND[t]:COND[t] + 1])
                    ins.then_inc(sem("h_act"), 1)
                    act.wait_ge(sem("h_act"), since("h_act", n) + t + 1)
                    fn(xh[:, 4:8, r], HF[:, 4:8, r], ACT.Copy).then_inc(sem("xhi_act"), 1)

            def gate_row(n, m, bank):
                act.wait_ge(sem("gt_ps"), since("gt_ps", n) + m + 1)
                fn(gate_room(n)[:, m // 2, 512 * (m % 2):512 * (m % 2) + 512], ps[:, bank, :], ACT.Copy
                   ).then_inc(sem("gt_evicted"), 1)

            def attention(l, g, mods=None):
                d, nk, kmap, scale = group(l, g)
                for n in range(1, 8 + nk, 2):
                    act.wait_ge(sem("qk_ps"), since("qk_ps", 2 * l + g) + n + 1)
                    if n < 8:
                        fn(QT[0:d, n, :], ps[0:d, 6 + n % 2, 0:TOK], ACT.Copy).then_inc(sem("qkT_act"), 1)
                    else:
                        fn(KT[0:d, n - 8, :], ps[0:d, 6 + n % 2, :], ACT.Copy).then_inc(sem("qkT_act"), 1)
                N = len(JOBS)
                biased = l == 1 and g == 1
                for i in range(N + 2):
                    if i < N:
                        j, t = JOBS[i]
                        kn = P if t == 0 else TOK
                        act.wait_ge(sem("mx"), since("mx", 2 * l + g) + i + 1)
                        if i >= 2:
                            act.wait_ge(sem("pT_ps"), since("pT_ps", 2 * l + g) + i - 1)
                        in_sb = biased and t > 0
                        src = SC[:, i % 2, 0:kn] if in_sb else ps[:, i % 2, 0:kn]
                        fn(PB[:, i % 2, 0:kn], src, ACT.Exp, bias=nms[:, i:i + 1], scale=1.0 if in_sb else scale,
                           accum_out=rs[:, i:i + 1]).then_inc(sem("p_ready"), 1)
                    if i >= 2:
                        m = i - 2
                        j, t = JOBS[m]
                        kn = P if t == 0 else TOK
                        act.wait_ge(sem("pT_ps"), since("pT_ps", 2 * l + g) + m + 1)
                        if m >= 2:
                            act.wait_ge(sem("o_ps"), since("o_ps", 2 * l + g) + m - 1)
                        fn(PT[:, m % 2, 0:kn], ps[:, 2 + m % 2, 0:kn], ACT.Copy).then_inc(sem("pT_ready"), 1)
                    if mods and 1 <= i <= N:
                        mod_done(mods[0], mods[1] + i - 1)

            def root(dst, src, scale, wait, done, pieces=1):
                act.wait_ge(sem(wait), pieces)
                fn(dst, src, ACT.Sqrt, scale=scale, bias=epsc).then_inc(sem(done), 1)

            def queries(l):
                for c in range(17):
                    if c < 16:
                        g = start["q", l] + c
                        act.wait_ge(used(g % RING), turn_of(g))
                        if c >= 2:
                            act.wait_ge(sem("s_ps"), since("s_ps", l) + c - 1)
                        fn(ar(Q_QS, 2 * TOK)[:, TOK * (c % 2):TOK * (c % 2) + TOK], ps[:, 6 + c % 2, 0:TOK],
                           ACT.Copy).then_inc(sem("qs_ready"), 1)
                        done(g)
                    if c >= 1 and c % 4 == 0:
                        cg = c // 4 - 1
                        act.wait_ge(sem("s_ps"), since("s_ps", l) + 4 * cg + 4)
                        for t in range(NT):
                            o = Q_S + t * 2048 + 512 * cg
                            fn(ar(o, 512), ps[:, t + 3 * (cg % 2), :], ACT.Copy
                               ).then_inc(sem("s_ready"), 1)

            def experts(l):
                b0 = start["uv", l] // RING
                groups = SPILL // 4
                b1 = b0 + 2 * groups
                at = {name: since(name, l) for name in ("gelu", "w_ready", "g_ps", "g_ready")}

                def gelu(pos, turn, bank, s):
                    act.wait_ge(used(pos), turn)
                    fn(GL[:, s, :], ps[:, bank, 0:TOK], ACT.Gelu).then_inc(sem("gelu"), 1)

                def part(p, bank, half, col):
                    act.wait_ge(sem("g_ps"), p + (at["g_ps"] + 1))
                    gv = ar(G_N * half, G_N).rearrange("p (e t) -> p e t", e=QUARTER)
                    fn(gv[:, :, bass.ds(col, PIECE)],
                       ps[:, bank, 0:PIECE * QUARTER].rearrange("p (t e) -> p e t", t=PIECE), ACT.Copy
                       ).then_inc(sem("g_ready"), 1)

                def early(i, s, piece=False, first=False):
                    if not first:
                        act.wait_ge(sem(f"gl_stored{s % 2}"), i * 32 + (16 * (s // 2) + 8 * SPILL * l))
                    gelu(s, i + (b0 + 1), 6 + s % 2, s % 2)
                    high(s, i + (b0 + 2))
                    if piece:
                        part(i * 4 + (s - QUARTER), s % 2, 0, i * (4 * PIECE) + PIECE * (s - QUARTER))

                for s in range(4):
                    early(0, s, first=s < 2)
                with act.Fori(1, groups // 2 - 1) as i:
                    for s in range(4):
                        early(i, s)
                act.wait_ge(sem("tv_ready"), since("tv_ready", l) + 1)
                fn(ar(Q_TV, 384), ar(Q_TV, 384), ACT.Exp).then_inc(sem("tv_exp"), 1)
                for s in range(4):
                    early(groups // 2 - 1, s)
                for q in range(3):
                    act.wait_ge(sem("pick_ps"), since("pick_ps", l) + q + 1)
                    dst = IT16[:, q, :] if q < 2 else ar(Q_W32, TOK)
                    fn(dst, ps[:, 2 + q, 0:TOK], ACT.Copy, scale=1.0 if q < 2 else G_SCALE
                       ).then_inc(sem("it_ready"), 1)
                act.wait_ge(sem("weights_split"), l + 1)
                with act.Fori(groups // 2, groups) as i:
                    for s in range(4):
                        early(i, s, True)
                for quarter in range(2):
                    if quarter:
                        act.wait_ge(sem("w_ready"), at["w_ready"] + QUARTER)
                    with act.Fori(quarter * groups // 2, (quarter + 1) * groups // 2) as i:
                        for s in range(4):
                            part(i * 4 + (QUARTER + s), 7, 1 - quarter,
                                 i * (4 * PIECE) + PIECE * (s - QUARTER * quarter))
                            act.wait_ge(used(s), i + (b0 + groups + 1))
                            high(s, i + (b0 + groups + 2))
                act.wait_ge(sem("w_ready"), at["w_ready"] + SPILL - 1)
                gelu(0, b1 + 1, 6, 0)
                high(0, b1 + 2)

                def step(i, s, piece, last=False, gates=None):
                    j = i * 2 + s
                    more = not (l == LAYERS - 1 and gates is not None)
                    if not last:
                        act.wait_ge(sem("w_ready"), j + (at["w_ready"] + SPILL))
                        gelu(1 + 2 * s, i + (b1 + 1), 6, (s + 1) % 2)
                        if more or gates < 2:
                            high(1 + 2 * s, i + (b1 + 2))
                    if piece:
                        part(j + 3 * QUARTER, 7, 1, i * (2 * PIECE) + PIECE * s)
                    if gates is not None:
                        gate_row(2 * l + 1, gates, 7)
                    pos = 3 if last else (2 + 2 * s) % 4
                    act.wait_ge(used(pos), i + (b1 + 1 + (0 if last else s)))
                    if more or gates < 1:
                        high(pos, i + (b1 + 2 + (0 if last else s)))

                act.wait_ge(sem("w_ready"), at["w_ready"] + 2 * QUARTER)
                with act.Fori(0, ROUNDS // 2) as i:
                    for s in range(2):
                        step(i, s, True)
                with act.Fori(ROUNDS // 2, ROUNDS - 2) as i:
                    for s in range(2):
                        step(i, s, False)
                for i in (ROUNDS - 2, ROUNDS - 1):
                    for s in range(2):
                        step(i, s, False, i == ROUNDS - 1 and s == 1, 2 * (i - ROUNDS + 2) + s)

            epsc = lam[:, 5:6]
            for l in range(LAYERS):
                n = 2 * l
                features(n)
                for g in range((IN_W[l] + 511) // 512):
                    w = min(512, IN_W[l] - 512 * g)
                    last = g == (IN_W[l] + 511) // 512 - 1
                    if not last:
                        for q in range(4):
                            done(start["in", l] + 4 * g + q)
                    for t in range(NT):
                        if last and t < NT - 1:
                            act.wait_ge(sem("rows_ps"), since("rows_ps", n) + t + 1)
                        elif last:
                            for q in range(4):
                                done(start["in", l] + 4 * g + q)
                        fn(PR[:, t, 512 * g:512 * g + w], ps[:, t + 3 * (g % 2), 0:w], ACT.Copy
                           ).then_inc(sem("pr_evicted"), 1)
                    if l and g == 2:
                        root(ss2[:, 0:30], ss[:, 0:30], 1 / 64, "c_ss", "c_root")
                if l == 0:
                    root(ss2[:, 0:3], ss[:, 0:3], 1 / 256, "cq_ss", "cq_root")
                    root(ss2[:, 3:6], ss[:, 3:6], 1 / 128, "ckv_ss", "ckv_root")
                    for m in range(4):
                        mod_done("mod_b", m)
                    for k in range(2):
                        act.wait_ge(sem("c_ps"), k + 1)
                        fn(cqT[:, TOK * k:TOK * k + TOK], ps[:, k, 0:TOK], ACT.Copy).then_inc(sem("cT_ready"), 1)
                    act.wait_ge(sem("c_ps"), 3)
                    fn(ckvT[:, :], ps[:, 2, :], ACT.Copy).then_inc(sem("cT_ready"), 1)
                    m = 0
                    for t in range(NT):
                        for q in range(2):
                            act.wait_ge(sem("up_ps"), m + 1)
                            w = 512 - 256 * q
                            fn(QR[:, t, 512 * q:512 * q + w], ps[:, 4 + m % 4, 0:w], ACT.Copy
                               ).then_inc(sem("up_ready"), 1)
                            m += 1
                    for b in range(4):
                        for q in range(2):
                            act.wait_ge(sem("up_ps"), m + 1)
                            kv = ps[:, 4 + m % 4, :].rearrange("p (h j n) -> p h j n", h=4, j=2)
                            fn(KR[:, b, 4 * q:4 * q + 4, 0:64], kv[:, :, 0, :], ACT.Copy)
                            fn(VR[:, b, 256 * q:256 * q + 256].rearrange("p (h n) -> p h n", h=4), kv[:, :, 1, :],
                               ACT.Copy).then_inc(sem("up_ready"), 1)
                            m += 1
                attention(l, 0, ("mod_d", 0) if l else ("mod_b", 4))
                if l == 0:
                    for m in range(28, 32):
                        mod_done("mod_b", m)
                attention(l, 1, None if l else ("mod_c", 0))
                if l == 0:
                    root(ss2[:, 0:12], ss[:, 0:12], 1 / 128, "sub_ss", "sub_root", NT)
                mod_back(l + 1)
                for b in range(6):
                    act.wait_ge(sem("o_turned"), since("o_turned", l) + b + 1)
                    t, q = b // 2, b % 2
                    fn(xh[:, 4 * q:4 * q + 4, P * t:P * t + P], ps[:, b, :].rearrange("p (k n) -> p k n", k=4),
                       ACT.Copy).then_inc(sem("oT_hi"), 1)
                for m in range(2):
                    gate_row(n, m, 6 + m)
                for c in range(8):
                    done(start["out", l] + c)
                    if c == 3:
                        for m in range(2):
                            gate_row(n, 2 + m, 6 + m)
                for w in range(2):
                    m = n + w
                    if w:
                        features(m)
                        queries(l)
                        experts(l)
                    for t in range(NT):
                        act.wait_ge(sem("var"), since("var", m) + t + 1)
                        fn(rstd[:, t:t + 1], mv[:, 2 * t + 1:2 * t + 2], ACT.Sqrt, bias=epsc
                           ).then_inc(sem("std"), 1)

        @block.vector
        def _(dve):
            linked = [0]

            def link(ins):
                linked[0] += 1
                ins.then_inc(sem("dve_link"), 1)
                dve.wait_ge(sem("dve_link"), linked[0])

            tt, ts, stt = dve.tensor_tensor, dve.tensor_scalar, dve.scalar_tensor_tensor

            dve.memset(lam[:, 5:6], EPS).then_inc(sem("eps_set"), 1)
            dve.wait_ge(sem("silu_exp"), 1)
            link(ts(cs[:, :], cs[:, :], 1.0, None, ALU.add))
            link(dve.reciprocal(cs[:, :], cs[:, :]))
            tt(cs[:, :], cs[:, :], cT[:, :], ALU.mult).then_inc(sem("silu_ready"), 1)
            dve.wait_ge(sem("silu_ready"), 1)
            csp = cs_parts[:, 0:4 * KC].rearrange("p (k j c) -> p k j c", k=KC, j=2)
            csv = cs[:, :].rearrange("p (k c) -> p k c", k=KC)
            dve.wait_ge(sem("const_in"), 16)
            dve.tensor_copy(cs_parts[:, 4 * KC:4 * KC + P], iota)
            link(dve.tensor_copy(csp[:, :, 0, :], csv))
            link(tt(csp[:, :, 1, :], csv, f32(csp[:, :, 0, :]), ALU.subtract))
            dve.wait_ge(sem("small_in"), 48)
            for j in range(2):
                link(tt(ar(A_TMP + 64 * j, 64), lq(2 * j), lq(2 * j + 1), ALU.mult))
            dve.tensor_reduce(lam[:, 0:2], ar(A_TMP, 128).rearrange("p (j n) -> p j n", j=2), AX.X, ALU.add
                              ).then_inc(sem("lam_dots"), 1)

            def mod_columns(b):
                m0, m = MOD_BATCHES[b]
                dve.wait_ge(sem("mod_turned"), b + 1)
                mv3 = mod[:, :].rearrange("p (c m) -> p c m", c=2)
                link(tt(mv3[:, :, m0:m0 + m], ps[:, 7, 0:2 * m].rearrange("p (c m) -> p c m", c=2),
                        bmod[:, m0:m0 + m].unsqueeze(1).to_broadcast([P, 2, m]), ALU.add))
                for at in range(KC, MODS, 3 * KC):
                    if m0 <= at < m0 + m:
                        ins = ts(mv3[:, :, at:at + KC], mv3[:, :, at:at + KC], 1.0, None, ALU.add)
                ins.then_inc(sem("mod_ready"), 1)
                dve.wait_ge(sem("mod_ready"), b + 1)

            mod_columns(0)
            dve.wait_ge(sem("lam_exp"), 1)
            link(tt(lam[:, 4:5], lam[:, 3:4], lam[:, 2:3], ALU.subtract))
            link(ts(lam[:, 4:5], lam[:, 4:5], -LAM_INIT, None, ALU.add))
            link(ts(rows[:, R_SUB:R_SUB + 128], rows[:, R_SUB:R_SUB + 128], 1.0 - LAM_INIT, None, ALU.mult))

            def features(n):
                l, w = n // 2, n % 2
                if n:
                    dve.wait_ge(sem(f"state{(n - 1) // 2}"), 64)
                for t in range(NT):
                    r = slice(P * t, P * t + P)
                    dve.wait_ge(sem("h_turned"), since("h_turned", n) + 2 * t + 1)
                    for k in range(4):
                        ins = ts(HF[:, k, r], ps[:, 2 * t, P * k:P * k + P],
                                 modv[:, l, 3 * w + 1, k, COND[t]:COND[t] + 1],
                                 modv[:, l, 3 * w, k, COND[t]:COND[t] + 1], ALU.mult, ALU.add)
                    link(ins)
                    link(dve.tensor_copy(xh[:, 0:4, r], HF[:, 0:4, r]))
                    tt(xl[:, 0:4, r], HF[:, 0:4, r], f32(xh[:, 0:4, r]), ALU.subtract).then_inc(sem("xlo_dve"), 1)

            def diagonals(n):
                l, w = n // 2, n % 2
                for c in range(2):
                    tt(diag_room(n, c).rearrange("p (k n) -> p k n", k=KC),
                       ident.unsqueeze(1).to_broadcast([P, KC, P]),
                       modv[:, l, 3 * w + 2, :, c:c + 1].to_broadcast([P, KC, P]), ALU.mult
                       ).then_inc(sem("diag"), 1)

            def out_columns(l):
                for b in range(6):
                    dve.wait_ge(sem("oT_hi"), since("oT_hi", l) + b + 1)
                    t, q = b // 2, b % 2
                    r = slice(P * t, P * t + P)
                    tt(xl[:, 4 * q:4 * q + 4, r], ps[:, b, :].rearrange("p (k n) -> p k n", k=4),
                       f32(xh[:, 4 * q:4 * q + 4, r]), ALU.subtract).then_inc(sem("oT_ready"), 1)

            def norm(n):
                dve.wait_ge(sem("gt_evicted"), since("gt_evicted", n) + 4)
                dve.wait_ge(sem("ln_in"), 16 * (n + 1))
                gtv = gate_room(n)
                tmp = work_room(n)
                lnv = norm_room(n).rearrange("p (j d) -> p j d", j=2)

                def residual(t):
                    if n % 2:
                        dve.wait_ge(used(3), turn_of(start["uv", n // 2] + 2 * KEYS - 1))
                    else:
                        c = start["out", n // 2]
                        if t == 0:
                            dve.wait_ge(used((c + 3) % RING), turn_of(c + 3))
                        if t < NT - 1:
                            dve.wait_ge(sem("rows_ps"), since("rows_ps", n + 1) + t + 1)
                        else:
                            dve.wait_ge(used((c + 7) % RING), turn_of(c + 7))
                    for q in range(2):
                        ins = tt(tmp[:, 512 * q:512 * q + 512], ps[:, t + 3 * q, :],
                                 gtv[:, COND[t], 512 * q:512 * q + 512], ALU.mult)
                    link(ins)
                    link(stt(Xv[:, t, :], Xv[:, t, :], ALPHA, tmp, ALU.mult, ALU.add))
                    for q in range(2):
                        ins = dve.bn_stats(stat[:, 12 * t + 6 * q:12 * t + 6 * q + 6], Xv[:, t, 512 * q:512 * q + 512])
                    link(ins)
                    dve.bn_aggr(mv[:, 2 * t:2 * t + 2], stat[:, 12 * t:12 * t + 12]).then_inc(sem("var"), 1)

                def scaled(t):
                    dve.wait_ge(sem("std"), since("std", n) + t + 1)
                    link(dve.reciprocal(rstd[:, t:t + 1], rstd[:, t:t + 1]))
                    link(ts(Xv[:, t, :], Xv[:, t, :], mv[:, 2 * t:2 * t + 1], rstd[:, t:t + 1],
                            ALU.subtract, ALU.mult))
                    link(tt(Xv[:, t, :], Xv[:, t, :], lnv[:, 0, :], ALU.mult))
                    tt(Xv[:, t, :], Xv[:, t, :], lnv[:, 1, :], ALU.add).then_inc(sem(f"x_ready{n + 1}"), 1)

                residual(0)
                residual(1)
                scaled(0)
                residual(2)
                scaled(1)
                scaled(2)

            TMP = ar(A_TMP, 2048)

            def rope(x, heads, half, cosv, sinv, done=None):
                tmp = TMP[:, 0:heads * 2 * half].rearrange("p (h n) -> p h n", h=heads)

                def over(v):
                    return v.unsqueeze(1).to_broadcast([P, heads, v.shape[-1]])
                tt(tmp[:, :, 0:half], x[:, :, half:2 * half], over(sinv[:, 0:half]), ALU.mult)
                link(tt(tmp[:, :, half:2 * half], x[:, :, 0:half], over(sinv[:, half:2 * half]), ALU.mult))
                link(tt(x, x, over(cosv), ALU.mult))
                ins = tt(x, x, tmp, ALU.add)
                if done:
                    ins.then_inc(sem(done), 1)
                else:
                    link(ins)

            def table(c, t, w):
                return TAB[:, c + w * (t - 1):c + w * t]

            def prep0():
                dve.wait_ge(sem("pr_evicted"), since("pr_evicted", 0) + 6)
                dve.wait_ge(sem("table_in"), 16)
                for t in (1, 2):
                    rope(PR[:, t, 0:1024].rearrange("p (h n) -> p h n", h=16), 16, 32,
                         table(T_COSA, t, 64), table(T_SINA, t, 64))
                dve.wait_ge(sem("pr_evicted"), since("pr_evicted", 0) + 12)
                for at, w, off, r, name in ((1536, 256, 0, R_CQ, "cq"), (1792, 128, 3, R_CKV, "ckv")):
                    x = PR[:, :, at:at + w]
                    tmp = TMP[:, 0:3 * w].rearrange("p (t n) -> p t n", t=NT)
                    link(tt(tmp, x, x, ALU.mult))
                    dve.tensor_reduce(ss[:, off:off + 3], tmp, AX.X, ALU.add).then_inc(sem(f"{name}_ss"), 1)
                    dve.wait_ge(sem(f"{name}_ss"), 1)
                for at, w, off, r, name in ((1536, 256, 0, R_CQ, "cq"), (1792, 128, 3, R_CKV, "ckv")):
                    x = PR[:, :, at:at + w]
                    dve.wait_ge(sem(f"{name}_root"), 1)
                    link(dve.reciprocal(ss2[:, off:off + 3], ss2[:, off:off + 3]))
                    link(tt(x, x, ss2[:, off:off + 3].unsqueeze(2).to_broadcast([P, NT, w]), ALU.mult))
                    tt(x, x, rows[:, r:r + w].unsqueeze(1).to_broadcast([P, NT, w]), ALU.mult
                       ).then_inc(sem("ckv_ready" if name == "ckv" else "cq_ready"), 1)
                for t in (1, 2):
                    rope(PR[:, t, 1920:1952].rearrange("p (h n) -> p h n", h=1), 1, 16,
                         table(T_COSB, t, 32), table(T_SINB, t, 32))
                dve.wait_ge(sem("cache0"), 64)
                for b in range(4):
                    src = PR[:, b, 1920:1952] if b < 3 else CB[:, 128:160]
                    ins = dve.tensor_copy(KR[:, b, :, 64:96], src.unsqueeze(1).to_broadcast([P, 8, 32]))
                ins.then_inc(sem("prep0"), 1)

            def prep1():
                dve.wait_ge(sem("pr_evicted"), since("pr_evicted", 1) + 6)
                dve.wait_ge(sem("table_in"), 32)
                x = PR[:, :, 0:640].rearrange("p t (h n) -> p t h n", h=10)
                tmp = TMP[:, 0:1920].rearrange("p (t h n) -> p t h n", t=NT, h=10)
                sv = ss[:, 0:30].rearrange("p (t h) -> p t h", t=NT)
                link(tt(tmp, x, x, ALU.mult))
                dve.tensor_reduce(sv, tmp, AX.X, ALU.add).then_inc(sem("c_ss"), 1)
                dve.wait_ge(sem("c_root"), 1)
                link(dve.reciprocal(ss2[:, 0:30], ss2[:, 0:30]))
                s2 = ss2[:, 0:30].rearrange("p (t h) -> p t h", t=NT)
                link(tt(x, x, s2.unsqueeze(3).to_broadcast([P, NT, 10, 64]), ALU.mult))
                for t in range(NT):
                    tt(x[:, t, 0:8, :], x[:, t, 0:8, :],
                       rows[:, R_QN:R_QN + 64].unsqueeze(1).to_broadcast([P, 8, 64]), ALU.mult)
                    link(tt(x[:, t, 8:10, :], x[:, t, 8:10, :],
                            rows[:, R_KN:R_KN + 64].unsqueeze(1).to_broadcast([P, 2, 64]), ALU.mult))
                for t in (1, 2):
                    rope(PR[:, t, 0:640].rearrange("p (h n) -> p h n", h=10), 10, 32,
                         table(T_COSA, t, 64), table(T_SINA, t, 64), "prep1" if t == 2 else None)

            def mask_bias():
                dve.wait_ge(sem("bias_in"), 16 * 32)
                bv = ar(A_BIAS, 4096).rearrange("p (n c) -> p n c", c=64)
                link(tt(bv, bv, TAB[:, T_MASK:T_MASK + 64].unsqueeze(1).to_broadcast([P, 64, 64]), ALU.add))

            def attention(l, g):
                d, nk, kmap, scale = group(l, g)
                if l == 0 and g == 1:
                    dve.wait_ge(sem("up_ready"), 6)
                    for t in (1, 2):
                        if t == 2:
                            dve.wait_ge(sem("q_roped"), 1)
                        rope(QR[:, t, :].rearrange("p (h n) -> p h n", h=8)[:, :, 64:96], 8, 16,
                             table(T_COSB, t, 32), table(T_SINB, t, 32), "q_roped")
                for n in range(0, 8 + nk, 2):
                    dve.wait_ge(sem("qk_ps"), since("qk_ps", 2 * l + g) + n + 1)
                    if n < 8:
                        dve.tensor_copy(QT[0:d, n, :], ps[0:d, 6, 0:TOK]).then_inc(sem("qkT_dve"), 1)
                    else:
                        dve.tensor_copy(KT[0:d, n - 8, :], ps[0:d, 6, :]).then_inc(sem("qkT_dve"), 1)
                N = len(JOBS)
                biased = l == 1 and g == 1
                for i in range(N + 3):
                    m = i - 3
                    if i < N:
                        j, t = JOBS[i]
                        kn = P if t == 0 else TOK
                        dve.wait_ge(sem("sc_ps"), since("sc_ps", 2 * l + g) + i + 1)
                        in_sb = biased and t > 0
                        if in_sb:
                            if i >= 2:
                                dve.wait_ge(sem("p_ready"), since("p_ready", 2 * l + g) + i - 1)
                            stt(SC[:, i % 2, 0:256], ps[:, i % 2, 0:256], scale, BIAS[:, t - 1, j, :],
                                ALU.mult, ALU.add)
                            link(ts(SC[:, i % 2, 256:384], ps[:, i % 2, 256:384], scale, None, ALU.mult))
                        ins = dve.tensor_reduce(nm[:, i:i + 1], SC[:, i % 2, :] if in_sb else ps[:, i % 2, 0:kn],
                                                AX.X, ALU.max)
                    if m >= 0:
                        dve.wait_ge(sem("p_ready"), since("p_ready", 2 * l + g) + m + 1)
                        ins = dve.reciprocal(rr[:, m:m + 1], rs[:, m:m + 1])
                    link(ins)
                    if i < N:
                        ts(nms[:, i:i + 1], nm[:, i:i + 1], -1.0 if in_sb else -scale, None, ALU.mult
                           ).then_inc(sem("mx"), 1)
                    if m >= 0:
                        j, t = JOBS[m]
                        c0, dv = out_cols(l, g, j)
                        subtracted = l == 0 and g == 0 and j % 2
                        if subtracted:
                            link(tt(rr[:, m:m + 1], rr[:, m:m + 1], lam[:, 4:5], ALU.mult))
                        dve.wait_ge(sem("o_ps"), since("o_ps", 2 * l + g) + m + 1)
                        off = v_off(l, g, j)
                        dst, src = out_rows(l, t, c0, dv), ps[:, 4 + m % 2, off:off + dv]
                        if subtracted:
                            stt(dst, src, rr[:, m:m + 1], dst, ALU.mult, ALU.add).then_inc(sem("o_ready"), 1)
                        else:
                            ts(dst, src, rr[:, m:m + 1], None, ALU.mult).then_inc(sem("o_ready"), 1)

            def sub_norm():
                dve.wait_ge(sem("o_ready"), since("o_ready", 0) + 24)
                for t in range(NT):
                    tmp = TMP[:, 0:512].rearrange("p (h n) -> p h n", h=4)
                    x = out_rows(0, t, 0, 512).rearrange("p (h n) -> p h n", h=4)
                    link(tt(tmp, x, x, ALU.mult))
                    dve.tensor_reduce(ss[:, 4 * t:4 * t + 4], tmp, AX.X, ALU.add).then_inc(sem("sub_ss"), 1)
                    dve.wait_ge(sem("sub_ss"), t + 1)
                dve.wait_ge(sem("sub_root"), 1)
                link(dve.reciprocal(ss2[:, 0:12], ss2[:, 0:12]))
                for t in range(NT):
                    x = out_rows(0, t, 0, 512).rearrange("p (h n) -> p h n", h=4)
                    link(tt(x, x, ss2[:, 4 * t:4 * t + 4].unsqueeze(2).to_broadcast([P, 4, 128]), ALU.mult))
                    tt(x, x, rows[:, R_SUB:R_SUB + 128].unsqueeze(1).to_broadcast([P, 4, 128]), ALU.mult
                       ).then_inc(sem("sub_normed"), 1)

            def retrieve(l):
                S = ar(Q_S, NT * 2048).rearrange("p (t c n) -> p t c n", t=NT, c=16)
                V = ar(Q_V, NT * 256).rearrange("p (t c n) -> p t c n", t=NT, c=16)
                Iu = ar(Q_I, NT * 256).bitcast(U32).rearrange("p (t c n) -> p t c n", t=NT, c=16)
                dve.tensor_copy(IOT, iota.unsqueeze(2).to_broadcast([P, KEYS, PIECE]))

                def top16(pieces):
                    for s, v, x in pieces:
                        ins = dve.max(v[:, 0:8], s)
                    link(ins)
                    for s, v, x in pieces:
                        ins = dve.max_index(x[:, 0:8], v[:, 0:8], s)
                    link(ins)
                    for s, v, x in pieces:
                        ins = dve.match_replace(s, v[:, 0:8], s, NEG)
                    link(ins)
                    for s, v, x in pieces:
                        ins = dve.max(v[:, 8:16], s)
                    link(ins)
                    for s, v, x in pieces:
                        ins = dve.max_index(x[:, 8:16], v[:, 8:16], s)
                    link(ins)

                for cg in range(4):
                    dve.wait_ge(sem("s_ready"), since("s_ready", l) + NT * (cg + 1))
                    top16([(S[:, t, c, :], V[:, t, c, :], Iu[:, t, c, :]) for t in range(NT)
                           for c in range(4 * cg, 4 * cg + 4)])
                dve.tensor_copy(ar(Q_IF, NT * 256), ar(Q_I, NT * 256).bitcast(U32))
                Vh = ar(Q_V, NT * 256).rearrange("p (t h j n) -> p t h j n", t=NT, h=HEADS, j=2)
                for t in range(NT):
                    ins = tt(ar(Q_S + 2048 * t, 2048).rearrange("p (h a b) -> p h a b", h=HEADS, a=TOPK),
                             Vh[:, t, :, 0, :].unsqueeze(3).to_broadcast([P, HEADS, TOPK, TOPK]),
                             Vh[:, t, :, 1, :].unsqueeze(2).to_broadcast([P, HEADS, TOPK, TOPK]), ALU.add)
                link(ins)
                C = ar(Q_S, NT * 2048).rearrange("p (t h n) -> p t h n", t=NT, h=HEADS)
                TV = ar(Q_TV, NT * 128).rearrange("p (t h n) -> p t h n", t=NT, h=HEADS)
                TP = ar(Q_TP, NT * 128).bitcast(U32).rearrange("p (t h n) -> p t h n", t=NT, h=HEADS)
                top16([(C[:, t, h, :], TV[:, t, h, :], TP[:, t, h, :]) for t in range(NT) for h in range(HEADS)])
                Tf = ar(Q_TV, NT * 128).rearrange("p (m n) -> p m n", n=TOPK)
                dve.tensor_copy(ss[:, 0:24], Tf[:, :, 0]).then_inc(sem("dve_link"), 1)
                linked[0] += 1
                dve.wait_ge(sem("dve_link"), linked[0])
                tt(Tf, Tf, ss[:, 0:24].unsqueeze(2).to_broadcast([P, 24, TOPK]), ALU.subtract
                   ).then_inc(sem("tv_ready"), 1)
                pos = ar(Q_TP, 384).bitcast(U32)
                ts(ar(Q_AB, 384).bitcast(U32), pos, 4, None, ALU.logical_shift_right)
                link(ts(ar(Q_AB + 384, 384).bitcast(U32), pos, 15, None, ALU.bitwise_and))
                link(dve.tensor_copy(ar(Q_ABF, 768), ar(Q_AB, 768).bitcast(U32)))
                IFh = ar(Q_IF, NT * 256).rearrange("p (t h j n) -> p t h j n", t=NT, h=HEADS, j=2)
                eq = ar(Q_EQ, 2048)
                for j in range(2):
                    for t in range(NT):
                        link(tt(eq.rearrange("p (m n) -> p m n", n=TOPK),
                                ar(Q_ABF + 384 * j + 128 * t, 128).unsqueeze(2).to_broadcast([P, 128, TOPK]),
                                iota[:, 0:TOPK].unsqueeze(1).to_broadcast([P, 128, TOPK]), ALU.is_equal))
                        e4 = eq.rearrange("p (h k n) -> p h k n", h=HEADS, k=TOPK)
                        link(tt(e4, e4, IFh[:, t, :, j, :].unsqueeze(2).to_broadcast([P, HEADS, TOPK, TOPK]), ALU.mult))
                        link(dve.tensor_reduce(ar(Q_ID + 128 * (NT * j + t), 128),
                                               eq.rearrange("p (m n) -> p m n", n=TOPK), AX.X, ALU.add))
                dve.wait_ge(sem("tv_exp"), since("tv_exp", l) + 1)
                link(dve.tensor_reduce(ss[:, 0:24], Tf, AX.X, ALU.add))
                link(dve.reciprocal(ss2[:, 0:24], ss[:, 0:24]))
                tt(ar(Q_ID + 768, 384).rearrange("p (m n) -> p m n", n=TOPK), Tf,
                   ss2[:, 0:24].unsqueeze(2).to_broadcast([P, 24, TOPK]), ALU.mult).then_inc(sem("picked"), 1)

            def experts(l):
                b0 = start["uv", l] // RING
                groups = SPILL // 4
                b1 = b0 + 2 * groups
                at = {name: since(name, l) for name in ("gelu", "w_ready", "g_ps", "oh_ready", "e2_ready", "w_full", "w_hi")}
                dve.wait_ge(sem("it_ready"), since("it_ready", l) + 3)
                link(dve.tensor_copy(IT16[:, 2, :], ar(Q_W32, TOK)))
                tt(IT16[:, 3, :], ar(Q_W32, TOK), IT16[:, 2, :], ALU.subtract).then_inc(sem("weights_split"), 1)
                dve.wait_ge(sem("weights_split"), l + 1)

                def one_hots(p, quarter, col, first=False):
                    def it(q, n):
                        return IT16[:, q, bass.ds(col, PIECE)].unsqueeze(1).to_broadcast([P, n, PIECE])
                    oa = ar(Q_OA, OA_N).bitcast(F16).rearrange("p (e t) -> p e t", e=KEYS)
                    ob = ar(Q_OB, 2 * OB_N).bitcast(F16).rearrange("p (j e t) -> p j e t", j=2,
                                                                                      e=QUARTER)
                    e2 = ar(Q_E2, OB_N).bitcast(F16).rearrange("p (e t) -> p e t", e=QUARTER)
                    if not first:
                        dve.wait_ge(sem("oh_ready"), p + at["oh_ready"])
                    tt(e2, it(1, QUARTER), IOT[:, QUARTER * quarter:QUARTER * quarter + QUARTER, :], ALU.is_equal
                       ).then_inc(sem("e2_ready"), 1)
                    if not first:
                        dve.wait_ge(sem("g_ps"), p + at["g_ps"])
                    tt(oa, it(0, KEYS), IOT[:, :, :], ALU.is_equal)
                    dve.wait_ge(sem("e2_ready"), p + (at["e2_ready"] + 1))
                    tt(ob[:, 0], e2, it(2, QUARTER), ALU.mult)
                    tt(ob[:, 1], e2, it(3, QUARTER), ALU.mult).then_inc(sem("oh_ready"), 1)

                def product(e, s, odd, half, col, pos, turn):
                    w = GL[:, s, :]
                    stt(w, w, 1.0 / G_SCALE, ar(G_N * half, G_N)[:, bass.ds(col, TOK)], ALU.mult, ALU.mult
                        ).then_inc(sem("w_full"), 1)
                    dve.wait_ge(used(pos), turn)
                    dve.wait_ge(sem("w_full"), e + (at["w_full"] + 1))
                    hi, lo = w_hi[:, TOK * odd:TOK * odd + TOK], w_lo[:, TOK * odd:TOK * odd + TOK]
                    dve.tensor_copy(hi, w).then_inc(sem("w_hi"), 1)
                    dve.wait_ge(sem("w_hi"), e + (at["w_hi"] + 1))
                    tt(lo, w, f32(hi), ALU.subtract).then_inc(sem("w_ready"), 1)

                for s in range(4):
                    one_hots(s, 0, PIECE * s, s == 0)
                with dve.Fori(1, groups // 2) as i:
                    for s in range(4):
                        one_hots(i * 4 + s, 0, i * (4 * PIECE) + PIECE * s)
                dve.wait_ge(sem("g_ready"), since("g_ready", l) + QUARTER)
                for quarter in range(2):
                    if quarter:
                        dve.wait_ge(sem("g_ready"), since("g_ready", l) + 2 * QUARTER)
                    with dve.Fori(quarter * groups // 2, (quarter + 1) * groups // 2) as i:
                        for s in range(4):
                            one_hots(i * 4 + (QUARTER + s), quarter + 1,
                                     i * (4 * PIECE) + PIECE * (s - QUARTER * quarter))
                            dve.wait_ge(sem(f"gl_loaded{s % 2}"), i * 32 + (16 * (s // 2 + 1) + 8 * SPILL * l))
                            product(i * 4 + s, s % 2, s % 2, quarter,
                                    i * (4 * TOK) + TOK * (s - QUARTER * quarter),
                                    (s + 2) % 4, i + (b0 + groups + (s >= 2)))

                def step(i, s, quarter, col):
                    j = i * 2 + s
                    if quarter == 2:
                        one_hots(j + 3 * QUARTER, 3, i * (2 * PIECE) + PIECE * s)
                    dve.wait_ge(sem("gelu"), j + (at["gelu"] + SPILL + 1))
                    product(j + SPILL, s, s, quarter % 2, col, 2 - 2 * s, i + (b1 + s))

                for quarter in (2, 3):
                    dve.wait_ge(sem("g_ready"), since("g_ready", l) + (quarter + 1) * QUARTER)
                    if quarter == 3:
                        diagonals(2 * l + 1)
                    with dve.Fori((quarter - 2) * ROUNDS // 2, (quarter - 1) * ROUNDS // 2) as i:
                        for s in range(2):
                            step(i, s, quarter, i * (2 * TOK) + TOK * (s - QUARTER * (quarter - 2)))

            for l in range(LAYERS):
                n = 2 * l
                features(n)
                (prep0 if l == 0 else prep1)()
                attention(l, 0)
                if l:
                    mask_bias()
                attention(l, 1)
                if l == 0:
                    sub_norm()
                mod_columns(l + 1)
                diagonals(n)
                out_columns(l)
                norm(n)
                features(n + 1)
                retrieve(l)
                experts(l)
                norm(n + 1)


def kernel(**inputs):
    import numpy as np
    import concourse.bacc as _bacc
    from concourse import mybir as _mybir
    from concourse.bass_utils import run_bass_kernel_spmd as _run

    g = {k: np.asarray(v) for k, v in inputs.items()}
    f = np.float32

    def columns(w, n):
        w = w.reshape(8, 128, n // 128, 128)
        return np.ascontiguousarray(w.transpose(2, 1, 0, 3)).reshape(n // 128, 128, 1024)

    def wide(w):
        n = -(-w.shape[1] // 512) * 512
        w = np.pad(w, ((0, 0), (0, n - w.shape[1])))
        w = w.reshape(4, 2, 128, n // 512, 512)
        return np.ascontiguousarray(w.transpose(3, 0, 2, 1, 4)).reshape(n // 128, 128, 1024)

    const = np.zeros((128, C_N), f)
    const[:, C_ID:C_ID + 128] = np.eye(128)
    const[:, C_IOTA:C_IOTA + 128] = np.arange(128)
    const[:, C_ONES:C_ONES + 128] = 1
    table = np.zeros((128, T_N), f)
    tok = np.arange(256)
    for rot, c_cos, c_sin in ((64, T_COSA, T_SINA), (32, T_COSB, T_SINB)):
        nf = rot // 4
        inv = (f(10000.0) ** (-np.arange(nf, dtype=f) / f(nf))).astype(f)
        ang = np.concatenate([(tok // 64).astype(f)[:, None] * inv, (tok % 64).astype(f)[:, None] * inv], 1)
        cos, sin = np.cos(ang).astype(f), np.sin(ang).astype(f)
        for t in range(2):
            r = slice(128 * t, 128 * t + 128)
            table[:, c_cos + rot * t:c_cos + rot * t + rot] = np.concatenate([cos[r], cos[r]], 1)
            table[:, c_sin + rot * t:c_sin + rot * t + rot] = np.concatenate([-sin[r], sin[r]], 1)
    qc = np.arange(128) % 64
    c0 = np.clip(qc - 8, 0, 48)
    kc = np.arange(64)
    ok = (kc[None] >= c0[:, None]) & (kc[None] < c0[:, None] + 16)
    table[:, T_MASK:T_MASK + 64] = np.where(ok, 0, -1e30)

    arrays = {
        "x": np.concatenate([g["x_prompt"][0], g["x_sample"][0]]),
        "const": const,
        "cT": np.stack([g["c_ctx"], g["c"][0]]).reshape(2, 8, 128).transpose(2, 1, 0).reshape(128, 16),
        "b_mod": g["b_mod"].reshape(96, 128).T,
        "table": table,
        "lam": np.concatenate([g["ev_lam_q1"][0], g["ev_lam_k1"][0], g["ev_lam_q2"][0], g["ev_lam_k2"][0]]),
        "rows": np.concatenate([g["ev_g_sub"][0], g["ev_g_cq"][0], g["ev_g_ckv"][0], g["od_g_qn"][0],
                                g["od_g_kn"][0]]),
        "ln": np.stack([np.concatenate([g[f"ln{w}_g"][l], g[f"ln{w}_b"][l]]) for l in range(2) for w in (1, 2)]),
        "w_mod": np.concatenate([wide(g["w_mod"][l]) for l in range(2)]),
        "w_in0": wide(g["ev_w_in"][0]), "w_in1": wide(g["od_w_in"][0]),
        "w_out0": wide(g["ev_w_out"][0]), "w_out1": wide(g["od_w_out"][0]),
        "w_q": np.stack([columns(g["pk_w_q"][l], 2048) for l in range(2)]),
        "u": g["pk_u"].reshape(2, 128, 128, 8, 128).transpose(0, 2, 4, 3, 1).reshape(2, 128, 128, 1024),
        "v": g["pk_v"].reshape(2, 128, 128, 1024).transpose(0, 2, 1, 3),
        "keys": np.stack([g["pk_k1"].transpose(0, 2, 1), g["pk_k2"].transpose(0, 2, 1)], 2),
        "w_uq": g["ev_w_uq"][0], "w_ukv": g["ev_w_ukv"][0],
        "rpb": np.pad(g["od_rpb"][0], ((0, 0), (0, 0), (48, 48))).reshape(120, 127),
        "cache_a_k": g["cache_a_k"].reshape(128, 512), "cache_a_v": g["cache_a_v"].reshape(128, 512),
        "cache_b_ckv": g["cache_b_ckv"].reshape(128, 128), "cache_b_kr": g["cache_b_kr"].reshape(128, 32),
        "cache_c_k": g["cache_c_k"].reshape(128, 128), "cache_c_v": g["cache_c_v"].reshape(128, 128),
        "cache_d_k": g["cache_d_k"].reshape(128, 512), "cache_d_v": g["cache_d_v"].reshape(128, 512),
    }
    outs = {"y": (384, 1024), "state_a_k": (128, 512), "state_a_v": (128, 512), "state_b_ckv": (128, 128),
            "state_b_kr": (128, 32), "state_c_k": (128, 128), "state_c_v": (128, 128), "state_d_k": (128, 512),
            "state_d_v": (128, 512)}
    nc = _bacc.Bacc("TRN2", target_bir_lowering=False, num_devices=1)
    sent, args = {}, {}
    for k, v in arrays.items():
        v = np.ascontiguousarray(v)
        assert v.dtype == np.float32, k
        sent[f"in_{k}"] = v
        args[k] = nc.dram_tensor(f"in_{k}", v.shape, _mybir.dt.float32, kind="ExternalInput").ap()
    for k, shape in outs.items():
        args[k] = nc.dram_tensor(f"out_{k}", shape, _mybir.dt.float32, kind="ExternalOutput").ap()
    build(nc, args)
    r = _run(nc, [sent], core_ids=[0]).results[0]
    o = {k: r[f"out_{k}"] for k in outs}
    return (o["y"][:128].reshape(1, 128, 1024), o["y"][128:].reshape(1, 256, 1024),
            o["state_a_k"].reshape(1, 1, 128, 4, 2, 64), o["state_a_v"].reshape(1, 1, 128, 4, 128),
            o["state_b_ckv"].reshape(1, 1, 128, 128), o["state_b_kr"].reshape(1, 1, 128, 32),
            o["state_c_k"].reshape(1, 1, 128, 2, 64), o["state_c_v"].reshape(1, 1, 128, 2, 64),
            o["state_d_k"].reshape(1, 1, 128, 8, 64), o["state_d_v"].reshape(1, 1, 128, 8, 64))
```
